# Optimizing a Trainium2 kernel written in Bass

```python
import math
import jax, jax.numpy as jnp
from jax import lax
import numpy as np

D_MODEL = 1024
BATCH = 1
SEQ = 256
DEPTH = 1

HEAD_DIM = 64
N_FOX_HEADS = 8
N_DSA_HEADS = 8
N_IDX_HEADS = 4
IDX_DIM = 64
TOPK_MAX = 256
Q_BLOCK = 128
N_BUCKETS = 32
MAX_DISTANCE = 128
D_FF = 4 * D_MODEL
EPS = 1e-6

FOX_W = N_FOX_HEADS * HEAD_DIM
DSA_W = N_DSA_HEADS * HEAD_DIM
SPLIT_SIZES = [
    FOX_W, FOX_W, FOX_W,
    N_FOX_HEADS,
    DSA_W, DSA_W, DSA_W,
    N_IDX_HEADS * IDX_DIM,
    IDX_DIM,
    N_IDX_HEADS,
    D_MODEL, D_MODEL,
]
D_IN = int(sum(SPLIT_SIZES))
SPLIT_POINTS = [int(v) for v in np.cumsum(SPLIT_SIZES)[:-1]]


def rmsnorm(x, g):
    xf = x.astype(jnp.float32)
    y = xf * lax.rsqrt(jnp.mean(xf * xf, axis=-1, keepdims=True) + EPS)
    return (y * g.astype(jnp.float32)).astype(x.dtype)

def t5_bucket(dist):
    n = jnp.maximum(dist, 0)
    max_exact = N_BUCKETS // 2
    is_small = n < max_exact
    nf = jnp.maximum(n, 1).astype(jnp.float32)
    large = max_exact + (jnp.log(nf / max_exact) / math.log(MAX_DISTANCE / max_exact)
                         * (N_BUCKETS - max_exact)).astype(jnp.int32)
    large = jnp.minimum(large, N_BUCKETS - 1)
    return jnp.where(is_small, n, large)

def forgetting_attention(q, k, v, cum_logf):
    B, S, H, Dh = q.shape
    n_blocks = S // Q_BLOCK
    scale = Dh ** -0.5
    Ft = jnp.transpose(cum_logf, (0, 2, 1))
    key_pos = jnp.arange(S)

    def block(i):
        start = i * Q_BLOCK
        qb = lax.dynamic_slice_in_dim(q, start, Q_BLOCK, axis=1)
        Fb = lax.dynamic_slice_in_dim(Ft, start, Q_BLOCK, axis=2)
        s = jnp.einsum('bqhd,bkhd->bhqk', qb, k).astype(jnp.float32) * scale
        s = s + Fb[..., :, None] - Ft[:, :, None, :]
        q_pos = start + jnp.arange(Q_BLOCK)
        mask = key_pos[None, :] <= q_pos[:, None]
        s = jnp.where(mask[None, None], s, -jnp.inf)
        p = jax.nn.softmax(s, axis=-1).astype(v.dtype)
        return jnp.einsum('bhqk,bkhd->bqhd', p, v)

    out = lax.map(block, jnp.arange(n_blocks))
    return jnp.transpose(out, (1, 0, 2, 3, 4)).reshape(B, S, H, Dh)

def indexer_sparse_attention(q, k, v, q_idx, k_idx, w_idx, rel_bias):
    B, S, H, Dh = q.shape
    n_blocks = S // Q_BLOCK
    topk = min(TOPK_MAX, S // 4)
    scale = Dh ** -0.5
    idx_scale = IDX_DIM ** -0.5
    key_pos = jnp.arange(S)
    gather = jax.vmap(lambda arr, ids: arr[ids])

    def block(i):
        start = i * Q_BLOCK
        qb = lax.dynamic_slice_in_dim(q, start, Q_BLOCK, axis=1)
        qib = lax.dynamic_slice_in_dim(q_idx, start, Q_BLOCK, axis=1)
        wib = lax.dynamic_slice_in_dim(w_idx, start, Q_BLOCK, axis=1)
        q_pos = start + jnp.arange(Q_BLOCK)
        sc = jnp.einsum('bqhd,bkd->bqhk', qib, k_idx).astype(jnp.float32) * idx_scale
        iscore = jnp.einsum('bqhk,bqh->bqk', jax.nn.relu(sc), wib.astype(jnp.float32))
        causal = key_pos[None, :] <= q_pos[:, None]
        iscore = jnp.where(causal[None], iscore, -jnp.inf)
        _, sel = lax.top_k(iscore, topk)
        kg = gather(k, sel)
        vg = gather(v, sel)
        logits = jnp.einsum('bqhd,bqkhd->bhqk', qb, kg).astype(jnp.float32) * scale
        dist = q_pos[None, :, None] - sel
        valid = dist >= 0
        bias = rel_bias[t5_bucket(dist)].astype(jnp.float32)
        logits = logits + jnp.transpose(bias, (0, 3, 1, 2))
        logits = jnp.where(valid[:, None], logits, -jnp.inf)
        p = jax.nn.softmax(logits, axis=-1).astype(vg.dtype)
        return jnp.einsum('bhqk,bqkhd->bqhd', p, vg)

    out = lax.map(block, jnp.arange(n_blocks))
    return jnp.transpose(out, (1, 0, 2, 3, 4)).reshape(B, S, H, Dh)

def first_inputs(seed: int = 0) -> dict:
    key = jax.random.key(seed)
    ks = jax.random.split(key, 16)
    D = D_MODEL
    nrm = lambda k, shape, s: jax.random.normal(k, shape, jnp.float32) * s
    return {
        "x": nrm(ks[0], (BATCH, SEQ, D), 1.0),
        "c": nrm(ks[1], (BATCH, D), 1.0),
        "w_ada": nrm(ks[2], (D, 6 * D), 0.5 * D ** -0.5),
        "b_ada": nrm(ks[3], (6 * D,), 0.02),
        "g_norm1": 1.0 + nrm(ks[4], (D,), 0.02),
        "w_in": nrm(ks[5], (D, D_IN), D ** -0.5),
        "b_forget": nrm(ks[6], (N_FOX_HEADS,), 0.1),
        "rel_bias": nrm(ks[7], (N_BUCKETS, N_DSA_HEADS), 0.5),
        "w_branch_fox": nrm(ks[8], (FOX_W, D), FOX_W ** -0.5),
        "w_branch_dsa": nrm(ks[9], (DSA_W, D), DSA_W ** -0.5),
        "w_out": nrm(ks[10], (D, D), D ** -0.5),
        "g_norm2": 1.0 + nrm(ks[11], (D,), 0.02),
        "w_mlp1": nrm(ks[12], (D, D_FF), D ** -0.5),
        "w_mlp2": nrm(ks[13], (D_FF, D), D_FF ** -0.5),
        "g_final": 1.0 + nrm(ks[14], (D,), 0.02),
    }

def first_block(x, c, w_ada, b_ada, g_norm1, w_in, b_forget, rel_bias, w_branch_fox,
              w_branch_dsa, w_out, g_norm2, w_mlp1, w_mlp2, g_final):
    B, S, D = x.shape
    ada = (c @ w_ada + b_ada)[:, None, :]
    shift1, scale1, gate1, shift2, scale2, gate2 = jnp.split(ada, 6, axis=-1)

    for _ in range(DEPTH):
        h = rmsnorm(x, g_norm1) * (1.0 + scale1) + shift1
        proj = h @ w_in
        (q_f, k_f, v_f, f_logit, q_d, k_d, v_d, q_i, k_i, w_i,
         gate_fox, gate_dsa) = jnp.split(proj, SPLIT_POINTS, axis=-1)
        hs = (B, S, -1, HEAD_DIM)
        log_f = jax.nn.log_sigmoid((f_logit + b_forget).astype(jnp.float32))
        cum_logf = jnp.cumsum(log_f, axis=1)
        y_fox = forgetting_attention(q_f.reshape(hs), k_f.reshape(hs), v_f.reshape(hs),
                                     cum_logf).reshape(B, S, FOX_W)
        w_i = w_i * (N_IDX_HEADS ** -0.5)
        y_dsa = indexer_sparse_attention(
            q_d.reshape(hs), k_d.reshape(hs), v_d.reshape(hs),
            q_i.reshape(B, S, N_IDX_HEADS, IDX_DIM), k_i, w_i, rel_bias
        ).reshape(B, S, DSA_W)
        merged = (jax.nn.sigmoid(gate_fox) * (y_fox @ w_branch_fox)
                  + jax.nn.sigmoid(gate_dsa) * (y_dsa @ w_branch_dsa))
        x = x + gate1 * (merged @ w_out)

        h2 = rmsnorm(x, g_norm2) * (1.0 + scale2) + shift2
        x = x + gate2 * (jnp.square(jax.nn.relu(h2 @ w_mlp1)) @ w_mlp2)

    return rmsnorm(x, g_final)


DEPTH_2 = 2

CHUNK = 64
MEM_LEN = 256
N_A_LAYERS = DEPTH_2 // 2
N_B_LAYERS = DEPTH_2 - N_A_LAYERS
MEM_HEADS = 4
MEM_HEAD_DIM = 64
MEM_W = MEM_HEADS * MEM_HEAD_DIM
MAIN_W = D_MODEL - MEM_W
CONV_W = MAIN_W
CONV_K = 3
DIFF_HEAD_DIM = 64
DIFF_HEADS = MAIN_W // (2 * DIFF_HEAD_DIM)
DIFF_QK = DIFF_HEADS * DIFF_HEAD_DIM
ROPE_DIM = DIFF_HEAD_DIM // 4
ROPE_THETA = 500000.0
D_FF_2 = 4 * D_MODEL
SUBLN_EPS = 1e-5


def rmsnorm_2(x, g, eps=EPS):
    xf = x.astype(jnp.float32)
    y = xf * lax.rsqrt(jnp.mean(xf * xf, axis=-1, keepdims=True) + eps)
    return (y * g.astype(jnp.float32)).astype(x.dtype)

def rope_tables(seq):
    inv = 1.0 / (ROPE_THETA ** (jnp.arange(0, ROPE_DIM, 2, dtype=jnp.float32) / ROPE_DIM))
    ang = jnp.arange(seq, dtype=jnp.float32)[:, None] * inv[None, :]
    return jnp.cos(ang), jnp.sin(ang)

def partial_rope(x, cos, sin):
    half = ROPE_DIM // 2
    c = cos[None, :, None, :].astype(x.dtype)
    s = sin[None, :, None, :].astype(x.dtype)
    x1, x2, xp = x[..., :half], x[..., half:ROPE_DIM], x[..., ROPE_DIM:]
    return jnp.concatenate([x1 * c - x2 * s, x1 * s + x2 * c, xp], axis=-1)

def short_conv_mixer(h, gate_b, gate_c, w_conv):
    u = gate_c * h
    s_len = u.shape[1]
    up = jnp.pad(u, ((0, 0), (CONV_K - 1, 0), (0, 0)))
    y = w_conv[0] * up[:, 0:s_len]
    for k in range(1, CONV_K):
        y = y + w_conv[k] * up[:, k:k + s_len]
    return gate_b * y

def memory_attention(q, mem_n, w_mem_kv, q_gain, k_gain):
    b, s, _ = q.shape
    m = mem_n.shape[1]
    kv = jnp.einsum('bmd,de->bme', mem_n, w_mem_kv)
    k = kv[..., :MEM_W].reshape(b, m, MEM_HEADS, MEM_HEAD_DIM)
    v = kv[..., MEM_W:].reshape(b, m, MEM_HEADS, MEM_HEAD_DIM)
    qh = rmsnorm_2(q.reshape(b, s, MEM_HEADS, MEM_HEAD_DIM), q_gain)
    k = rmsnorm_2(k, k_gain)
    sc = jnp.einsum('bshd,bmhd->bhsm', qh, k).astype(jnp.float32) * (MEM_HEAD_DIM ** -0.5)
    p = jax.nn.softmax(sc, axis=-1).astype(v.dtype)
    o = jnp.einsum('bhsm,bmhd->bshd', p, v)
    return o.reshape(b, s, MEM_W)

def diff_attention(q1, q2, k1, k2, v, lam):
    b, s, h, dh = q1.shape
    nblk = s // Q_BLOCK
    scale = dh ** -0.5
    key_chunk = jnp.arange(s) // CHUNK
    qb1 = jnp.moveaxis(q1.reshape(b, nblk, Q_BLOCK, h, dh), 1, 0)
    qb2 = jnp.moveaxis(q2.reshape(b, nblk, Q_BLOCK, h, dh), 1, 0)

    def one_block(args):
        a1, a2, i = args
        q_chunk = (i * Q_BLOCK + jnp.arange(Q_BLOCK)) // CHUNK
        mask = (key_chunk[None, :] <= q_chunk[:, None])[None, None]
        s1 = jnp.einsum('bqhd,bkhd->bhqk', a1, k1).astype(jnp.float32) * scale
        s2 = jnp.einsum('bqhd,bkhd->bhqk', a2, k2).astype(jnp.float32) * scale
        p1 = jax.nn.softmax(jnp.where(mask, s1, -jnp.inf), axis=-1)
        p2 = jax.nn.softmax(jnp.where(mask, s2, -jnp.inf), axis=-1)
        p = (p1 - lam * p2).astype(v.dtype)
        return jnp.einsum('bhqk,bkhe->bqhe', p, v)

    out = lax.map(one_block, (qb1, qb2, jnp.arange(nblk)))
    return jnp.moveaxis(out, 0, 1).reshape(b, s, h, 2 * dh)

def sqrelu_mlp(h, w_up, w_down):
    u = jnp.einsum('bsd,df->bsf', h, w_up)
    return jnp.einsum('bsf,fd->bsd', jnp.square(jax.nn.relu(u)), w_down)

def second_inputs(seed: int = 0) -> dict:
    key = jax.random.key(seed)
    ks = jax.random.split(key, 24)
    f32 = jnp.float32
    nrm = lambda k, shp, sc: jax.random.normal(k, shp, f32) * sc
    gain = lambda k, shp: 1.0 + 0.02 * jax.random.normal(k, shp, f32)
    return {
        "x": nrm(ks[0], (BATCH, SEQ, D_MODEL), 1.0),
        "mem": nrm(ks[1], (BATCH, MEM_LEN, D_MODEL), 1.0),
        "norm_mix": gain(ks[2], (DEPTH_2, D_MODEL)),
        "norm_mlp": gain(ks[3], (DEPTH_2, D_MODEL)),
        "a_w_in": nrm(ks[4], (N_A_LAYERS, D_MODEL, 3 * CONV_W + MEM_W), D_MODEL ** -0.5),
        "a_conv": nrm(ks[5], (N_A_LAYERS, CONV_K, CONV_W), CONV_K ** -0.5),
        "b_w_q": nrm(ks[6], (N_B_LAYERS, D_MODEL, 2 * DIFF_QK + MEM_W), D_MODEL ** -0.5),
        "b_q_norm": gain(ks[7], (N_B_LAYERS, DIFF_HEAD_DIM)),
        "b_lam": nrm(ks[8], (N_B_LAYERS, 4, DIFF_HEAD_DIM), 0.1),
        "b_subln": gain(ks[9], (N_B_LAYERS, 2 * DIFF_HEAD_DIM)),
        "kv_norm": gain(ks[10], (D_MODEL,)),
        "w_kv": nrm(ks[11], (D_MODEL, 2 * DIFF_QK + MAIN_W), D_MODEL ** -0.5),
        "k_norm": gain(ks[12], (DIFF_HEAD_DIM,)),
        "mem_norm": gain(ks[13], (D_MODEL,)),
        "w_mem_kv": nrm(ks[14], (DEPTH_2, D_MODEL, 2 * MEM_W), D_MODEL ** -0.5),
        "mem_q_norm": gain(ks[15], (DEPTH_2, MEM_HEAD_DIM)),
        "mem_k_norm": gain(ks[16], (DEPTH_2, MEM_HEAD_DIM)),
        "w_o": nrm(ks[17], (DEPTH_2, MAIN_W + MEM_W, D_MODEL), (MAIN_W + MEM_W) ** -0.5),
        "w_up": nrm(ks[18], (DEPTH_2, D_MODEL, D_FF_2), D_MODEL ** -0.5),
        "w_down": nrm(ks[19], (DEPTH_2, D_FF_2, D_MODEL), 0.5 * D_FF_2 ** -0.5),
    }

def second_block(x, mem, norm_mix, norm_mlp, a_w_in, a_conv, b_w_q, b_q_norm, b_lam, b_subln,
              kv_norm, w_kv, k_norm, mem_norm, w_mem_kv, mem_q_norm, mem_k_norm,
              w_o, w_up, w_down):
    b, s, _ = x.shape
    cos, sin = rope_tables(s)
    mem_n = rmsnorm_2(mem, mem_norm)
    k1 = k2 = v = None
    for l in range(DEPTH_2):
        h = rmsnorm_2(x, norm_mix[l])
        if l < N_A_LAYERS:
            proj = jnp.einsum('bsd,de->bse', h, a_w_in[l])
            gate_b = proj[..., :CONV_W]
            gate_c = proj[..., CONV_W:2 * CONV_W]
            hv = proj[..., 2 * CONV_W:3 * CONV_W]
            qm = proj[..., 3 * CONV_W:]
            main = short_conv_mixer(hv, gate_b, gate_c, a_conv[l])
        else:
            j = l - N_A_LAYERS
            proj = jnp.einsum('bsd,de->bse', h, b_w_q[j])
            q1 = proj[..., :DIFF_QK].reshape(b, s, DIFF_HEADS, DIFF_HEAD_DIM)
            q2 = proj[..., DIFF_QK:2 * DIFF_QK].reshape(b, s, DIFF_HEADS, DIFF_HEAD_DIM)
            qm = proj[..., 2 * DIFF_QK:]
            q1 = partial_rope(rmsnorm_2(q1, b_q_norm[j]), cos, sin)
            q2 = partial_rope(rmsnorm_2(q2, b_q_norm[j]), cos, sin)
            lam_init = 0.8 - 0.6 * float(np.exp(-0.3 * l))
            lp = b_lam[j].astype(jnp.float32)
            lam = (jnp.exp(jnp.sum(lp[0] * lp[1])) - jnp.exp(jnp.sum(lp[2] * lp[3]))
                   + lam_init)
            o = diff_attention(q1, q2, k1, k2, v, lam)
            o = rmsnorm_2(o, b_subln[j], SUBLN_EPS) * (1.0 - lam_init)
            main = o.reshape(b, s, MAIN_W)
        mo = memory_attention(qm, mem_n, w_mem_kv[l], mem_q_norm[l], mem_k_norm[l])
        x = x + jnp.einsum('bse,ed->bsd', jnp.concatenate([main, mo], axis=-1), w_o[l])
        x = x + sqrelu_mlp(rmsnorm_2(x, norm_mlp[l]), w_up[l], w_down[l])
        if l == N_A_LAYERS - 1:
            kvh = rmsnorm_2(x, kv_norm)
            kv = jnp.einsum('bsd,de->bse', kvh, w_kv)
            k1 = kv[..., :DIFF_QK].reshape(b, s, DIFF_HEADS, DIFF_HEAD_DIM)
            k2 = kv[..., DIFF_QK:2 * DIFF_QK].reshape(b, s, DIFF_HEADS, DIFF_HEAD_DIM)
            v = kv[..., 2 * DIFF_QK:].reshape(b, s, DIFF_HEADS, 2 * DIFF_HEAD_DIM)
            k1 = partial_rope(rmsnorm_2(k1, k_norm), cos, sin)
            k2 = partial_rope(rmsnorm_2(k2, k_norm), cos, sin)
    return x


def setup_inputs(seed=0):
    out = dict(first_inputs(seed))
    for name, value in second_inputs(seed + 1).items():
        if name != "x":
            out[name + "_2"] = value
    return out


def reference(
    x, c, w_ada, b_ada, g_norm1, w_in, b_forget, rel_bias, w_branch_fox, w_branch_dsa, w_out,
    g_norm2, w_mlp1, w_mlp2, g_final, mem_2, norm_mix_2, norm_mlp_2, a_w_in_2, a_conv_2,
    b_w_q_2, b_q_norm_2, b_lam_2, b_subln_2, kv_norm_2, w_kv_2, k_norm_2, mem_norm_2,
    w_mem_kv_2, mem_q_norm_2, mem_k_norm_2, w_o_2, w_up_2, w_down_2,
):
    x = first_block(
        x, c, w_ada, b_ada, g_norm1, w_in, b_forget, rel_bias, w_branch_fox, w_branch_dsa,
        w_out, g_norm2, w_mlp1, w_mlp2, g_final,
    )
    return second_block(
        x, mem_2, norm_mix_2, norm_mlp_2, a_w_in_2, a_conv_2, b_w_q_2, b_q_norm_2, b_lam_2,
        b_subln_2, kv_norm_2, w_kv_2, k_norm_2, mem_norm_2, w_mem_kv_2, mem_q_norm_2,
        mem_k_norm_2, w_o_2, w_up_2, w_down_2,
    )


_drawn_inputs = setup_inputs


def setup_inputs(seed=0):
    import zlib

    import numpy as np

    out = dict(_drawn_inputs(seed))
    spreads = {}
    factors = {'g_norm1': 3.106,
     'b_forget': 4.674,
     'g_norm2': 2.995,
     'norm_mlp_2': 4.221,
     'b_q_norm_2': 8.0,
     'b_lam_2': 3.909,
     'b_subln_2': 8.0,
     'kv_norm_2': 6.675,
     'k_norm_2': 8.0,
     'mem_norm_2': 8.0,
     'mem_q_norm_2': 8.0,
     'mem_k_norm_2': 8.0}
    for name, (base, spread) in spreads.items():
        noise = np.random.default_rng([zlib.crc32(name.encode()), seed]).standard_normal(out[name].shape)
        drawn = base * np.exp(spread * noise) if base else spread * noise
        out[name] = __import__('jax').numpy.asarray(drawn.astype(out[name].dtype))
    for name, factor in factors.items():
        out[name] = (out[name] * factor).astype(out[name].dtype)
    return out
```

```python
from contextlib import ExitStack

import numpy as np

import concourse.bass as bass
from concourse import mybir

F32 = mybir.dt.float32
F32R = mybir.dt.float32r
ALU = mybir.AluOpType
ACT = mybir.ActivationFunctionType
AX = mybir.AxisListType

P = 128
T = 256
TT = T // P
D = 1024
KT = D // P
HD = 64
HEADS = 8
IDX_HEADS = 4
TOPK = T // 4
FF = 4 * D
MEM_HEADS = 4
MEM_W = MEM_HEADS * HD
MAIN_W = D - MEM_W
CT = MAIN_W // P
DIFF_HEADS = MAIN_W // (2 * HD)
EPS = 1e-6
SUBLN_EPS = 1e-5
LAM_INIT = 0.8 - 0.6 * float(np.exp(-0.3 * 1))
MASKED = -1e30
PICKED = -3e38

C_QF, C_KF, C_VF, C_F = 0, 512, 1024, 1536
C_QD, C_KD, C_VD = 1544, 2056, 2568
C_QI, C_KI, C_WI = 3080, 3336, 3400
C_GF, C_GD = 3404, 4428

V_C, V_ADA, V_G1, V_G2, V_GF, V_MIX, V_MLP, V_KV, V_MEM = 0, 8, 56, 64, 72, 80, 96, 112, 120
V_CONV, V_SUBLN, V_BQ, V_K, V_MQ, V_MK = 128, 146, 147, 148, 149, 151
VEC_ROWS2 = 25

RING = 4
AHEAD = 3
FF_STEPS = FF // 512
MLP_LOOPS = 3
BODY = 8


def plan_units(w):
    units = []

    def n_unit(name, src, col, user, pieces=None):
        cols = src.rearrange("(k p) n -> p k n", p=P)
        pieces = pieces or [(0, col, 256)]
        units.append(("N", name, [(at, cols[:, :, c:c + width]) for at, c, width in pieces], user))

    def k_unit(name, src, row, col, user=None):
        rows = src[row:row + 512, col:col + 512].rearrange("(k p) n -> p k n", p=P)
        units.append(("K", name, [(0, rows)], user))

    def mlp(name, up, down):
        for j in range(FF_STEPS + 1):
            if j < FF_STEPS:
                n_unit(f"{name}.up", up, 512 * j, "a")
                n_unit(f"{name}.up", up, 512 * j + 256, "a")
            if j >= 1:
                k_unit(f"{name}.down", down, 512 * (j - 1), 0)
                k_unit(f"{name}.down", down, 512 * (j - 1), 512)

    for l in range(2):
        n_unit(f"mem{l}.k", w["w_mem_kv"][l], 0, "a")
        n_unit(f"mem{l}.v", w["w_mem_kv"][l], MEM_W, "a")
    w_in = w["w_in"]
    n_unit("idx.k", w_in, 0, "a", [(0, C_KI, 64), (64, C_KI, 128), (192, C_F, 64)])
    n_unit("idx.q", w_in, C_QI, "a")
    for c in (C_QF, C_KF, C_VF):
        n_unit("fox", w_in, c, "a")
        n_unit("fox", w_in, c + 256, "a")
    for i in range(4):
        n_unit("gate.fox", w_in, C_GF + 256 * i, "a")
    for c in (C_QD, C_KD, C_VD):
        n_unit("dsa", w_in, c, "a")
        n_unit("dsa", w_in, c + 256, "a")
    for i in range(4):
        n_unit("gate.dsa", w_in, C_GD + 256 * i, "a")
    for name in ("w_branch_fox", "w_branch_dsa"):
        k_unit("branch", w[name], 0, 0)
        k_unit("branch", w[name], 0, 512)
    for i in range(4):
        n_unit("out", w["w_out"], 256 * i, "v")
    mlp("mlp0", w["w_mlp1"], w["w_mlp2"])
    a_in = w["a_w_in"][0]
    n_unit("qm0", a_in, 3 * MAIN_W, "a")
    for c, user in ((MAIN_W, "a"), (2 * MAIN_W, "v"), (0, "v")):
        for i in range(3):
            n_unit("conv", a_in, c + 256 * i, user)
    for i in range(4):
        n_unit("o0", w["w_o"][0], 256 * i, "v")
    mlp("mlp1", w["w_up"][0], w["w_down"][0])
    for i in range(3):
        n_unit("k", w["w_kv"], 256 * i, "a")
    for i in range(4):
        n_unit("q", w["b_w_q"][0], 256 * i, "a")
    for i in range(3):
        n_unit("v", w["w_kv"], MAIN_W + 256 * i, "a")
    for i in range(4):
        n_unit("o1", w["w_o"][1], 256 * i, "v")
    mlp("mlp2", w["w_up"][1], w["w_down"][1])
    return units


N_MEM, N_IDX, N_FOX, N_GF, N_DSA, N_GD, N_BR, N_OUT, N_MLP0 = 0, 4, 6, 12, 16, 22, 26, 30, 34
N_QM0, N_CONV, N_O0, N_MLP1, N_K, N_Q, N_V, N_O1, N_MLP2 = 66, 67, 76, 80, 112, 115, 119, 122, 126
N_UNITS = 158

MISC = (["vec", "qk.mem0", "sum1", "qk.mem1", "wi", "row"] + [f"fox{g}" for g in range(4)]
        + [f"dsa{g}" for g in range(4)] + ["sum2", "sum3", "sum4", "qk.qm0", "mem0.0", "mem0.1", "sum5", "sum6",
           "qk.k0", "qk.k1", "rope.k0", "qk.k2", "rope.k1", "qk.q0", "rope.k2", "qk.q1", "rope.q0", "qk.q2", "rope.q1",
           "qk.qm1", "rope.q2", "mem1.0", "mem1.1", "pv0"]
        + [f"{what}{h - (what == 'oT')}" for h in range(1, DIFF_HEADS) for what in ("pv", "oT")] + ["oT5", "sum7"])
POWERS = [m for m in MISC if m[:3] in ("sum", "qk.")]
QK_NORMS = [m for m in MISC if m.startswith("qk.")]
ROPES = [m for m in MISC if m.startswith("rope.")]

J_MEM, J_H1, J_FOX, J_DSA, J_MERGED, J_H2, J_MLP0 = 0, 4, 8, 10, 12, 16, 20
J_H4, J_YM0, J_CONV, J_H5, J_MLP1 = 36, 40, 41, 44, 48
J_KV, J_MIX1, J_YM1, J_DIFF, J_H7, J_MLP2 = 64, 68, 72, 73, 76, 80
G_FOX, G_DSA, G_M0, G_M1 = 0, 4, 8, 10


class Count:

    def __init__(self):
        self.n, self.turn, self.per = 0, None, 0

    def up(self, k=1):
        self.n += k
        return self.now()

    def now(self, off=0):
        v = self.n + off
        return v if self.turn is None else self.turn * self.per + v

    def enter(self, turn, per):
        self.turn, self.per, self.entered = turn, per, self.n

    def leave(self, turns):
        assert self.n - self.entered == self.per, (self.n - self.entered, self.per)
        self.n = self.entered + self.per * turns
        self.turn = None


def host_tables():
    t = np.arange(P)
    ident = np.eye(P, dtype=np.float32)
    ones = np.ones((P, P), np.float32)
    heads2 = (t[:, None] // HD == t[None, :] // HD).astype(np.float32)
    causal = np.where(t[None, :] <= t[:, None], 0, MASKED).astype(np.float32)
    chunk = np.where(t[None, :] // 64 <= t[:, None] // 64, 0, MASKED).astype(np.float32)
    consts = np.concatenate([ident, ones, heads2, causal], 1)
    chunks = np.concatenate([chunk, np.zeros((P, P), np.float32), chunk], 1)
    half = 8
    inv = (1.0 / (np.float32(500000.0) ** (np.arange(0, 2 * half, 2, dtype=np.float32) / np.float32(2 * half))))
    ang = np.arange(T, dtype=np.float32)[None, :] * inv.astype(np.float32)[:, None]
    cos, sin = np.ones((P, T), np.float32), np.zeros((P, T), np.float32)
    perm = np.zeros((P, P), np.float32)
    for base in (0, HD):
        for i in range(half):
            cos[base + i] = cos[base + half + i] = np.cos(ang[i])
            sin[base + i] = sin[base + half + i] = np.sin(ang[i])
            perm[base + half + i, base + i] = -1.0
            perm[base + i, base + half + i] = 1.0
    rope = np.concatenate([cos, sin, perm], 1)
    dist = 255 - np.arange(384)
    n = np.maximum(dist, 0)
    large = 16 + (np.log(np.maximum(n, 1).astype(np.float32) / np.float32(16)) / np.float32(np.log(8.0))
                  * np.float32(16)).astype(np.int32)
    bucket = np.where(n < 16, n, np.minimum(large, 31))
    buckets = np.zeros((33, 384), np.float32)
    buckets[bucket, np.arange(384)] = dist >= 0
    buckets[32] = np.where(dist >= 0, 0, MASKED)
    return {"consts": consts, "chunks": chunks, "rope": rope, "buckets": buckets}


def two_blocks(nc, x, w, vectors, tables, out):
    units = plan_units(w)
    assert len(units) == N_UNITS
    raw_value, lin_bank, before, evac_value = [], [], [], []
    slot_count, emptied, order = [0] * RING, {"a": 0, "v": 0}, []
    for n, (_, _, pieces, user) in enumerate(units):
        slot_count[n % RING] += 16 * len(pieces)
        raw_value.append(slot_count[n % RING])
        lin_bank.append(len(order) % 2 if user else None)
        before.append(order[-2] if user and len(order) >= 2 else None)
        if user:
            emptied[user] += 1
            order.append((user, emptied[user]))
        evac_value.append(emptied[user] if user else None)

    misc_no = {name: i for i, name in enumerate(MISC)}
    power_no = {name: i for i, name in enumerate(POWERS)}
    qk_no = {name: i for i, name in enumerate(QK_NORMS)}
    rope_no = {name: i for i, name in enumerate(ROPES)}

    ctx = ExitStack()
    with ctx:
        def sb(name, shape, dt=F32):
            return ctx.enter_context(nc.sbuf_tensor(name, shape, dt))

        def sem(name):
            return ctx.enter_context(nc.semaphore(name))

        w_raw = sb("w_raw", [P, RING, 2048])
        w_hi = sb("w_hi", [P, RING, 2048], F32R)
        w_lo = sb("w_lo", [P, RING, 2048], F32R)
        xT = sb("xT", [P, KT, T])
        h_hi = sb("h_hi", [P, KT, T], F32R)
        h_lo = sb("h_lo", [P, KT, T], F32R)
        u_hi = sb("u_hi", [P, KT, T], F32R)
        u_lo = sb("u_lo", [P, KT, T], F32R)
        fresh = sb("fresh", [P, 2, 512])
        qk = sb("qk", [P, 8, T])
        v_tok = sb("v_tok", [P, TT, 512])
        big = sb("big", [P, 16, T])
        head_bias = sb("head_bias", [P, HEADS, 384])
        idx = sb("idx", [P, 384])
        probs = sb("probs", [P, 2, 512])
        probsT = sb("probsT", [P, 2, 512])
        y_tok = sb("y_tok", [P, TT, 512])
        mem_k = sb("mem_k", [P, 2, 2, T])
        mem_v = sb("mem_v", [P, 2, TT, MEM_W])
        consts = sb("consts", [P, 4 * P])
        vec = sb("vec", [P, 2 * P])
        ada = sb("ada", [P, 48])
        gs = sb("gs", [P, 2, KT])
        rstd = sb("rstd", [P, 512])
        stat = sb("stat", [P, 96])
        top8 = sb("top8", [P, 2, 8])
        minus_half = sb("minus_half", [P, 1])
        rel = sb("rel", [P, 8])

        def flat(t, a, b):
            return t[:, a:b, :].rearrange("p a n -> p (a n)")

        ident, ones, heads2, causal = (consts[:, i * P:i * P + P] for i in range(4))
        ada_ring = [big[:, 8 * s:8 * s + 8, :] for s in range(2)]
        mem_tok = flat(qk, 0, 8).rearrange("p (t n) -> p t n", t=TT)
        x_tok = flat(head_bias, 0, HEADS)[:, 0:TT * D].rearrange("p (t n) -> p t n", t=TT)
        out_tok = x_tok
        qi, ki = v_tok[:, 0, :].rearrange("p (a n) -> p a n", a=2), v_tok[:, 1, 0:T]
        f_cum, rows, f_raw, sq_sum = y_tok[:, 0, 0:T], y_tok[:, 0, T:2 * T], y_tok[:, 1, 0:T], y_tok[:, 1, T:2 * T]
        buckets, bias_row = probsT[:, 0, 0:384], probsT[:, 1, 0:384]
        toeplitz = big[:, 8:16, :]
        cosT, sinT, perm = big[:, 6, :], big[:, 7, :], big[:, 8, 0:P]
        lam_in = big[:, 9, :].rearrange("p (a d) -> p a d", a=4)
        diff_v = flat(big, 0, 6).rearrange("p (t n) -> p t n", t=TT)
        diff_q = big[:, 10:16, :]
        chunk_mask = head_bias[:, 4, :]
        S_MEM, S_WI, S_MAX, S_NMAX, S_SUM, S_INV, S_DOT, S_LAM, S_NLAM = 0, 8, 16, 20, 24, 32, 36, 38, 40
        S_DMAX, S_DNMAX, S_DSUM, S_DINV, S_OSS, S_ORSTD = 44, 52, 60, 68, 76, 80

        bank = [ctx.enter_context(nc.psum_tensor(f"bank{i}", [P, 512], F32)) for i in range(8)]
        lin, acc, ps_ada, ps_misc = bank[0:2], bank[2:6], bank[6], bank[7]
        SKEW = 384 + 1
        bias_dram = nc.dram_tensor("bias_rows", (HEADS, P * SKEW), F32, kind="Internal").ap()

        raw_full = [sem(f"raw_full{s}") for s in range(RING)]
        ada_full = [sem(f"ada_full{s}") for s in range(2)]
        consts_in, rows_in, mem_in, x_in, small_in = (sem(s) for s in (
            "consts_in", "rows_in", "mem_in", "x_in", "small_in"))
        bias_out, bias_in, late_in, y_out = (sem(s) for s in ("bias_out", "bias_in", "late_in", "y_out"))
        hi_w, lo_w, unit_done, evac_a, evac_v = (sem(s) for s in ("hi_w", "lo_w", "unit_done", "evac_a", "evac_v"))
        fresh_ready, fresh_hi, fresh_lo = sem("fresh_ready"), sem("fresh_hi"), sem("fresh_lo")
        chain_v, chain_a, chain_g = sem("chain_v"), sem("chain_a"), sem("chain_g")
        misc_full, misc_read = sem("misc_full"), sem("misc_read")
        filled, vec_ready = sem("filled"), sem("vec_ready")
        mem_sq, mem_var, mem_rstd, mem_scaled, mem_turned = (sem(s) for s in (
            "mem_sq", "mem_var", "mem_rstd", "mem_scaled", "mem_turned"))
        ada_done, ada_ready, x_turned = sem("ada_done"), sem("ada_ready"), sem("x_turned")
        xt_ready, sq_ready, sq_added, rstd_ready = (sem(s) for s in ("xt_ready", "sq_ready", "sq_added", "rstd_ready"))
        qk_normed, rope_cos, rope_done = (sem(s) for s in ("qk_normed", "rope_cos", "rope_done"))
        f_in, f_exp, f_ln, f_ready, sel_ready, f_bc, f_copied, fox_bias = (sem(s) for s in (
            "f_in", "f_exp", "f_ln", "f_ready", "sel_ready", "f_bc", "f_copied", "fox_bias"))
        idx_mm, idx_relu, idx_added, picked, dsa_bias = (sem(s) for s in (
            "idx_mm", "idx_relu", "idx_added", "picked", "dsa_bias"))
        score_mm, score_max, exp_done, turned, turned_copied, y_turned, y_copied = (sem(s) for s in (
            "score_mm", "score_max", "exp_done", "turned", "turned_copied", "y_turned", "y_copied"))
        branch_done, half_done = sem("branch_done"), sem("half_done")
        lam_dots, lam_exp = sem("lam_dots"), sem("lam_exp")
        d_score, d_max, d_exp, mixed, d_turned, d_copied, o_copied, o_sq, o_var, o_rstd, o_scaled = (sem(s) for s in (
            "d_score", "d_max", "d_exp", "mixed", "d_turned", "d_copied", "o_copied", "o_sq", "o_var", "o_rstd", "o_scaled"))
        out_turned, out_copied = sem("out_turned"), sem("out_copied")

        CAUSAL_BLOCKS, CAUSAL_SPAN = [(0, 0, 0), (1, 0, 128), (1, 1, 256)], [(0, 128), (128, 384)]
        FULL_BLOCKS, FULL_SPAN = [(0, 0, 0), (0, 1, 128), (1, 0, 256), (1, 1, 384)], [(0, 256), (256, 512)]

        block = ctx.enter_context(nc.Block())

        @block.sync
        def _(sp):
            def slot_view(n, at, width):
                if units[n][0] == "N":
                    return w_raw[:, n % RING, :].rearrange("p (k n) -> p k n", k=KT)[:, :, at:at + width]
                return w_raw[:, n % RING, :].rearrange("p (k n) -> p k n", k=4)

            def load_unit(n):
                if n >= RING:
                    sp.wait_ge(lo_w, n - RING + 1)
                for at, src in units[n][2]:
                    sp.dma_start(slot_view(n, at, src.shape[-1]), src).then_inc(raw_full[n % RING], 16)

            def load_ada(a):
                if a >= 2:
                    sp.wait_ge(ada_done, a - 1)
                cols = w["w_ada"].rearrange("(k p) n -> p k n", p=P)[:, :, 256 * a:256 * a + 256]
                sp.dma_start(ada_ring[a % 2], cols).then_inc(ada_full[a % 2], 16)

            def load_mlp(n0, up, down):
                up_cols = up.rearrange("(k p) n -> p k n", p=P)
                down_rows = down.rearrange("(j k p) n -> p j k n", j=FF_STEPS, p=P)
                for n in range(n0, n0 + 6):
                    load_unit(n)
                with sp.Fori(0, MLP_LOOPS) as turn:
                    for k in range(BODY):
                        n = n0 + 6 + k
                        is_up = k % 4 < 2
                        step = 2 + k // 4 if is_up else 1 + k // 4
                        at = sp.snap(turn * 1024 + (512 * step + 256 * (k % 2))) if is_up else sp.snap(turn * 2 + step)
                        free = sp.snap(turn * BODY + (n - RING + 1))
                        sp.wait_ge(lo_w, free)
                        if is_up:
                            sp.dma_start(slot_view(n, 0, 256), up_cols[:, :, bass.ds(at, 256)])\
                                .then_inc(raw_full[n % RING], 16)
                        else:
                            c0 = 512 * (k % 2)
                            sp.dma_start(w_raw[:, n % RING, :].rearrange("p (j k n) -> p j k n", j=1, k=4),
                                         down_rows[:, bass.ds(at, 1), :, c0:c0 + 512]).then_inc(raw_full[n % RING], 16)
                for n in range(n0 + 30, n0 + 32):
                    load_unit(n)

            sp.dma_start(consts[:, :], tables["consts"]).then_inc(consts_in, 16)
            sp.dma_start(mem_tok, vectors["mem"].rearrange("(t p) d -> p t d", p=P)).then_inc(mem_in, 16)
            sp.wait_ge(filled, 1)
            at = 0
            for name, count in (("c", 8), ("b_ada", 48), ("g_norm1", 8), ("g_norm2", 8), ("g_final", 8),
                                ("norm_mix", 16), ("norm_mlp", 16), ("kv_norm", 8), ("mem_norm", 8)):
                sp.dma_start(rows[at:at + count, 0:P], vectors[name].rearrange("(r p) -> r p", p=P)).then_inc(rows_in, 16)
                at += count
            sp.dma_start(rows[0:18, P:2 * P], vectors["a_conv"].rearrange("(r p) -> r p", p=P)).then_inc(rows_in, 16)
            sp.dma_start(rows[18:19, P:2 * P], vectors["b_subln"].rearrange("(r p) -> r p", p=P)).then_inc(rows_in, 16)
            at = 19
            for name, count in (("b_q_norm", 1), ("k_norm", 1), ("mem_q_norm", 2), ("mem_k_norm", 2)):
                for side in range(2):
                    sp.dma_start(rows[at:at + count, P + HD * side:P + HD * side + HD],
                                 vectors[name].rearrange("(r p) -> r p", p=HD)).then_inc(rows_in, 16)
                at += count
            load_ada(0)
            load_ada(1)
            load_unit(0)
            sp.dma_start(x_tok, x.rearrange("(t p) d -> p t d", p=P)).then_inc(x_in, 16)
            load_unit(1)
            sp.dma_start(rel[0:32, :], vectors["rel_bias"].rearrange("(b h) -> b h", h=HEADS)).then_inc(small_in, 16)
            sp.dma_start(rel[64:64 + HEADS, 0:1], vectors["b_forget"].rearrange("(h o) -> h o", o=1)).then_inc(small_in, 16)
            sp.dma_start(buckets[0:33, :], tables["buckets"]).then_inc(small_in, 16)
            for a in (2, 4, 6):
                load_ada(a)
                load_ada(a + 1)
                if a < 6:
                    load_unit(1 + a // 2)
            for n in range(4, 8):
                load_unit(n)
            for k in range(8):
                load_ada(8 + 2 * k)
                load_ada(9 + 2 * k)
                load_unit(8 + k)
            sp.wait_ge(misc_read, misc_no["row"] + 1)
            sp.dma_start(bass.AP(bias_dram.tensor, bias_dram.offset, [[P * SKEW, HEADS], [SKEW, P], [1, 384]]),
                         bias_row[0:HEADS, :].unsqueeze(1).to_broadcast([HEADS, P, 384])).then_inc(bias_out, 16)
            sp.wait_ge(bias_out, 16)
            sp.wait_ge(ada_done, 24)
            sp.dma_start(toeplitz, bass.AP(bias_dram.tensor, bias_dram.offset + P - 1, [[SKEW - 1, P], [P * SKEW, HEADS], [1, T]]))\
                .then_inc(bias_in, 16)
            for n in range(16, N_MLP0):
                load_unit(n)
            load_mlp(N_MLP0, w["w_mlp1"], w["w_mlp2"])
            for n in range(N_QM0, N_MLP1):
                load_unit(n)
            load_mlp(N_MLP1, w["w_up"][0], w["w_down"][0])
            sp.dma_start(flat(big, 6, 9)[:, 0:2 * T + P], tables["rope"]).then_inc(late_in, 16)
            sp.dma_start(big[:, 9, :], vectors["b_lam"].partition_broadcast(P)).then_inc(late_in, 16)
            sp.dma_start(chunk_mask, tables["chunks"]).then_inc(late_in, 16)
            for n in range(N_K, N_MLP2):
                load_unit(n)
            load_mlp(N_MLP2, w["w_up"][1], w["w_down"][1])
            for tt in range(TT):
                sp.wait_ge(out_copied, 2 * tt + 2)
                sp.dma_start(out.rearrange("(t p) d -> p t d", p=P)[:, tt, :], out_tok[:, tt, :]).then_inc(y_out, 16)
            sp.wait_ge(y_out, 32)

        @block.tensor
        def _(pe):
            heads, pairs = Count(), Count()

            def mm(dst, lhsT, rhs, start, stop):
                return pe.matmul(dst, lhsT, rhs, start=start, stop=stop, skip_group_check=True)

            def into_misc(name):
                if misc_no[name]:
                    pe.wait_ge(misc_read, misc_no[name])

            def start_unit(n, turn):
                pe.wait_ge(lo_w, n + 1 if turn is None else turn * BODY + (n + 1))
                if before[n]:
                    user, value = before[n]
                    pe.wait_ge(evac_a if user == "a" else evac_v, value if turn is None else turn * 4 + value)

            def product(n, hi, lo, first_tile=0, banks=None, start=True, turn=None, bank_order=False, job=None):
                start_unit(n, turn)
                banks = banks or [lin[lin_bank[n]]]
                kts, nts = (KT, 2) if units[n][0] == "N" else (4, 4)
                wh = w_hi[:, n % RING, :].rearrange("p (k n) -> p k n", k=kts)
                wl = w_lo[:, n % RING, :].rearrange("p (k n) -> p k n", k=kts)
                order = [(kt, nt) for kt in range(kts) for nt in range(nts)]
                if bank_order:
                    order = [(kt, 2 * b + i) for b in range(nts // 2) for kt in range(kts) for i in range(2)]
                for kt, nt in order:
                    if job is not None and kt % 2 == 0 and nt == 0:
                        pe.wait_ge(fresh_lo, job + kt // 2 + 1)
                    for i, (a, b) in enumerate(((wh, hi), (wh, lo), (wl, hi))):
                        last = mm(banks[nt // 2][:, (nt % 2) * T:(nt % 2) * T + T], a[:, kt, nt * P:nt * P + P],
                                  b[:, first_tile + kt, :], start and kt == 0 and nt % 2 == 0 and i == 0, kt == kts - 1 and i == 2)
                    if bank_order and kt == kts - 1 and nt == 1:
                        last.then_inc(half_done, 1)
                last.then_inc(unit_done, 1)

            def product_tok(n, hi, lo):
                start_unit(n, None)
                wh = w_hi[:, n % RING, :].rearrange("p (k n) -> p k n", k=KT)
                wl = w_lo[:, n % RING, :].rearrange("p (k n) -> p k n", k=KT)
                for kt in range(KT):
                    for tt in range(TT):
                        for i, (a, b) in enumerate(((hi, wh), (lo, wh), (hi, wl))):
                            last = mm(lin[lin_bank[n]][:, tt * T:tt * T + T], a[:, kt, tt * P:tt * P + P], b[:, kt, :],
                                      kt == 0 and tt == 0 and i == 0, kt == KT - 1 and i == 2)
                last.then_inc(unit_done, 1)

            def ada_unit(a):
                pe.wait_ge(ada_full[a % 2], 16 * (a // 2 + 1))
                if a == 8:
                    pe.wait_ge(ada_ready, 1)
                for nt in range(2):
                    for kt in range(KT):
                        last = mm(ps_ada[:, 2 * a + nt:2 * a + nt + 1], ada_ring[a % 2][:, kt, nt * P:nt * P + P],
                                  vec[:, V_C + kt:V_C + kt + 1], kt == 0, kt == KT - 1)
                last.then_inc(ada_done, 1)

            def sum_squares(s):
                into_misc(f"sum{s}")
                pe.wait_ge(sq_added, 4 * s)
                mm(ps_misc[:, 0:T], ones, sq_sum, True, True).then_inc(misc_full, 1)

            def qk_squares(name, n):
                into_misc("qk." + name)
                pe.wait_ge(evac_a, evac_value[n])
                mm(ps_misc[:, :], heads2, probs[:, qk_no["qk." + name] % 2, :], True, True).then_inc(misc_full, 1)

            def rotate(name, src):
                into_misc("rope." + name)
                pe.wait_ge(qk_normed, qk_no["qk." + name] + 1)
                mm(ps_misc[:, :], perm, src, True, True).then_inc(misc_full, 1)

            def to_T(dst_banks, src, sem_done, wait_q=None):
                for q, dst in enumerate(dst_banks):
                    if wait_q:
                        wait_q(q)
                    for i in range(2):
                        for tt in range(TT):
                            c0 = (2 * q + i) * P
                            last = pe.transpose(dst[:, i * T + tt * P:i * T + tt * P + P], src[:, tt, c0:c0 + P], ident)
                    last.then_inc(sem_done, 1)

            def scores(q_tile, k_tile, span):
                for odd in range(2):
                    heads.up()
                    base = HD * odd
                    for tt, (c0, c1) in enumerate(span):
                        last = mm(acc[odd][:, c0:c1], q_tile[base:base + HD, tt * P:tt * P + P],
                                  k_tile[base:base + HD, 0:c1 - c0], True, True)
                    last.then_inc(score_mm, 1)

            def attention(name, n_pairs, q_tile, k_tile, values, blocks, span, filler):
                scores(q_tile(0), k_tile(0), span)
                for g in range(n_pairs):
                    filler(g)
                    G = pairs.up() - 1
                    for odd in range(2):
                        h = 2 * G + odd
                        pe.wait_ge(exp_done, h + 1)
                        if h >= 2:
                            pe.wait_ge(turned_copied, h - 1)
                        for _, _, c0 in blocks:
                            last = pe.transpose(acc[2 + odd][:, c0:c0 + P], probs[:, odd, c0:c0 + P], ident)
                        last.then_inc(turned, 1)
                    if g + 1 < n_pairs:
                        scores(q_tile(g + 1), k_tile(g + 1), span)
                    into_misc(f"{name}{g}")
                    for odd in range(2):
                        pe.wait_ge(turned_copied, 2 * G + odd + 1)
                        for tt in range(TT):
                            mine = [(s, c0) for t, s, c0 in blocks if t == tt]
                            for i, (s, c0) in enumerate(mine):
                                at = (2 * odd + tt) * HD
                                last = mm(ps_misc[:, at:at + HD], probsT[:, odd, c0:c0 + P], values(2 * g + odd, s),
                                          i == 0, i == len(mine) - 1)
                    last.then_inc(misc_full, 1)

            pe.wait_ge(consts_in, 16)
            pe.wait_ge(rows_in, 16 * 19)
            pe.transpose(ps_misc[:, 0:P], rows[:, 0:P], ident)
            pe.transpose(ps_misc[:, P:2 * P], rows[:, P:2 * P], ident).then_inc(misc_full, 1)
            pe.wait_ge(mem_scaled, 2)
            to_T(acc, mem_tok, mem_turned)
            pe.wait_ge(vec_ready, 1)
            ada_unit(0)
            ada_unit(1)
            product(0, u_hi, u_lo, job=J_MEM)
            ada_unit(2)
            ada_unit(3)
            product_tok(1, u_hi, u_lo)
            qk_squares("mem0", 0)
            pe.wait_ge(x_in, 16)
            to_T(acc, x_tok, x_turned, lambda q: pe.wait_ge(fresh_ready, q + 1))
            ada_unit(4)
            ada_unit(5)
            product(2, u_hi, u_lo)
            sum_squares(1)
            ada_unit(6)
            ada_unit(7)
            product_tok(3, u_hi, u_lo)
            qk_squares("mem1", 2)
            for k in range(8):
                n = N_IDX + k
                ada_unit(8 + 2 * k)
                ada_unit(9 + 2 * k)
                if n < 10:
                    product(n, h_hi, h_lo, job=J_H1 if n == N_IDX else None)
                else:
                    product_tok(n, h_hi, h_lo)
                if n == 5:
                    into_misc("wi")
                    pe.wait_ge(evac_a, evac_value[4])
                    for tt in range(TT):
                        last = pe.transpose(ps_misc[:, tt * P:tt * P + P], f_raw[:, tt * P:tt * P + P], ident)
                    last.then_inc(misc_full, 1)
                if n == 6:
                    pe.wait_ge(evac_a, evac_value[5])
                    for h in range(IDX_HEADS):
                        base = HD * (h % 2)
                        for tt, (c0, c1) in enumerate(CAUSAL_SPAN):
                            last = mm(acc[h][:, c0:c1], qi[base:base + HD, h // 2, tt * P:tt * P + P],
                                      ki[base:base + HD, 0:c1 - c0], True, True)
                        last.then_inc(idx_mm, 1)
                if n == 8:
                    pe.wait_ge(f_ready, 1)
                    pe.wait_ge(sel_ready, 1)
                    pe.wait_ge(idx_relu, IDX_HEADS)
                    for h in range(HEADS):
                        last = mm(acc[h // 2][:, (h % 2) * T:(h % 2) * T + T], head_bias[:, h, 0:P], f_cum, True, True)
                        if h % 2:
                            last.then_inc(f_bc, 1)
                if n == 9:
                    into_misc("row")
                    pe.wait_ge(small_in, 48)
                    mm(ps_misc[0:HEADS, 0:384], rel[0:33, :], buckets[0:33, :], True, True).then_inc(misc_full, 1)
            pe.wait_ge(f_copied, 4)
            pe.wait_ge(evac_a, evac_value[11])
            attention("fox", 4, lambda g: qk[:, g, :], lambda g: qk[:, 4 + g, :],
                      lambda h, s: v_tok[:, s, h * HD:h * HD + HD], CAUSAL_BLOCKS, CAUSAL_SPAN,
                      lambda g: product(N_GF + g, h_hi, h_lo))
            product(N_DSA, h_hi, h_lo)
            pe.wait_ge(misc_read, misc_no["fox3"] + 1)
            to_T(acc[0:2], y_tok, y_turned)
            for n in range(N_DSA + 1, N_GD):
                if n < N_DSA + 4:
                    product(n, h_hi, h_lo)
                else:
                    product_tok(n, h_hi, h_lo)
            pe.wait_ge(fresh_ready, J_DSA)
            pe.wait_ge(evac_a, evac_value[N_GD - 1])
            attention("dsa", 4, lambda g: qk[:, g, :], lambda g: qk[:, 4 + g, :],
                      lambda h, s: v_tok[:, s, h * HD:h * HD + HD], CAUSAL_BLOCKS, CAUSAL_SPAN,
                      lambda g: product(N_GD + g, h_hi, h_lo))
            product(N_BR, u_hi, u_lo, 0, acc[0:2], job=J_FOX)
            product(N_BR + 1, u_hi, u_lo, 0, acc[2:4])
            pe.wait_ge(misc_read, misc_no["dsa3"] + 1)
            to_T(acc[0:2], y_tok, y_turned, lambda q: pe.wait_ge(branch_done, q + 1))
            pe.wait_ge(fresh_ready, J_MERGED)
            product(N_BR + 2, u_hi, u_lo, 4, acc[0:2], job=J_DSA)
            pe.wait_ge(branch_done, 4)
            product(N_BR + 3, u_hi, u_lo, 4, acc[2:4])
            for i in range(4):
                product(N_OUT + i, h_hi, h_lo, job=J_MERGED if i == 0 else None)

            def mlp(n0, s, job_h, job_u):
                def up(n, turn=None, job=None):
                    product(n, h_hi, h_lo, turn=turn, job=job)
                    product(n + 1, h_hi, h_lo, turn=turn)

                def down(n, step, turn=None, last=False):
                    ready = job_u + 2 * step + 2
                    pe.wait_ge(fresh_lo, ready if turn is None else turn * 4 + ready)
                    for half in range(2):
                        product(n + half, u_hi, u_lo, 4 * (step % 2), acc[2 * half:2 * half + 2], start=step == 0,
                                turn=turn, bank_order=last)

                sum_squares(s)
                up(n0, job=job_h)
                up(n0 + 2)
                down(n0 + 4, 0)
                with pe.Fori(0, MLP_LOOPS) as turn:
                    for k in range(2):
                        up(n0 + 6 + 4 * k, turn)
                        down(n0 + 8 + 4 * k, 1 + k, turn)
                down(n0 + 30, FF_STEPS - 1, last=True)

            pe.wait_ge(fresh_ready, J_H2)
            mlp(N_MLP0, 2, J_H2, J_MLP0)
            sum_squares(3)
            sum_squares(4)
            product(N_QM0, h_hi, h_lo, job=J_H4)
            product(N_CONV, h_hi, h_lo)
            qk_squares("qm0", N_QM0)
            product(N_CONV + 1, h_hi, h_lo)
            product(N_CONV + 2, h_hi, h_lo)
            pe.wait_ge(qk_normed, qk_no["qk.qm0"] + 1)
            attention("mem0.", 2, lambda g: qi[:, g, :], lambda g: mem_k[:, 0, g, :],
                      lambda h, s: mem_v[:, 0, s, h * HD:h * HD + HD], FULL_BLOCKS, FULL_SPAN,
                      lambda g: product(N_CONV + 3 + g, h_hi, h_lo))
            product(N_CONV + 5, h_hi, h_lo)
            pe.wait_ge(misc_read, misc_no["mem0.1"] + 1)
            to_T(acc[0:1], y_tok, y_turned)
            for n in range(N_CONV + 6, N_O0):
                product(n, h_hi, h_lo)
            pe.wait_ge(fresh_lo, J_H5)
            for i in range(4):
                product(N_O0 + i, u_hi, u_lo)
            mlp(N_MLP1, 5, J_H5, J_MLP1)
            sum_squares(6)
            product(N_K, h_hi, h_lo, job=J_KV)
            product(N_K + 1, h_hi, h_lo)
            pe.wait_ge(late_in, 48)
            qk_squares("k0", N_K)
            product(N_K + 2, h_hi, h_lo)
            qk_squares("k1", N_K + 1)
            rotate("k0", flat(qk, 0, 2))
            product(N_Q, u_hi, u_lo, job=J_MIX1)
            qk_squares("k2", N_K + 2)
            rotate("k1", flat(qk, 2, 4))
            product(N_Q + 1, u_hi, u_lo)
            qk_squares("q0", N_Q)
            rotate("k2", flat(qk, 4, 6))
            product(N_Q + 2, u_hi, u_lo)
            qk_squares("q1", N_Q + 1)
            rotate("q0", flat(big, 10, 12))
            product(N_Q + 3, u_hi, u_lo)
            qk_squares("q2", N_Q + 2)
            rotate("q1", flat(big, 12, 14))
            product_tok(N_V, h_hi, h_lo)
            qk_squares("qm1", N_Q + 3)
            rotate("q2", flat(big, 14, 16))
            pe.wait_ge(qk_normed, qk_no["qk.qm1"] + 1)
            attention("mem1.", 2, lambda g: qi[:, g, :], lambda g: mem_k[:, 1, g, :],
                      lambda h, s: mem_v[:, 1, s, h * HD:h * HD + HD], FULL_BLOCKS, FULL_SPAN,
                      lambda g: product_tok(N_V + 1 + g, h_hi, h_lo))
            pe.wait_ge(misc_read, misc_no["mem1.1"] + 1)
            to_T(acc[0:1], y_tok, y_turned)

            def d_scores(h):
                base, odd = HD * (h % 2), h % 2
                for m in range(2):
                    for tt, (c0, c1) in enumerate(CAUSAL_SPAN):
                        last = mm(acc[2 * odd + m][:, c0:c1], diff_q[base:base + HD, 3 * m + h // 2, tt * P:tt * P + P],
                                  qk[base:base + HD, 3 * m + h // 2, 0:c1 - c0], True, True)
                last.then_inc(d_score, 1)

            def turn_o(h):
                into_misc(f"oT{h}")
                pe.wait_ge(o_scaled, h + 1)
                for tt in range(TT):
                    last = pe.transpose(ps_misc[:, tt * P:tt * P + P], y_tok[:, tt, (h % 2) * P:(h % 2) * P + P], ident)
                last.then_inc(misc_full, 1)

            pe.wait_ge(rope_done, len(ROPES))
            pe.wait_ge(fresh_ready, J_YM1 + 1)
            pe.wait_ge(evac_a, evac_value[N_V + 2])
            d_scores(0)
            for h in range(DIFF_HEADS):
                if h + 1 < DIFF_HEADS:
                    if h >= 1:
                        pe.wait_ge(d_max, h)
                    d_scores(h + 1)
                pe.wait_ge(mixed, h + 1)
                if h >= 1:
                    pe.wait_ge(d_copied, h)
                for _, _, c0 in CAUSAL_BLOCKS:
                    last = pe.transpose(ps_ada[:, c0:c0 + P], head_bias[:, 2 * (h % 2), c0:c0 + P], ident)
                last.then_inc(d_turned, 1)
                into_misc(f"pv{h}")
                pe.wait_ge(d_copied, h + 1)
                for tt in range(TT):
                    mine = [(s, c0) for t, s, c0 in CAUSAL_BLOCKS if t == tt]
                    for i, (s, c0) in enumerate(mine):
                        last = mm(ps_misc[:, tt * P:tt * P + P], probsT[:, h % 2, c0:c0 + P], diff_v[:, s, h * P:h * P + P],
                                  i == 0, i == len(mine) - 1)
                last.then_inc(misc_full, 1)
                if h >= 1:
                    turn_o(h - 1)
            turn_o(DIFF_HEADS - 1)
            pe.wait_ge(fresh_lo, J_H7)
            for i in range(4):
                product(N_O1 + i, u_hi, u_lo)
            mlp(N_MLP2, 7, J_H7, J_MLP2)
            for tt in range(TT):
                for q in range(2):
                    pe.wait_ge(xt_ready, 24 + 2 * q + 2)
                    if tt == 0 and q == 0:
                        pe.wait_ge(evac_a, emptied["a"])
                    dst = (lin[0], lin[1], ps_ada, ps_misc)[2 * tt + q]
                    for i in range(4):
                        last = pe.transpose(dst[:, i * P:i * P + P], xT[:, 4 * q + i, tt * P:tt * P + P], ident)
                    last.then_inc(out_turned, 1)

        @block.scalar
        def _(act):
            chain, heads, squares = Count(), Count(), Count()

            def link(ins):
                ins.then_inc(chain_a, 1)
                act.wait_ge(chain_a, chain.up())

            def split_w(n, turn=None):
                if n >= N_UNITS:
                    return
                at = lambda value, per: value if turn is None else turn * per + value
                act.wait_ge(raw_full[n % RING], at(raw_value[n], 32))
                if n >= RING:
                    act.wait_ge(unit_done, at(n - RING + 1, BODY))
                act.activation(w_hi[:, n % RING, :], w_raw[:, n % RING, :], ACT.Copy).then_inc(hi_w, 1)

            def split_h(job, hi, tile, turn=None, free=None):
                at = lambda value, per: value if turn is None else turn * per + value
                act.wait_ge(fresh_ready, at(job + 1, 4))
                if free:
                    act.wait_ge(unit_done, at(free, BODY))
                act.activation(flat(hi, tile, tile + 2), fresh[:, job % 2, :], ACT.Copy).then_inc(fresh_hi, 1)

            def evac(n, dst, func=ACT.Copy, scale=1.0):
                act.wait_ge(unit_done, n + 1)
                act.activation(dst, lin[lin_bank[n]][:, :], func, scale=scale).then_inc(evac_a, 1)

            def evac_qk(name, n, dst):
                act.wait_ge(unit_done, n + 1)
                act.activation(dst, lin[lin_bank[n]][:, :], ACT.Copy)
                i = qk_no["qk." + name]
                if i >= 2:
                    act.wait_ge(misc_full, misc_no[QK_NORMS[i - 2]] + 1)
                act.activation(probs[:, i % 2, :], lin[lin_bank[n]][:, :], ACT.Square).then_inc(evac_a, 1)

            def square_pair(s, q, src):
                if s > 1 or q >= 2:
                    act.wait_ge(sq_added, 4 * (s - 1) + q - 1)
                act.activation(probs[:, q % 2, :], src, ACT.Square).then_inc(sq_ready, 1)

            def square_x(s):
                for q in range(4):
                    act.wait_ge(xt_ready, 4 * (s - 2) + q + 1)
                    square_pair(s, q, flat(xT, 2 * q, 2 * q + 2))

            def exps(G, span, from_bank=False):
                for odd in range(2):
                    h = 2 * G + odd
                    act.wait_ge(score_max, h + 1)
                    if from_bank and h >= 2:
                        act.wait_ge(turned, h - 1)
                    for tt, (c0, c1) in enumerate(span):
                        at = 2 * odd + tt
                        last = act.activation(probs[:, odd, c0:c1], (acc[odd] if from_bank else probs[:, odd, :])[:, c0:c1],
                                              ACT.Exp, bias=stat[:, S_NMAX + at:S_NMAX + at + 1],
                                              accum_out=stat[:, S_SUM + 4 * (G % 2) + at:S_SUM + 4 * (G % 2) + at + 1])
                    last.then_inc(exp_done, 1)

            def copy_turned(name, g, G, width):
                before_me = misc_no[f"{name}{g}"]
                for odd in range(2):
                    h = 2 * G + odd
                    act.wait_ge(turned, h + 1)
                    if g >= 1:
                        act.wait_ge(misc_full, before_me)
                    act.activation(probsT[:, odd, 0:width], acc[2 + odd][:, 0:width], ACT.Copy).then_inc(turned_copied, 1)

            def sigmoid_unit(n, tile):
                evac(n, flat(big, tile, tile + 2), ACT.Tanh, 0.5)

            act.wait_ge(mem_in, 16)
            for tt in range(TT):
                last = act.activation(flat(xT, 4 * tt, 4 * tt + 4), mem_tok[:, tt, :], ACT.Square,
                                      accum_out=stat[:, S_MEM + tt:S_MEM + tt + 1])
            last.then_inc(mem_sq, 1)
            for q in range(4):
                split_h(J_MEM + q, u_hi, 2 * q)
            for n in range(AHEAD):
                split_w(n)
            split_w(3)
            evac_qk("mem0", 0, flat(mem_k[:, 0], 0, 2))
            split_w(4)
            evac(1, flat(mem_v[:, 0], 0, 2))
            act.wait_ge(misc_full, misc_no["qk.mem0"] + 1)
            act.wait_ge(mem_turned, 4)
            for q in range(4):
                act.wait_ge(x_turned, q + 1)
                act.activation(flat(xT, 2 * q, 2 * q + 2), acc[q][:, :], ACT.Copy)
                square_pair(1, q, acc[q][:, :])
            split_w(5)
            act.wait_ge(sq_added, 4)
            evac_qk("mem1", 2, flat(mem_k[:, 1], 0, 2))
            split_w(6)
            evac(3, flat(mem_v[:, 1], 0, 2))
            for q in range(4):
                split_h(J_H1 + q, h_hi, 2 * q)
            split_w(7)
            act.wait_ge(unit_done, 5)
            act.wait_ge(misc_full, misc_no["vec"] + 1)
            act.activation(ki, lin[lin_bank[4]][:, 0:T], ACT.Copy)
            act.activation(f_raw, lin[lin_bank[4]][:, T:2 * T], ACT.Copy).then_inc(evac_a, 1)
            split_w(8)
            evac(5, v_tok[:, 0, :], scale=HD ** -0.5)
            act.wait_ge(f_in, 1)
            link(act.activation(rstd[64:64 + HEADS, 0:T], rstd[64:64 + HEADS, 0:T], ACT.Exp))
            act.activation(rstd[64:64 + HEADS, 0:T], rstd[64:64 + HEADS, 0:T], ACT.Ln, bias=1.0).then_inc(f_ln, 1)
            split_w(9)
            evac(6, flat(qk, 0, 2), scale=HD ** -0.5)
            act.wait_ge(misc_full, misc_no["qk.mem1"] + 1)
            for h in range(IDX_HEADS):
                act.wait_ge(idx_mm, h + 1)
                if h >= 2:
                    act.wait_ge(idx_added, h - 1)
                act.activation(probs[:, h % 2, 0:384], acc[h][:, 0:384], ACT.Relu).then_inc(idx_relu, 1)
            split_w(10)
            evac(7, flat(qk, 2, 4), scale=HD ** -0.5)
            split_w(11)
            evac(8, flat(qk, 4, 6))
            for q in range(4):
                act.wait_ge(f_bc, 4)
                act.activation(head_bias[:, 2 * q:2 * q + 2, 128:384], acc[q][:, :].rearrange("p (h s) -> p h s", h=2),
                               ACT.Copy, scale=-1.0).then_inc(f_copied, 1)
            split_w(12)
            evac(9, flat(qk, 6, 8))
            for n in (10, 11):
                split_w(n + AHEAD)
                act.wait_ge(unit_done, n + 1)
                c0 = 256 * (n - 10)
                act.activation(v_tok[:, :, c0:c0 + 256], lin[lin_bank[n]][:, :].rearrange("p (t c) -> p t c", t=TT),
                               ACT.Copy).then_inc(evac_a, 1)
            act.wait_ge(bias_out, 16)
            for g in range(4):
                exps(G_FOX + g, CAUSAL_SPAN)
                split_w(N_GF + g + AHEAD)
                sigmoid_unit(N_GF + g, 2 * g)
                copy_turned("fox", g, G_FOX + g, 384)
            split_w(N_DSA + AHEAD)
            act.wait_ge(misc_full, misc_no["fox3"] + 1)
            evac(N_DSA, flat(qk, 0, 2), scale=HD ** -0.5)
            for q in range(2):
                split_h(J_FOX + q, u_hi, 2 * q)
            for i in range(1, 4):
                split_w(N_DSA + i + AHEAD)
                evac(N_DSA + i, flat(qk, 2 * i, 2 * i + 2), scale=HD ** -0.5 if i < 2 else 1.0)
            for i in range(4, 6):
                n = N_DSA + i
                split_w(n + AHEAD)
                act.wait_ge(unit_done, n + 1)
                c0 = 256 * (i - 4)
                act.activation(v_tok[:, :, c0:c0 + 256], lin[lin_bank[n]][:, :].rearrange("p (t c) -> p t c", t=TT),
                               ACT.Copy).then_inc(evac_a, 1)
            for g in range(4):
                exps(G_DSA + g, CAUSAL_SPAN)
                split_w(N_GD + g + AHEAD)
                sigmoid_unit(N_GD + g, 8 + 2 * g)
                copy_turned("dsa", g, G_DSA + g, 384)
            split_w(N_BR + AHEAD)
            split_w(N_BR + 1 + AHEAD)
            for q in range(2):
                split_h(J_DSA + q, u_hi, 4 + 2 * q)
            split_w(N_BR + 2 + AHEAD)
            for q in range(4):
                if q == 2:
                    split_w(N_BR + 3 + AHEAD)
                split_h(J_MERGED + q, h_hi, 2 * q)
            for i in range(4):
                split_w(N_OUT + i + AHEAD)
                act.wait_ge(xt_ready, i + 1)
                square_pair(2, i, flat(xT, 2 * i, 2 * i + 2))
            for q in range(4):
                split_h(J_H2 + q, h_hi, 2 * q)

            def mlp(n0, job_u, ahead=AHEAD):
                def up_step(n, step, turn=None, first=0):
                    at = lambda value, per: value if turn is None else turn * per + value
                    job = job_u + 2 * step
                    free = n0 + 6 + 4 * (step - 2) if step >= 2 else None
                    for half in range(2):
                        split_w(n + half + ahead, turn)
                        if half:
                            split_h(job, u_hi, 4 * (step % 2), turn, free)
                        act.wait_ge(unit_done, at(n + half + 1, BODY))
                        act.wait_ge(fresh_lo, at(job + half - 1, 4))
                        act.activation(fresh[:, half, :], lin[half][:, :], ACT.Relu).then_inc(evac_a, 1)

                def down_step(n, step, turn=None, pending=None):
                    for half in range(2):
                        split_w(n + half + ahead, turn)
                        if half == 0 and pending is not None:
                            free = n0 + 6 + 4 * (pending - 2) if pending >= 2 else None
                            split_h(job_u + 2 * pending + 1, u_hi, 4 * (pending % 2) + 2, turn, free)

                up_step(n0, 0)
                split_h(job_u + 1, u_hi, 2)
                up_step(n0 + 2, 1)
                down_step(n0 + 4, 0, pending=1)
                with act.Fori(0, MLP_LOOPS) as turn:
                    for k in range(2):
                        up_step(n0 + 6 + 4 * k, 2 + k, turn)
                        down_step(n0 + 8 + 4 * k, 1 + k, turn, pending=2 + k)
                down_step(n0 + 30, FF_STEPS - 1)

            mlp(N_MLP0, J_MLP0)
            square_x(3)
            square_x(4)
            for q in range(4):
                split_h(J_H4 + q, h_hi, 2 * q)
            split_w(N_QM0 + AHEAD)
            act.wait_ge(sq_added, 16)
            evac_qk("qm0", N_QM0, v_tok[:, 0, :])
            for i in range(3):
                split_w(N_CONV + i + AHEAD)
                evac(N_CONV + i, flat(big, 2 * i, 2 * i + 2))
            act.wait_ge(misc_full, misc_no["qk.qm0"] + 1)
            for g in range(2):
                exps(G_M0 + g, FULL_SPAN, from_bank=True)
                split_w(N_CONV + 3 + g + AHEAD)
                copy_turned("mem0.", g, G_M0 + g, 512)
            split_w(N_CONV + 5 + AHEAD)
            split_h(J_YM0, u_hi, 6)
            for i in range(3):
                split_w(N_CONV + 6 + i + AHEAD)
                split_h(J_CONV + i, u_hi, 2 * i)
            for i in range(4):
                split_w(N_O0 + i + AHEAD)
                act.wait_ge(xt_ready, 12 + i + 1)
                square_pair(5, i, flat(xT, 2 * i, 2 * i + 2))
            for q in range(4):
                split_h(J_H5 + q, h_hi, 2 * q)
            mlp(N_MLP1, J_MLP1)
            square_x(6)
            for q in range(4):
                split_h(J_KV + q, h_hi, 2 * q)
            for q in range(4):
                split_h(J_MIX1 + q, u_hi, 2 * q)
            act.wait_ge(sq_added, 24)
            for i in range(3):
                split_w(N_K + i + AHEAD)
                evac_qk(f"k{i}", N_K + i, flat(qk, 2 * i, 2 * i + 2))
            for i in range(3):
                split_w(N_Q + i + AHEAD)
                evac_qk(f"q{i}", N_Q + i, flat(big, 10 + 2 * i, 12 + 2 * i))
            split_w(N_Q + 3 + AHEAD)
            evac_qk("qm1", N_Q + 3, v_tok[:, 0, :])
            act.wait_ge(lam_dots, 1)
            act.activation(stat[:, S_LAM:S_LAM + 2], stat[:, S_DOT:S_DOT + 2], ACT.Exp).then_inc(lam_exp, 1)

            def evac_v_unit(i):
                act.wait_ge(unit_done, N_V + i + 1)
                act.activation(diff_v[:, :, 256 * i:256 * i + 256],
                               lin[lin_bank[N_V + i]][:, :].rearrange("p (t c) -> p t c", t=TT), ACT.Copy).then_inc(evac_a, 1)

            split_w(N_V + AHEAD)
            evac_v_unit(0)
            act.wait_ge(misc_full, misc_no["qk.qm1"] + 1)
            act.wait_ge(rope_done, len(ROPES))
            for g in range(2):
                exps(G_M1 + g, FULL_SPAN, from_bank=True)
                split_w(N_V + 1 + g + AHEAD)
                evac_v_unit(1 + g)
                copy_turned("mem1.", g, G_M1 + g, 512)
            def d_exps(h):
                act.wait_ge(d_max, h + 1)
                for m in range(2):
                    p = head_bias[:, 2 * (h % 2) + m, :]
                    for tt, (c0, c1) in enumerate(CAUSAL_SPAN):
                        at = 4 * (h % 2) + 2 * m + tt
                        last = act.activation(p[:, c0:c1], p[:, c0:c1], ACT.Exp, bias=stat[:, S_DNMAX + at:S_DNMAX + at + 1],
                                              accum_out=stat[:, S_DSUM + at:S_DSUM + at + 1])
                last.then_inc(d_exp, 1)

            d_exps(0)
            split_h(J_YM1, u_hi, 6)
            for h in range(DIFF_HEADS):
                if h + 1 < DIFF_HEADS:
                    d_exps(h + 1)
                act.wait_ge(d_turned, h + 1)
                if h >= 2:
                    act.wait_ge(misc_full, misc_no[f"pv{h - 2}"] + 1)
                act.activation(probsT[:, h % 2, 0:384], ps_ada[:, 0:384], ACT.Copy).then_inc(d_copied, 1)
                act.wait_ge(o_copied, h + 1)
                for tt in range(TT):
                    at = S_OSS + 2 * (h % 2) + tt
                    last = act.activation(probs[:, h % 2, tt * P:tt * P + P], y_tok[:, tt, (h % 2) * P:(h % 2) * P + P],
                                          ACT.Square, accum_out=stat[:, at:at + 1])
                last.then_inc(o_sq, 1)
                if h >= 2 and h % 2 == 0:
                    split_h(J_DIFF + h // 2 - 1, u_hi, h - 2)
            split_h(J_DIFF + 2, u_hi, 4)
            for i in range(4):
                if i < 3:
                    split_w(N_O1 + i + AHEAD)
                act.wait_ge(xt_ready, 20 + i + 1)
                square_pair(7, i, flat(xT, 2 * i, 2 * i + 2))
            for q in range(4):
                split_h(J_H7 + q, h_hi, 2 * q)
            mlp(N_MLP2, J_MLP2, AHEAD - 1)
            for i in range(4):
                act.wait_ge(out_turned, i + 1)
                tt, q = i // 2, i % 2
                act.activation(out_tok[:, tt, 512 * q:512 * q + 512], (lin[0], lin[1], ps_ada, ps_misc)[i][:, :], ACT.Copy)\
                    .then_inc(out_copied, 1)

        @block.gpsimd
        def _(pool):
            def split_h(job, lo, hi, tile, turn=None):
                pool.wait_ge(fresh_hi, job + 1 if turn is None else turn * 4 + (job + 1))
                pool.tensor_tensor(flat(lo, tile, tile + 2), fresh[:, job % 2, :], flat(hi, tile, tile + 2).bitcast(F32),
                                   ALU.subtract).then_inc(fresh_lo, 1)

            def power(name, width=512):
                pool.wait_ge(misc_read, misc_no[name] + 1)
                pool.tensor_tensor(rstd[:, 0:width], rstd[:, 0:width], minus_half[:, 0:1].to_broadcast([P, width]), ALU.pow)\
                    .then_inc(rstd_ready, 1)

            def add_squares(s):
                chained = 0
                for q in range(4):
                    pool.wait_ge(sq_ready, 4 * (s - 1) + q + 1)
                    if q == 0:
                        if s > 1:
                            pool.wait_ge(misc_full, misc_no[f"sum{s - 1}"] + 1)
                        pool.tensor_tensor(sq_sum, probs[:, 0, 0:T], probs[:, 0, T:2 * T], ALU.add).then_inc(sq_added, 1)
                        continue
                    pool.wait_ge(sq_added, 4 * (s - 1) + q)
                    pool.tensor_tensor(sq_sum, sq_sum, probs[:, q % 2, 0:T], ALU.add).then_inc(chain_g, 1)
                    pool.wait_ge(chain_g, 3 * (s - 1) + q)
                    pool.tensor_tensor(sq_sum, sq_sum, probs[:, q % 2, T:2 * T], ALU.add).then_inc(sq_added, 1)

            def cos_part(name, src):
                i = rope_no["rope." + name]
                pool.wait_ge(qk_normed, qk_no["qk." + name] + 1)
                if i >= 2:
                    pool.wait_ge(rope_done, i - 1)
                for a in range(2):
                    last = pool.tensor_tensor(probsT[:, i % 2, a * T:a * T + T], src[:, a * T:a * T + T], cosT, ALU.mult)
                last.then_inc(rope_cos, 1)

            pool.memset(minus_half[:, :], -0.5)
            pool.memset(rel[:, :], 1.0)
            pool.memset(rows, 0.0).then_inc(filled, 1)
            pool.memset(f_cum, 0.0)
            pool.wait_ge(mem_var, 1)
            pool.tensor_tensor(stat[:, S_MEM:S_MEM + 2], stat[:, S_MEM:S_MEM + 2], minus_half[:, 0:1].to_broadcast([P, 2]),
                               ALU.pow).then_inc(mem_rstd, 1)
            for q in range(4):
                split_h(J_MEM + q, u_lo, u_hi, 2 * q)
            power("qk.mem0")
            add_squares(1)
            pool.wait_ge(x_turned, 4)
            pool.tensor_copy(head_bias[:, :, 0:P], ident[:, 64:64 + HEADS].unsqueeze(2).to_broadcast([P, HEADS, P]))\
                .then_inc(sel_ready, 1)
            power("sum1", T)
            for q in range(4):
                split_h(J_H1 + q, h_lo, h_hi, 2 * q)
            power("qk.mem1")
            pool.wait_ge(f_copied, 4)
            mask = causal.unsqueeze(1).to_broadcast([P, HEADS, P])
            pool.tensor_tensor(head_bias[:, :, 0:P], head_bias[:, :, P:2 * P], mask, ALU.add)
            pool.tensor_tensor(head_bias[:, :, 2 * P:3 * P], head_bias[:, :, 2 * P:3 * P], mask, ALU.add).then_inc(fox_bias, 1)
            for q in range(2):
                split_h(J_FOX + q, u_lo, u_hi, 2 * q)
            pool.wait_ge(bias_in, 16)
            pool.wait_ge(picked, 1)
            pool.wait_ge(score_max, HEADS)
            pool.tensor_tensor(head_bias[:, :, 0:P], toeplitz[:, :, P:2 * P], idx[:, 0:P].unsqueeze(1).to_broadcast([P, HEADS, P]),
                               ALU.add)
            pool.tensor_tensor(head_bias[:, :, P:3 * P], toeplitz, idx[:, P:3 * P].unsqueeze(1).to_broadcast([P, HEADS, 2 * P]),
                               ALU.add).then_inc(dsa_bias, 1)
            for q in range(2):
                split_h(J_DSA + q, u_lo, u_hi, 4 + 2 * q)
            for q in range(4):
                split_h(J_MERGED + q, h_lo, h_hi, 2 * q)

            def norm(s, job=None):
                add_squares(s)
                power(f"sum{s}", T)
                if job is not None:
                    for q in range(4):
                        split_h(job + q, h_lo, h_hi, 2 * q)

            def mlp(job_u):
                for i in range(4):
                    split_h(job_u + i, u_lo, u_hi, 2 * (i % 4))
                with pool.Fori(0, MLP_LOOPS) as turn:
                    for i in range(4):
                        split_h(job_u + 4 + i, u_lo, u_hi, 2 * (i % 4), turn)

            norm(2, J_H2)
            mlp(J_MLP0)
            norm(3)
            norm(4, J_H4)
            power("qk.qm0")
            split_h(J_YM0, u_lo, u_hi, 6)
            for i in range(3):
                split_h(J_CONV + i, u_lo, u_hi, 2 * i)
            norm(5, J_H5)
            mlp(J_MLP1)
            norm(6, J_KV)
            for q in range(4):
                split_h(J_MIX1 + q, u_lo, u_hi, 2 * q)
            pool.wait_ge(late_in, 48)
            power("qk.k0")
            cos_part("k0", flat(qk, 0, 2))
            power("qk.k1")
            cos_part("k1", flat(qk, 2, 4))
            power("qk.k2")
            cos_part("k2", flat(qk, 4, 6))
            power("qk.q0")
            cos_part("q0", flat(big, 10, 12))
            power("qk.q1")
            cos_part("q1", flat(big, 12, 14))
            power("qk.q2")
            cos_part("q2", flat(big, 14, 16))
            power("qk.qm1")
            split_h(J_YM1, u_lo, u_hi, 6)
            for h in range(DIFF_HEADS):
                pool.wait_ge(o_var, h + 1)
                at = S_ORSTD + 2 * (h % 2)
                pool.tensor_tensor(stat[:, at:at + 2], stat[:, at:at + 2], minus_half[:, 0:1].to_broadcast([P, 2]), ALU.pow)\
                    .then_inc(o_rstd, 1)
                if h >= 2 and h % 2 == 0:
                    split_h(J_DIFF + h // 2 - 1, u_lo, u_hi, h - 2)
            split_h(J_DIFF + 2, u_lo, u_hi, 4)
            norm(7, J_H7)
            mlp(J_MLP2)

        @block.vector
        def _(dve):
            chain = Count()

            def link(ins):
                ins.then_inc(chain_v, 1)
                dve.wait_ge(chain_v, chain.up())

            def split_w(n, turn=None):
                if n >= N_UNITS:
                    return
                dve.wait_ge(hi_w, n + 1 if turn is None else turn * BODY + (n + 1))
                dve.tensor_tensor(w_lo[:, n % RING, :], w_raw[:, n % RING, :], w_hi[:, n % RING, :].bitcast(F32),
                                  ALU.subtract).then_inc(lo_w, 1)

            def from_misc(name):
                dve.wait_ge(misc_full, misc_no[name] + 1)

            def mean_square(name, width, count, eps=EPS):
                from_misc(name)
                dve.tensor_scalar(rstd[:, 0:width], ps_misc[:, 0:width], 1.0 / count, eps, ALU.mult, ALU.add)\
                    .then_inc(misc_read, 1)

            def fresh_slot(job):
                if job >= 2:
                    dve.wait_ge(fresh_lo, job - 1)
                return fresh[:, job % 2, :]

            def normed(job, gains, shift=None):
                for q in range(4):
                    dst = fresh_slot(job + q)
                    for i in range(2):
                        k = 2 * q + i
                        last = dve.scalar_tensor_tensor(out=dst[:, i * T:i * T + T], in0=xT[:, k, :], scalar=gains[:, k:k + 1],
                                                        in1=rstd[:, 0:T], op0=ALU.mult, op1=ALU.mult)
                    if shift is not None:
                        link(last)
                        for i in range(2):
                            k = 2 * q + i
                            last = dve.tensor_scalar(dst[:, i * T:i * T + T], dst[:, i * T:i * T + T], shift[:, k:k + 1], None,
                                                     ALU.add)
                    last.then_inc(fresh_ready, 1)
                dve.wait_ge(fresh_ready, job + 4)

            def qk_var(name):
                mean_square("qk." + name, 512, HD)

            def qk_scale(name, dst, gain):
                dve.wait_ge(rstd_ready, power_no["qk." + name] + 1)
                dve.scalar_tensor_tensor(out=dst, in0=dst, scalar=vec[:, gain:gain + 1], in1=rstd[:, :],
                                         op0=ALU.mult, op1=ALU.mult).then_inc(qk_normed, 1)
                dve.wait_ge(qk_normed, qk_no["qk." + name] + 1)

            def rope_add(name, dst):
                from_misc("rope." + name)
                tmp = flat(y_tok, 0, 1)
                for a in range(2):
                    last = dve.tensor_tensor(tmp[:, a * T:a * T + T], ps_misc[:, a * T:a * T + T], sinT, ALU.mult)
                last.then_inc(misc_read, 1)
                dve.wait_ge(misc_read, misc_no["rope." + name] + 1)
                i = rope_no["rope." + name]
                dve.wait_ge(rope_cos, i + 1)
                dve.tensor_tensor(dst, tmp, probsT[:, i % 2, :], ALU.add).then_inc(rope_done, 1)

            def maxima(G, span, biased):
                for odd in range(2):
                    h = 2 * G + odd
                    dve.wait_ge(score_mm, h + 1)
                    if h >= 2:
                        dve.wait_ge(turned, h - 1)
                    at = 2 * odd
                    if biased is not None:
                        for tt, (c0, c1) in enumerate(span):
                            last = dve.tensor_tensor_reduce(probs[:, odd, c0:c1], acc[odd][:, c0:c1],
                                                            head_bias[:, (2 * (G - biased)) + odd, c0:c1], 1.0, PICKED,
                                                            ALU.add, ALU.max, stat[:, S_MAX + at + tt:S_MAX + at + tt + 1])
                        link(last)
                    else:
                        link(dve.tensor_reduce(stat[:, S_MAX + at:S_MAX + at + 2],
                                               acc[odd][:, :].rearrange("p (t s) -> p t s", t=TT), AX.X, ALU.max))
                    dve.tensor_scalar(stat[:, S_NMAX + at:S_NMAX + at + 2], stat[:, S_MAX + at:S_MAX + at + 2], -1.0, None,
                                      ALU.mult).then_inc(score_max, 1)

            def attended(name, g, G, y_free=None):
                s0 = S_SUM + 4 * (G % 2)
                dve.wait_ge(exp_done, 2 * G + 2)
                link(dve.reciprocal(stat[:, S_INV:S_INV + 4], stat[:, s0:s0 + 4]))
                from_misc(f"{name}{g}")
                for odd in range(2):
                    for tt in range(TT):
                        at, c0 = 2 * odd + tt, (2 * g + odd) * HD
                        last = dve.tensor_scalar(y_tok[:, tt, c0:c0 + HD], ps_misc[:, at * HD:at * HD + HD],
                                                 stat[:, S_INV + at:S_INV + at + 1], None, ALU.mult)
                last.then_inc(misc_read, 1)

            def y_copy(job, bank_no, y_no):
                dve.wait_ge(y_turned, y_no)
                dve.tensor_copy(fresh_slot(job), acc[bank_no][:, :]).then_inc(fresh_ready, 1)

            from_misc("vec")
            dve.tensor_copy(vec[:, :], ps_misc[:, 0:2 * P]).then_inc(misc_read, 1)
            dve.wait_ge(misc_read, 1)
            dve.tensor_scalar(vec[:, V_BQ:V_BQ + 1], vec[:, V_BQ:V_BQ + 1], HD ** -0.5, None, ALU.mult)
            dve.tensor_scalar(vec[:, V_SUBLN:V_SUBLN + 1], vec[:, V_SUBLN:V_SUBLN + 1], 1.0 - LAM_INIT, None, ALU.mult)
            dve.tensor_scalar(vec[:, V_MQ:V_MQ + 2], vec[:, V_MQ:V_MQ + 2], HD ** -0.5, None, ALU.mult).then_inc(vec_ready, 1)
            dve.wait_ge(mem_sq, 1)
            dve.tensor_scalar(stat[:, S_MEM:S_MEM + 2], stat[:, S_MEM:S_MEM + 2], 1.0 / D, EPS, ALU.mult, ALU.add)\
                .then_inc(mem_var, 1)
            dve.wait_ge(mem_rstd, 1)
            for tt in range(TT):
                dve.tensor_scalar(mem_tok[:, tt, :], mem_tok[:, tt, :], stat[:, S_MEM + tt:S_MEM + tt + 1], None, ALU.mult)\
                    .then_inc(mem_scaled, 1)
            dve.wait_ge(vec_ready, 1)
            for q in range(4):
                dst = fresh_slot(J_MEM + q)
                dve.wait_ge(mem_turned, q + 1)
                for i in range(2):
                    k = 2 * q + i
                    last = dve.tensor_scalar(dst[:, i * T:i * T + T], acc[q][:, i * T:i * T + T], vec[:, V_MEM + k:V_MEM + k + 1],
                                             None, ALU.mult)
                last.then_inc(fresh_ready, 1)
            for n in range(AHEAD + 1):
                split_w(n)
            qk_var("mem0")
            qk_scale("mem0", flat(mem_k[:, 0], 0, 2), V_MK)
            split_w(4)
            mean_square("sum1", T, D)
            split_w(5)
            dve.wait_ge(ada_done, 8)
            dve.tensor_tensor(ada[:, 0:16], ps_ada[:, 0:16], vec[:, V_ADA:V_ADA + 16], ALU.add).then_inc(ada_ready, 1)
            dve.wait_ge(ada_ready, 1)
            link(dve.scalar_tensor_tensor(out=gs[:, 0, :], in0=ada[:, 8:16], scalar=1.0, in1=vec[:, V_G1:V_G1 + 8],
                                          op0=ALU.add, op1=ALU.mult))
            dve.wait_ge(rstd_ready, power_no["sum1"] + 1)
            normed(J_H1, gs[:, 0, :], ada[:, 0:8])
            split_w(6)
            qk_var("mem1")
            qk_scale("mem1", flat(mem_k[:, 1], 0, 2), V_MK + 1)
            split_w(7)
            z, low = idx[64:64 + HEADS, 0:T], rstd[64:64 + HEADS, 0:T]
            dve.wait_ge(evac_a, evac_value[4])
            dve.wait_ge(small_in, 48)
            link(dve.tensor_scalar(z, f_raw[64:64 + HEADS, :], rel[64:64 + HEADS, 0:1], None, ALU.add))
            link(dve.tensor_scalar(low, z, -1.0, None, ALU.mult))
            dve.tensor_tensor(low, low, z, ALU.min).then_inc(f_in, 1)
            split_w(8)
            from_misc("wi")
            for tt in range(TT):
                last = dve.tensor_scalar(stat[:, S_WI + 4 * tt:S_WI + 4 * tt + 4], ps_misc[:, tt * P:tt * P + 4],
                                         IDX_HEADS ** -0.5, None, ALU.mult)
            last.then_inc(misc_read, 1)
            dve.wait_ge(f_ln, 1)
            link(dve.scalar_tensor_tensor(out=z, in0=z, scalar=0.0, in1=low, op0=ALU.min, op1=ALU.subtract))
            dve.tensor_tensor_scan(f_cum[64:64 + HEADS, :], ones[64:64 + HEADS, 0:1].to_broadcast([HEADS, T]), z, 0.0,
                                   ALU.mult, ALU.add).then_inc(f_ready, 1)
            dve.wait_ge(f_ready, 1)
            split_w(9)
            for h in range(IDX_HEADS):
                dve.wait_ge(idx_relu, h + 1)
                if h:
                    dve.wait_ge(idx_added, h)
                for tt, (c0, c1) in enumerate(CAUSAL_SPAN):
                    wi = stat[:, S_WI + 4 * tt + h:S_WI + 4 * tt + h + 1]
                    if h == 0:
                        dve.wait_ge(misc_read, misc_no["wi"] + 1)
                        last = dve.tensor_scalar(idx[:, c0:c1], probs[:, 0, c0:c1], wi, None, ALU.mult)
                    else:
                        last = dve.scalar_tensor_tensor(out=idx[:, c0:c1], in0=probs[:, h % 2, c0:c1], scalar=wi,
                                                        in1=idx[:, c0:c1], op0=ALU.mult, op1=ALU.add)
                last.then_inc(idx_added, 1)
            dve.wait_ge(idx_added, IDX_HEADS)
            dve.tensor_tensor(idx[:, 0:P], idx[:, 0:P], causal, ALU.add)
            link(dve.tensor_tensor(idx[:, 2 * P:3 * P], idx[:, 2 * P:3 * P], causal, ALU.add))

            def pick_eight():
                for tt, (c0, c1) in enumerate(CAUSAL_SPAN):
                    last = dve.max(top8[:, tt, :], idx[:, c0:c1])
                link(last)
                for tt, (c0, c1) in enumerate(CAUSAL_SPAN):
                    last = dve.match_replace(out=idx[:, c0:c1], in_to_replace=top8[:, tt, :], in_values=idx[:, c0:c1],
                                             imm_value=PICKED)
                link(last)

            pick_eight()
            for n in (10, 11):
                split_w(n)
                pick_eight()
            split_w(12)
            pick_eight()
            from_misc("row")
            dve.tensor_copy(bias_row[0:HEADS, :], ps_misc[0:HEADS, 0:384]).then_inc(misc_read, 1)
            split_w(13)
            pick_eight()
            split_w(14)
            pick_eight()
            dve.wait_ge(ada_done, 24)
            link(dve.tensor_tensor(ada[:, 16:48], ps_ada[:, 16:48], vec[:, V_ADA + 16:V_ADA + 48], ALU.add))
            dve.scalar_tensor_tensor(out=gs[:, 1, :], in0=ada[:, 32:40], scalar=1.0, in1=vec[:, V_G2:V_G2 + 8],
                                     op0=ALU.add, op1=ALU.mult)
            dve.wait_ge(fox_bias, 1)

            def sigmoid(n, tile):
                dve.wait_ge(evac_a, evac_value[n])
                gate = flat(big, tile, tile + 2)
                dve.tensor_scalar(gate, gate, 0.5, 0.5, ALU.mult, ALU.add)

            for g in range(4):
                maxima(G_FOX + g, CAUSAL_SPAN, G_FOX)
                split_w(N_GF + g + AHEAD)
                if g < 2:
                    pick_eight()
                if g == 2:
                    dve.tensor_scalar(idx[:, :], idx[:, :], PICKED, MASKED, ALU.not_equal, ALU.mult).then_inc(picked, 1)
                sigmoid(N_GF + g, 2 * g)
                attended("fox", g, G_FOX + g)
            split_w(N_DSA + AHEAD)
            for q in range(2):
                y_copy(J_FOX + q, q, q + 1)
            for i in range(1, 6):
                split_w(N_DSA + i + AHEAD)
            dve.wait_ge(dsa_bias, 1)
            for g in range(4):
                maxima(G_DSA + g, CAUSAL_SPAN, G_DSA)
                split_w(N_GD + g + AHEAD)
                sigmoid(N_GD + g, 8 + 2 * g)
                attended("dsa", g, G_DSA + g)
            for half in range(2):
                split_w(N_BR + half + AHEAD)
                dve.wait_ge(unit_done, N_BR + half + 1)
                for q in (2 * half, 2 * half + 1):
                    gate = flat(big, 2 * q, 2 * q + 2)
                    dve.tensor_tensor(gate, gate, acc[q][:, :], ALU.mult).then_inc(branch_done, 1)
            for q in range(2):
                y_copy(J_DSA + q, q, 2 + q + 1)
            for half in range(2):
                split_w(N_BR + 2 + half + AHEAD)
                dve.wait_ge(unit_done, N_BR + 2 + half + 1)
                for q in (2 * half, 2 * half + 1):
                    gate = flat(big, 8 + 2 * q, 8 + 2 * q + 2)
                    link(dve.tensor_tensor(gate, gate, acc[q][:, :], ALU.mult))
                    dve.tensor_tensor(fresh_slot(J_MERGED + q), gate, flat(big, 2 * q, 2 * q + 2), ALU.add)\
                        .then_inc(fresh_ready, 1)
            for i in range(4):
                n = N_OUT + i
                split_w(n + AHEAD)
                dve.wait_ge(unit_done, n + 1)
                for j in range(2):
                    k = 2 * i + j
                    last = dve.scalar_tensor_tensor(out=xT[:, k, :], in0=lin[lin_bank[n]][:, j * T:j * T + T],
                                                    scalar=ada[:, 16 + k:17 + k], in1=xT[:, k, :], op0=ALU.mult, op1=ALU.add)
                    if j == 0:
                        continue
                    last.then_inc(evac_v, 1)
                dve.drain().then_inc(xt_ready, 1)
            mean_square("sum2", T, D)
            dve.wait_ge(rstd_ready, power_no["sum2"] + 1)
            normed(J_H2, gs[:, 1, :], ada[:, 24:32])

            halves = Count()

            def mlp(n0, job_u, gate=None, ahead=AHEAD):
                def up_step(n, step, turn=None):
                    at = lambda value, per: value if turn is None else turn * per + value
                    for half in range(2):
                        split_w(n + half + ahead, turn)
                        dve.wait_ge(evac_a, at(evac_value[n + half], 4))
                        dve.tensor_tensor(fresh[:, half, :], fresh[:, half, :], fresh[:, half, :], ALU.mult)\
                            .then_inc(fresh_ready, 1)

                def down_step(n, turn=None):
                    for half in range(2):
                        split_w(n + half + ahead, turn)

                up_step(n0, 0)
                up_step(n0 + 2, 1)
                down_step(n0 + 4)
                with dve.Fori(0, MLP_LOOPS) as turn:
                    for k in range(2):
                        up_step(n0 + 6 + 4 * k, 2 + k, turn)
                        down_step(n0 + 8 + 4 * k, turn)
                down_step(n0 + 30)
                for q in range(4):
                    if q % 2 == 0:
                        dve.wait_ge(half_done, halves.up())
                    else:
                        dve.wait_ge(unit_done, n0 + 30 + q // 2 + 1)
                    if gate is None:
                        pair = flat(xT, 2 * q, 2 * q + 2)
                        dve.tensor_tensor(pair, acc[q][:, :], pair, ALU.add).then_inc(xt_ready, 1)
                    else:
                        for j in range(2):
                            k = 2 * q + j
                            last = dve.scalar_tensor_tensor(out=xT[:, k, :], in0=acc[q][:, j * T:j * T + T],
                                                            scalar=gate[:, k:k + 1], in1=xT[:, k, :], op0=ALU.mult, op1=ALU.add)
                        last.then_inc(xt_ready, 1)

            mlp(N_MLP0, J_MLP0, ada[:, 40:48])
            mean_square("sum3", T, D)
            dve.wait_ge(rstd_ready, power_no["sum3"] + 1)
            for q in range(4):
                for j in range(2):
                    k = 2 * q + j
                    last = dve.scalar_tensor_tensor(out=xT[:, k, :], in0=xT[:, k, :], scalar=vec[:, V_GF + k:V_GF + k + 1],
                                                    in1=rstd[:, 0:T], op0=ALU.mult, op1=ALU.mult)
                last.then_inc(xt_ready, 1)
            mean_square("sum4", T, D)
            dve.wait_ge(rstd_ready, power_no["sum4"] + 1)
            dve.wait_ge(xt_ready, 12)
            normed(J_H4, vec[:, V_MIX:V_MIX + 8])
            split_w(N_QM0 + AHEAD)
            split_w(N_CONV + AHEAD)
            qk_var("qm0")
            qk_scale("qm0", v_tok[:, 0, :], V_MQ)
            split_w(N_CONV + 1 + AHEAD)
            split_w(N_CONV + 2 + AHEAD)

            def conv(i):
                n = N_CONV + 3 + i
                dve.wait_ge(unit_done, n + 1)
                dve.wait_ge(evac_a, evac_value[N_CONV + i])
                c = flat(big, 2 * i, 2 * i + 2)
                dve.tensor_tensor(c, c, lin[lin_bank[n]][:, :], ALU.mult).then_inc(evac_v, 1)
                dve.wait_ge(evac_v, evac_value[n])
                for tap, back in ((V_CONV + 12, 0), (V_CONV + 6, 1), (V_CONV, 2)):
                    for j in range(2):
                        k = 2 * i + j
                        u, y, tap_w = big[:, k, :], big[:, 6 + k, :], vec[:, tap + k:tap + k + 1]
                        if back == 0:
                            last = dve.tensor_scalar(y, u, tap_w, None, ALU.mult)
                        else:
                            last = dve.scalar_tensor_tensor(out=y[:, back:T], in0=u[:, 0:T - back], scalar=tap_w,
                                                            in1=y[:, back:T], op0=ALU.mult, op1=ALU.add)
                    link(last)

            for g in range(2):
                maxima(G_M0 + g, FULL_SPAN, None)
                split_w(N_CONV + 3 + g + AHEAD)
                conv(g)
                attended("mem0.", g, G_M0 + g)
            split_w(N_CONV + 5 + AHEAD)
            conv(2)
            y_copy(J_YM0, 0, 5)
            for i in range(3):
                n = N_CONV + 6 + i
                split_w(n + AHEAD)
                dve.wait_ge(unit_done, n + 1)
                dst = fresh_slot(J_CONV + i)
                dve.tensor_tensor(dst, flat(big, 6 + 2 * i, 8 + 2 * i), lin[lin_bank[n]][:, :], ALU.mult).then_inc(evac_v, 1)
                dve.drain().then_inc(fresh_ready, 1)

            def residual(n0, splits=4):
                for i in range(4):
                    n = n0 + i
                    if i < splits:
                        split_w(n + AHEAD)
                    dve.wait_ge(unit_done, n + 1)
                    pair = flat(xT, 2 * i, 2 * i + 2)
                    dve.tensor_tensor(pair, lin[lin_bank[n]][:, :], pair, ALU.add).then_inc(evac_v, 1)
                    dve.drain().then_inc(xt_ready, 1)

            residual(N_O0)
            mean_square("sum5", T, D)
            dve.wait_ge(rstd_ready, power_no["sum5"] + 1)
            normed(J_H5, vec[:, V_MLP:V_MLP + 8])
            mlp(N_MLP1, J_MLP1)
            mean_square("sum6", T, D)
            dve.wait_ge(rstd_ready, power_no["sum6"] + 1)
            normed(J_KV, vec[:, V_KV:V_KV + 8])
            normed(J_MIX1, vec[:, V_MIX + 8:V_MIX + 16])
            dve.wait_ge(late_in, 48)
            split_w(N_K + AHEAD)
            dve.tensor_tensor_reduce(lam_in[:, 0, :], lam_in[:, 0, :], lam_in[:, 1, :], 1.0, 0.0, ALU.mult, ALU.add,
                                     stat[:, S_DOT:S_DOT + 1])
            dve.tensor_tensor_reduce(lam_in[:, 2, :], lam_in[:, 2, :], lam_in[:, 3, :], 1.0, 0.0, ALU.mult, ALU.add,
                                     stat[:, S_DOT + 1:S_DOT + 2]).then_inc(lam_dots, 1)
            split_w(N_K + 1 + AHEAD)
            qk_var("k0")
            qk_scale("k0", flat(qk, 0, 2), V_K)
            split_w(N_K + 2 + AHEAD)
            qk_var("k1")
            rope_add("k0", flat(qk, 0, 2))
            qk_scale("k1", flat(qk, 2, 4), V_K)
            split_w(N_Q + AHEAD)
            qk_var("k2")
            rope_add("k1", flat(qk, 2, 4))
            qk_scale("k2", flat(qk, 4, 6), V_K)
            split_w(N_Q + 1 + AHEAD)
            qk_var("q0")
            rope_add("k2", flat(qk, 4, 6))
            qk_scale("q0", flat(big, 10, 12), V_BQ)
            split_w(N_Q + 2 + AHEAD)
            qk_var("q1")
            rope_add("q0", flat(big, 10, 12))
            qk_scale("q1", flat(big, 12, 14), V_BQ)
            split_w(N_Q + 3 + AHEAD)
            qk_var("q2")
            rope_add("q1", flat(big, 12, 14))
            qk_scale("q2", flat(big, 14, 16), V_BQ)
            split_w(N_V + AHEAD)
            qk_var("qm1")
            rope_add("q2", flat(big, 14, 16))
            qk_scale("qm1", v_tok[:, 0, :], V_MQ + 1)
            dve.wait_ge(lam_exp, 1)
            link(dve.tensor_tensor(stat[:, S_NLAM:S_NLAM + 1], stat[:, S_LAM + 1:S_LAM + 2], stat[:, S_LAM:S_LAM + 1],
                                   ALU.subtract))
            dve.tensor_scalar(stat[:, S_NLAM:S_NLAM + 1], stat[:, S_NLAM:S_NLAM + 1], -LAM_INIT, None, ALU.add)
            for g in range(2):
                maxima(G_M1 + g, FULL_SPAN, None)
                split_w(N_V + 1 + g + AHEAD)
                attended("mem1.", g, G_M1 + g)

            def d_maxima(h):
                dve.wait_ge(d_score, h + 1)
                if h >= 2:
                    dve.wait_ge(d_turned, h - 1)
                for m in range(2):
                    for tt, (c0, c1) in enumerate(CAUSAL_SPAN):
                        at = 4 * (h % 2) + 2 * m + tt
                        last = dve.tensor_tensor_reduce(head_bias[:, 2 * (h % 2) + m, c0:c1], acc[2 * (h % 2) + m][:, c0:c1],
                                                        chunk_mask[:, c0:c1], 1.0, PICKED, ALU.add, ALU.max,
                                                        stat[:, S_DMAX + at:S_DMAX + at + 1])
                link(last)
                at = 4 * (h % 2)
                dve.tensor_scalar(stat[:, S_DNMAX + at:S_DNMAX + at + 4], stat[:, S_DMAX + at:S_DMAX + at + 4], -1.0, None,
                                  ALU.mult).then_inc(d_max, 1)

            def mix(h):
                dve.wait_ge(d_exp, h + 1)
                at = 4 * (h % 2)
                inv = stat[:, S_DINV + at:S_DINV + at + 4]
                link(dve.reciprocal(inv, stat[:, S_DSUM + at:S_DSUM + at + 4]))
                link(dve.tensor_scalar(inv[:, 2:4], inv[:, 2:4], stat[:, S_NLAM:S_NLAM + 1], None, ALU.mult))
                p1, p2 = head_bias[:, 2 * (h % 2), :], head_bias[:, 2 * (h % 2) + 1, :]
                for tt, (c0, c1) in enumerate(CAUSAL_SPAN):
                    last = dve.tensor_scalar(p2[:, c0:c1], p2[:, c0:c1], inv[:, 2 + tt:3 + tt], None, ALU.mult)
                link(last)
                for tt, (c0, c1) in enumerate(CAUSAL_SPAN):
                    last = dve.scalar_tensor_tensor(out=p1[:, c0:c1], in0=p1[:, c0:c1], scalar=inv[:, tt:tt + 1],
                                                    in1=p2[:, c0:c1], op0=ALU.mult, op1=ALU.add)
                last.then_inc(mixed, 1)

            def o_copy(h):
                from_misc(f"pv{h}")
                c0 = (h % 2) * P
                for tt in range(TT):
                    last = dve.tensor_copy(y_tok[:, tt, c0:c0 + P], ps_misc[:, tt * P:tt * P + P])
                last.then_inc(misc_read, 1)
                dve.drain().then_inc(o_copied, 1)

            def o_mean(h):
                dve.wait_ge(o_sq, h + 1)
                at = 2 * (h % 2)
                dve.tensor_scalar(stat[:, S_ORSTD + at:S_ORSTD + at + 2], stat[:, S_OSS + at:S_OSS + at + 2], 1.0 / (2 * HD),
                                  SUBLN_EPS, ALU.mult, ALU.add).then_inc(o_var, 1)

            def o_scale(h):
                dve.wait_ge(o_rstd, h + 1)
                c0 = (h % 2) * P
                for tt in range(TT):
                    at = S_ORSTD + 2 * (h % 2) + tt
                    last = dve.tensor_scalar(y_tok[:, tt, c0:c0 + P], y_tok[:, tt, c0:c0 + P], stat[:, at:at + 1], None, ALU.mult)
                last.then_inc(o_scaled, 1)

            def o_take(h):
                job = J_DIFF + h // 2
                from_misc(f"oT{h}")
                dst = fresh_slot(job)[:, (h % 2) * T:(h % 2) * T + T]
                dve.tensor_scalar(dst, ps_misc[:, 0:T], vec[:, V_SUBLN:V_SUBLN + 1], None, ALU.mult).then_inc(misc_read, 1)
                if h % 2:
                    dve.drain().then_inc(fresh_ready, 1)

            y_copy(J_YM1, 0, 6)
            d_maxima(0)
            for h in range(DIFF_HEADS):
                mix(h)
                if h >= 1:
                    o_mean(h - 1)
                if h + 1 < DIFF_HEADS:
                    d_maxima(h + 1)
                if h >= 1:
                    o_scale(h - 1)
                o_copy(h)
                if h >= 1:
                    o_take(h - 1)
            o_mean(DIFF_HEADS - 1)
            o_scale(DIFF_HEADS - 1)
            o_take(DIFF_HEADS - 1)
            residual(N_O1, 3)
            mean_square("sum7", T, D)
            dve.wait_ge(rstd_ready, power_no["sum7"] + 1)
            normed(J_H7, vec[:, V_MLP + 8:V_MLP + 16])
            mlp(N_MLP2, J_MLP2, ahead=AHEAD - 1)


_WEIGHTS = {"w_ada": "w_ada", "w_in": "w_in", "w_branch_fox": "w_branch_fox", "w_branch_dsa": "w_branch_dsa",
            "w_out": "w_out", "w_mlp1": "w_mlp1", "w_mlp2": "w_mlp2", "a_w_in": "a_w_in_2", "b_w_q": "b_w_q_2",
            "w_kv": "w_kv_2", "w_mem_kv": "w_mem_kv_2", "w_o": "w_o_2", "w_up": "w_up_2", "w_down": "w_down_2"}
_VECTORS = {"c": "c", "b_ada": "b_ada", "g_norm1": "g_norm1", "g_norm2": "g_norm2", "g_final": "g_final",
            "norm_mix": "norm_mix_2", "norm_mlp": "norm_mlp_2", "kv_norm": "kv_norm_2", "mem_norm": "mem_norm_2",
            "a_conv": "a_conv_2", "b_subln": "b_subln_2", "b_q_norm": "b_q_norm_2", "k_norm": "k_norm_2",
            "mem_q_norm": "mem_q_norm_2", "mem_k_norm": "mem_k_norm_2", "rel_bias": "rel_bias",
            "b_forget": "b_forget", "b_lam": "b_lam_2"}


def kernel(**inputs):
    import numpy as _np
    import concourse.bacc as _bacc
    from concourse import mybir as _mybir
    from concourse.bass_utils import run_bass_kernel_spmd as _run

    nc = _bacc.Bacc("TRN2", target_bir_lowering=False, num_devices=1)
    arrays = {}

    def give(name, a):
        a = _np.ascontiguousarray(a)
        arrays[f"in_{name}"] = a
        return nc.dram_tensor(f"in_{name}", a.shape, _mybir.dt.from_np(a.dtype), kind="ExternalInput").ap()

    x = give("x", _np.asarray(inputs["x"]).reshape(T, D))
    w = {name: give(name, inputs[key]) for name, key in _WEIGHTS.items()}
    vectors = {name: give(name, _np.asarray(inputs[key]).reshape(-1)) for name, key in _VECTORS.items()}
    vectors["mem"] = give("mem", _np.asarray(inputs["mem_2"]).reshape(T, D))
    tables = {name: give(name, table) for name, table in host_tables().items()}
    out = nc.dram_tensor("out_dram", (1, T, D), _mybir.dt.float32, kind="ExternalOutput").ap()
    two_blocks(nc, x, w, vectors, tables, out.rearrange("b t d -> (b t) d"))
    r = _run(nc, [arrays], core_ids=[0])
    return r.results[0]["out_dram"]
```

```python
from contextlib import ExitStack

import numpy as np

import concourse.bass as bass
from concourse import mybir

F32 = mybir.dt.float32
F32R = mybir.dt.float32r
ALU = mybir.AluOpType
ACT = mybir.ActivationFunctionType
AX = mybir.AxisListType

P = 128
T = 256
TT = T // P
D = 1024
KT = D // P
HD = 64
HEADS = 8
IDX_HEADS = 4
TOPK = T // 4
FF = 4 * D
MEM_HEADS = 4
MEM_W = MEM_HEADS * HD
MAIN_W = D - MEM_W
CT = MAIN_W // P
DIFF_HEADS = MAIN_W // (2 * HD)
EPS = 1e-6
SUBLN_EPS = 1e-5
LAM_INIT = 0.8 - 0.6 * float(np.exp(-0.3 * 1))
MASKED = -1e30
PICKED = -3e38

C_QF, C_KF, C_VF, C_F = 0, 512, 1024, 1536
C_QD, C_KD, C_VD = 1544, 2056, 2568
C_QI, C_KI, C_WI = 3080, 3336, 3400
C_GF, C_GD = 3404, 4428

V_C, V_ADA, V_G1, V_G2, V_GF, V_MIX, V_MLP, V_KV, V_MEM = 0, 8, 56, 64, 72, 80, 96, 112, 120
V_CONV, V_SUBLN, V_BQ, V_K, V_MQ, V_MK = 128, 146, 147, 148, 149, 151
VEC_ROWS2 = 25

RING = 4
AHEAD = 3
FF_STEPS = FF // 512
MLP_LOOPS = 3
BODY = 8


ADA_UNITS = 24
ADA_FIRST = 8


def plan_loads():
    order = [("w", 0), ("a", 0), ("w", 1), ("a", 1), ("a", 2), ("w", 2)] + [("a", a) for a in range(3, ADA_FIRST)]
    order += [("w", 3), ("w", 4)]
    a = ADA_FIRST
    for n in range(5, N_UNITS):
        order.append(("w", n))
        if a < ADA_UNITS and n % 5 != 4:
            order.append(("a", a))
            a += 1
    return order


def plan_units(w):
    units = []

    def n_unit(name, src, col, user, pieces=None):
        cols = src.rearrange("(k p) n -> p k n", p=P)
        pieces = pieces or [(0, col, 256)]
        units.append(("N", name, [(at, cols[:, :, c:c + width]) for at, c, width in pieces], user))

    def k_unit(name, src, row, col, user=None):
        rows = src[row:row + 512, col:col + 512].rearrange("(k p) n -> p k n", p=P)
        units.append(("K", name, [(0, rows)], user))

    def mlp(name, up, down):
        for j in range(FF_STEPS + 1):
            if j < FF_STEPS:
                n_unit(f"{name}.up", up, 512 * j, "a")
                n_unit(f"{name}.up", up, 512 * j + 256, "a")
            if j >= 1:
                k_unit(f"{name}.down", down, 512 * (j - 1), 0)
                k_unit(f"{name}.down", down, 512 * (j - 1), 512)

    for l in range(2):
        n_unit(f"mem{l}.k", w["w_mem_kv"][l], 0, "a")
        n_unit(f"mem{l}.v", w["w_mem_kv"][l], MEM_W, "a")
    w_in = w["w_in"]
    n_unit("idx.k", w_in, 0, "a", [(0, C_KI, 64), (64, C_KI, 128), (192, C_F, 64)])
    n_unit("idx.q", w_in, C_QI, "a")
    for c in (C_QF, C_KF, C_VF):
        n_unit("fox", w_in, c, "a")
        n_unit("fox", w_in, c + 256, "a")
    for i in range(4):
        n_unit("gate.fox", w_in, C_GF + 256 * i, "a")
    for c in (C_QD, C_KD, C_VD):
        n_unit("dsa", w_in, c, "a")
        n_unit("dsa", w_in, c + 256, "a")
    for i in range(4):
        n_unit("gate.dsa", w_in, C_GD + 256 * i, "a")
    for name in ("w_branch_fox", "w_branch_dsa"):
        k_unit("branch", w[name], 0, 0)
        k_unit("branch", w[name], 0, 512)
    for i in range(4):
        n_unit("out", w["w_out"], 256 * i, "v")
    mlp("mlp0", w["w_mlp1"], w["w_mlp2"])
    a_in = w["a_w_in"][0]
    n_unit("qm0", a_in, 3 * MAIN_W, "a")
    for c, user in ((MAIN_W, "a"), (2 * MAIN_W, "v"), (0, "v")):
        for i in range(3):
            n_unit("conv", a_in, c + 256 * i, user)
    for i in range(4):
        n_unit("o0", w["w_o"][0], 256 * i, "v")
    mlp("mlp1", w["w_up"][0], w["w_down"][0])
    for i in range(3):
        n_unit("k", w["w_kv"], 256 * i, "a")
    for i in (3, 0, 1, 2):
        n_unit("q", w["b_w_q"][0], 256 * i, "a")
    for i in range(3):
        n_unit("v", w["w_kv"], MAIN_W + 256 * i, "a")
    for i in range(4):
        n_unit("o1", w["w_o"][1], 256 * i, "v")
    mlp("mlp2", w["w_up"][1], w["w_down"][1])
    return units


N_MEM, N_IDX, N_FOX, N_GF, N_DSA, N_GD, N_BR, N_OUT, N_MLP0 = 0, 4, 6, 12, 16, 22, 26, 30, 34
N_QM0, N_CONV, N_O0, N_MLP1, N_K, N_Q, N_V, N_O1, N_MLP2 = 66, 67, 76, 80, 112, 115, 119, 122, 126
N_UNITS = 158

MISC = (["vec", "qk.mem0", "sum1", "qk.mem1", "wi", "row"] + [f"fox{g}" for g in range(4)]
        + [f"dsa{g}" for g in range(4)] + ["sum2", "sum3", "sum4", "qk.qm0", "mem0.0", "mem0.1", "sum5", "sum6",
           "qk.k0", "qk.k1", "qk.k2", "rope.k0", "qk.qm1", "rope.k1", "qk.q0", "rope.k2", "qk.q1", "qk.q2", "rope.q0",
           "rope.q1", "mem1.0", "rope.q2", "mem1.1", "pv0"]
        + [f"{what}{h - (what == 'oT')}" for h in range(1, DIFF_HEADS) for what in ("pv", "oT")] + ["oT5", "sum7"])
POWERS = [m for m in MISC if m[:3] in ("sum", "qk.")]
QK_NORMS = [m for m in MISC if m.startswith("qk.")]
ROPES = [m for m in MISC if m.startswith("rope.")]
SPREAD = ["sum1", "qk.mem0", "qk.mem1"] + [m for m in POWERS if m not in ("sum1", "qk.mem0", "qk.mem1")]

J_MEM, J_H1, J_FOX, J_DSA, J_MERGED, J_H2, J_MLP0 = 0, 4, 8, 10, 12, 16, 20
J_H4, J_YM0, J_CONV, J_H5, J_MLP1 = 36, 40, 41, 44, 48
J_KV, J_MIX1, J_YM1, J_DIFF, J_H7, J_MLP2 = 64, 68, 72, 73, 76, 80
G_FOX, G_DSA, G_M0, G_M1 = 0, 4, 8, 10


class Count:

    def __init__(self):
        self.n, self.turn, self.per = 0, None, 0

    def up(self, k=1):
        self.n += k
        return self.now()

    def now(self, off=0):
        v = self.n + off
        return v if self.turn is None else self.turn * self.per + v

    def enter(self, turn, per):
        self.turn, self.per, self.entered = turn, per, self.n

    def leave(self, turns):
        assert self.n - self.entered == self.per, (self.n - self.entered, self.per)
        self.n = self.entered + self.per * turns
        self.turn = None


def host_tables():
    t = np.arange(P)
    ident = np.eye(P, dtype=np.float32)
    ones = np.ones((P, P), np.float32)
    heads2 = (t[:, None] // HD == t[None, :] // HD).astype(np.float32)
    causal = np.where(t[None, :] <= t[:, None], 0, MASKED).astype(np.float32)
    chunk = np.where(t[None, :] // 64 <= t[:, None] // 64, 0, MASKED).astype(np.float32)
    consts = np.concatenate([ident, ones, heads2, causal], 1)
    chunks = np.concatenate([chunk, np.zeros((P, P), np.float32), chunk], 1)
    half = 8
    inv = (1.0 / (np.float32(500000.0) ** (np.arange(0, 2 * half, 2, dtype=np.float32) / np.float32(2 * half))))
    ang = np.arange(T, dtype=np.float32)[None, :] * inv.astype(np.float32)[:, None]
    cos, sin = np.ones((P, T), np.float32), np.zeros((P, T), np.float32)
    perm = np.zeros((P, P), np.float32)
    for base in (0, HD):
        for i in range(half):
            cos[base + i] = cos[base + half + i] = np.cos(ang[i])
            sin[base + i] = sin[base + half + i] = np.sin(ang[i])
            perm[base + half + i, base + i] = -1.0
            perm[base + i, base + half + i] = 1.0
    rope = np.concatenate([cos, sin, perm], 1)
    dist = 255 - np.arange(384)
    n = np.maximum(dist, 0)
    large = 16 + (np.log(np.maximum(n, 1).astype(np.float32) / np.float32(16)) / np.float32(np.log(8.0))
                  * np.float32(16)).astype(np.int32)
    bucket = np.where(n < 16, n, np.minimum(large, 31))
    buckets = np.zeros((33, 384), np.float32)
    buckets[bucket, np.arange(384)] = dist >= 0
    buckets[32] = np.where(dist >= 0, 0, MASKED)
    return {"consts": consts, "chunks": chunks, "rope": rope, "buckets": buckets}


def two_blocks(nc, x, w, vectors, tables, out):
    units = plan_units(w)
    assert len(units) == N_UNITS
    loads = plan_loads()
    slot_of, value_of, slot_count = {}, {}, [0] * RING
    for i, (kind, n) in enumerate(loads):
        slot_count[i % RING] += 16 * (len(units[n][2]) if kind == "w" else 1)
        slot_of[kind, n], value_of[kind, n] = i % RING, slot_count[i % RING]
    assert all(slot_of["w", n] == n % RING for n in range(N_MLP0, N_UNITS))
    lin_bank, before, evac_value = [], [], []
    emptied, order = {"a": 0, "v": 0}, []
    for n, (_, _, _, user) in enumerate(units):
        lin_bank.append(len(order) % 2 if user else None)
        before.append(order[-2] if user and len(order) >= 2 else None)
        if user:
            emptied[user] += 1
            order.append((user, emptied[user]))
        evac_value.append(emptied[user] if user else None)

    misc_no = {name: i for i, name in enumerate(MISC)}
    power_no = {name: i for i, name in enumerate(POWERS)}
    spread_no = {name: i for i, name in enumerate(SPREAD)}
    root_at, root_columns = {}, 0
    for name in POWERS:
        root_at[name] = root_columns
        root_columns += 2 if name.startswith("sum") else 8
    qk_no = {name: i for i, name in enumerate(QK_NORMS)}
    rope_no = {name: i for i, name in enumerate(ROPES)}

    ctx = ExitStack()
    with ctx:
        def sb(name, shape, dt=F32):
            return ctx.enter_context(nc.sbuf_tensor(name, shape, dt))

        def sem(name):
            return ctx.enter_context(nc.semaphore(name))

        w_raw = sb("w_raw", [P, RING, 2048])
        w_hi = sb("w_hi", [P, RING, 2048], F32R)
        w_lo = sb("w_lo", [P, RING, 2048], F32R)
        xT = sb("xT", [P, KT, T])
        h_hi = sb("h_hi", [P, KT, T], F32R)
        h_lo = sb("h_lo", [P, KT, T], F32R)
        u_hi = sb("u_hi", [P, KT, T], F32R)
        u_lo = sb("u_lo", [P, KT, T], F32R)
        fresh = sb("fresh", [P, 2, 512])
        qk = sb("qk", [P, 8, T])
        v_tok = sb("v_tok", [P, TT, 512])
        big = sb("big", [P, 16, T])
        head_bias = sb("head_bias", [P, HEADS, 384])
        idx = sb("idx", [P, 384])
        probs = sb("probs", [P, 2, 512])
        probsT = sb("probsT", [P, 2, 512])
        y_tok = sb("y_tok", [P, TT, 512])
        mem_k = sb("mem_k", [P, 2, 2, T])
        mem_v = sb("mem_v", [P, 2, TT, MEM_W])
        consts = sb("consts", [P, 4 * P])
        vec = sb("vec", [P, 2 * P])
        ada = sb("ada", [P, 48])
        gs = sb("gs", [P, 2, KT])
        root = sb("root", [P, root_columns])
        ada_late = sb("ada_late", [P, 2, T])
        stat = sb("stat", [P, 96])
        top8 = sb("top8", [P, 2, 8])
        minus_half = sb("minus_half", [P, 1])
        rel = sb("rel", [P, 8])

        def flat(t, a, b):
            return t[:, a:b, :].rearrange("p a n -> p (a n)")

        ident, ones, heads2, causal = (consts[:, i * P:i * P + P] for i in range(4))
        ada_row = flat(big, 0, 8)[0:1, :]
        mem_tok = flat(qk, 0, 8).rearrange("p (t n) -> p t n", t=TT)
        x_tok = flat(head_bias, 0, HEADS)[:, 0:TT * D].rearrange("p (t n) -> p t n", t=TT)
        out_tok = x_tok
        qi, ki = v_tok[:, 0, :].rearrange("p (a n) -> p a n", a=2), v_tok[:, 1, 0:T]
        f_cum, rows, f_raw, f_low = y_tok[:, 0, 0:T], y_tok[:, 0, T:2 * T], y_tok[:, 1, 0:T], y_tok[:, 1, T:2 * T]
        buckets, bias_row = probsT[:, 0, 0:384], probsT[:, 1, 0:384]
        toeplitz = big[:, 8:16, :]
        cosT, sinT, perm = big[:, 6, :], big[:, 7, :], big[:, 8, 0:P]
        lam_in = big[:, 9, :].rearrange("p (a d) -> p a d", a=4)
        diff_v = flat(big, 0, 6).rearrange("p (t n) -> p t n", t=TT)
        diff_q = big[:, 10:16, :]
        chunk_mask = head_bias[:, 4, :]
        rope_sin = flat(head_bias, 0, 2)[:, 0:2 * T]
        rope_cosines = flat(head_bias, 5, 8)[:, 0:4 * T].rearrange("p (a n) -> p a n", a=2)
        head_ones = heads2.rearrange("p (h d) -> p h d", d=HD)[:, :, 0]
        S_MEM, S_WI, S_MAX, S_NMAX, S_SUM, S_INV, S_DOT, S_LAM, S_NLAM = 0, 8, 16, 20, 24, 32, 36, 38, 40
        S_DMAX, S_DNMAX, S_DSUM, S_DINV, S_OSS, S_ORSTD = 44, 52, 60, 68, 76, 80

        bank = [ctx.enter_context(nc.psum_tensor(f"bank{i}", [P, 512], F32)) for i in range(8)]
        lin, acc, ps_ada, ps_misc = bank[0:2], bank[2:6], bank[6], bank[7]
        SKEW = 384 + 1
        bias_dram = nc.dram_tensor("bias_rows", (HEADS, P * SKEW), F32, kind="Internal").ap()

        raw_full = [sem(f"raw_full{s}") for s in range(RING)]
        consts_in, rows_in, mem_in, x_in, small_in = (sem(s) for s in (
            "consts_in", "rows_in", "mem_in", "x_in", "small_in"))
        bias_out, bias_in, late_in, y_out = (sem(s) for s in ("bias_out", "bias_in", "late_in", "y_out"))
        hi_w, lo_w, unit_done, evac_a, evac_v = (sem(s) for s in ("hi_w", "lo_w", "unit_done", "evac_a", "evac_v"))
        fresh_ready, fresh_hi, fresh_lo = sem("fresh_ready"), sem("fresh_hi"), sem("fresh_lo")
        chain_v, chain_a, chain_g = sem("chain_v"), sem("chain_a"), sem("chain_g")
        misc_full, misc_read = sem("misc_full"), sem("misc_read")
        filled, vec_ready = sem("filled"), sem("vec_ready")
        mem_sq, mem_var, mem_rstd, mem_scaled, mem_turned = (sem(s) for s in (
            "mem_sq", "mem_var", "mem_rstd", "mem_scaled", "mem_turned"))
        ada_used, ada_copied, ada_scaled, ada_part_sum = (sem(s) for s in (
            "ada_used", "ada_copied", "ada_scaled", "ada_part_sum"))
        ada_done, ada_ready, x_turned = sem("ada_done"), sem("ada_ready"), sem("x_turned")
        xt_ready, sq_ready, sq_used, root_ready, spread_full, spread_read = (sem(s) for s in (
            "xt_ready", "sq_ready", "sq_used", "root_ready", "spread_full", "spread_read"))
        qk_normed, rope_cos, rope_done = (sem(s) for s in ("qk_normed", "rope_cos", "rope_done"))
        f_in, f_exp, f_ln, f_ready, sel_ready, f_bc, f_copied, fox_bias = (sem(s) for s in (
            "f_in", "f_exp", "f_ln", "f_ready", "sel_ready", "f_bc", "f_copied", "fox_bias"))
        idx_mm, idx_relu, idx_added, picked, dsa_bias = (sem(s) for s in (
            "idx_mm", "idx_relu", "idx_added", "picked", "dsa_bias"))
        score_mm, score_max, exp_done, turned, turned_copied, y_turned, y_copied = (sem(s) for s in (
            "score_mm", "score_max", "exp_done", "turned", "turned_copied", "y_turned", "y_copied"))
        branch_done, half_done = sem("branch_done"), sem("half_done")
        lam_dots, lam_exp = sem("lam_dots"), sem("lam_exp")
        d_score, d_max, d_exp, mixed, d_turned, d_copied, o_copied, o_sq, o_var, o_rstd, o_scaled = (sem(s) for s in (
            "d_score", "d_max", "d_exp", "mixed", "d_turned", "d_copied", "o_copied", "o_sq", "o_var", "o_rstd", "o_scaled"))
        out_turned, out_copied = sem("out_turned"), sem("out_copied")

        CAUSAL_BLOCKS, CAUSAL_SPAN = [(0, 0, 0), (1, 0, 128), (1, 1, 256)], [(0, 128), (128, 384)]
        FULL_BLOCKS, FULL_SPAN = [(0, 0, 0), (0, 1, 128), (1, 0, 256), (1, 1, 384)], [(0, 256), (256, 512)]

        ada_after = {loads[i - 1][1]: a for i, (kind, a) in enumerate(loads) if kind == "a" and a >= ADA_FIRST}

        block = ctx.enter_context(nc.Block())

        @block.sync
        def _(sp):
            def slot_view(n, at, width):
                slot = w_raw[:, slot_of["w", n], :]
                if units[n][0] == "N":
                    return slot.rearrange("p (k n) -> p k n", k=KT)[:, :, at:at + width]
                return slot.rearrange("p (k n) -> p k n", k=4)

            position = {what: i for i, what in enumerate(loads)}

            def slot_free(kind, n):
                i = position[kind, n] - RING
                if i < 0:
                    return
                kind, m = loads[i]
                if kind == "w":
                    sp.wait_ge(lo_w, m + 1)
                elif m < ADA_FIRST:
                    sp.wait_ge(ada_used, m + 1)
                else:
                    sp.wait_ge(ada_part_sum, m - ADA_FIRST + 1)

            def load_unit(n):
                slot_free("w", n)
                for at, src in units[n][2]:
                    sp.dma_start(slot_view(n, at, src.shape[-1]), src).then_inc(raw_full[slot_of["w", n]], 16)

            def load_ada(a):
                slot_free("a", a)
                s = slot_of["a", a]
                cols = w["w_ada"].rearrange("(k p) n -> p k n", p=P)[:, :, 256 * a:256 * a + 256]
                sp.dma_start(w_raw[:, s, :].rearrange("p (k n) -> p k n", k=KT), cols).then_inc(raw_full[s], 16)

            def load(first, last):
                for kind, n in loads[position[first]:position[last] + 1]:
                    (load_unit if kind == "w" else load_ada)(n)

            def load_mlp(n0, up, down):
                up_cols = up.rearrange("(k p) n -> p k n", p=P)
                down_rows = down.rearrange("(j k p) n -> p j k n", j=FF_STEPS, p=P)
                for n in range(n0, n0 + 6):
                    load_unit(n)
                with sp.Fori(0, MLP_LOOPS) as turn:
                    for k in range(BODY):
                        n = n0 + 6 + k
                        is_up = k % 4 < 2
                        step = 2 + k // 4 if is_up else 1 + k // 4
                        at = sp.snap(turn * 1024 + (512 * step + 256 * (k % 2))) if is_up else sp.snap(turn * 2 + step)
                        free = sp.snap(turn * BODY + (n - RING + 1))
                        sp.wait_ge(lo_w, free)
                        if is_up:
                            sp.dma_start(slot_view(n, 0, 256), up_cols[:, :, bass.ds(at, 256)])\
                                .then_inc(raw_full[n % RING], 16)
                        else:
                            c0 = 512 * (k % 2)
                            sp.dma_start(w_raw[:, n % RING, :].rearrange("p (j k n) -> p j k n", j=1, k=4),
                                         down_rows[:, bass.ds(at, 1), :, c0:c0 + 512]).then_inc(raw_full[n % RING], 16)
                for n in range(n0 + 30, n0 + 32):
                    load_unit(n)

            sp.dma_start(consts[:, :], tables["consts"]).then_inc(consts_in, 16)
            sp.dma_start(mem_tok, vectors["mem"].rearrange("(t p) d -> p t d", p=P)).then_inc(mem_in, 16)
            load(("w", 0), ("a", 0))
            sp.dma_start(x_tok, x.rearrange("(t p) d -> p t d", p=P)).then_inc(x_in, 16)
            load(("w", 1), ("w", 2))
            sp.dma_start(rel[0:32, :], vectors["rel_bias"].rearrange("(b h) -> b h", h=HEADS)).then_inc(small_in, 16)
            sp.dma_start(rel[64:64 + HEADS, 0:1], vectors["b_forget"].rearrange("(h o) -> h o", o=1)).then_inc(small_in, 16)
            sp.dma_start(buckets[0:33, :], tables["buckets"]).then_inc(small_in, 16)
            load(("a", 3), ("w", 15))
            sp.wait_ge(misc_read, misc_no["row"] + 1)
            sp.dma_start(bass.AP(bias_dram.tensor, bias_dram.offset, [[P * SKEW, HEADS], [SKEW, P], [1, 384]]),
                         bias_row[0:HEADS, :].unsqueeze(1).to_broadcast([HEADS, P, 384])).then_inc(bias_out, 16)
            sp.wait_ge(bias_out, 16)
            sp.wait_ge(ada_ready, 1)
            sp.dma_start(toeplitz, bass.AP(bias_dram.tensor, bias_dram.offset + P - 1, [[SKEW - 1, P], [P * SKEW, HEADS], [1, T]]))\
                .then_inc(bias_in, 16)
            load(loads[position["w", 15] + 1], ("w", N_MLP0 - 1))
            load_mlp(N_MLP0, w["w_mlp1"], w["w_mlp2"])
            for n in range(N_QM0, N_MLP1):
                load_unit(n)
            load_mlp(N_MLP1, w["w_up"][0], w["w_down"][0])
            sp.dma_start(flat(big, 6, 9)[:, 0:2 * T + P], tables["rope"]).then_inc(late_in, 16)
            sp.dma_start(big[:, 9, :], vectors["b_lam"].partition_broadcast(P)).then_inc(late_in, 16)
            sp.dma_start(chunk_mask, tables["chunks"]).then_inc(late_in, 16)
            for n in range(N_K, N_MLP2):
                load_unit(n)
            load_mlp(N_MLP2, w["w_up"][1], w["w_down"][1])
            for tt in range(TT):
                sp.wait_ge(out_copied, 2 * tt + 2)
                sp.dma_start(out.rearrange("(t p) d -> p t d", p=P)[:, tt, :], out_tok[:, tt, :]).then_inc(y_out, 16)
            sp.wait_ge(y_out, 32)

        @block.tensor
        def _(pe):
            pairs = Count()

            def mm(dst, lhsT, rhs, start, stop):
                return pe.matmul(dst, lhsT, rhs, start=start, stop=stop, skip_group_check=True)

            def into_misc(name):
                if misc_no[name]:
                    pe.wait_ge(misc_read, misc_no[name])

            def start_unit(n, turn):
                pe.wait_ge(lo_w, n + 1 if turn is None else turn * BODY + (n + 1))
                if before[n]:
                    user, value = before[n]
                    pe.wait_ge(evac_a if user == "a" else evac_v, value if turn is None else turn * 4 + value)

            def product(n, hi, lo, first_tile=0, banks=None, start=True, turn=None, bank_order=False, job=None,
                        tiles_first=0):
                start_unit(n, turn)
                banks = banks or [lin[lin_bank[n]]]
                kts, nts = (KT, 2) if units[n][0] == "N" else (4, 4)
                wh = w_hi[:, n % RING, :].rearrange("p (k n) -> p k n", k=kts)
                wl = w_lo[:, n % RING, :].rearrange("p (k n) -> p k n", k=kts)
                order = [(kt, nt) for kt in range(kts) for nt in range(nts)]
                if bank_order:
                    order = [(kt, 2 * b + i) for b in range(nts // 2) for kt in range(kts) for i in range(2)]
                steps = [(kt, nt, i) for kt, nt in order for i in range(3)]
                if job is not None:
                    order = [((kt + tiles_first) % kts, nt) for kt in range(kts) for nt in range(nts)]
                    steps = [(kt, nt, i) for kt, nt in order for i in (0, 2)] + [(kt, nt, 1) for kt, nt in order]
                parts, started = ((wh, hi), (wh, lo), (wl, hi)), set()
                for at, (kt, nt, i) in enumerate(steps):
                    if job is not None and kt % 2 == 0 and nt == 0 and i != 2:
                        pair = (kt - tiles_first) % kts // 2
                        pe.wait_ge(fresh_lo if i == 1 else fresh_hi, job + pair + 1)
                    a, b = parts[i]
                    bank_no = nt // 2
                    last = mm(banks[bank_no][:, (nt % 2) * T:(nt % 2) * T + T], a[:, kt, nt * P:nt * P + P],
                              b[:, first_tile + kt, :], start and bank_no not in started,
                              all(n != nt for _, n, _ in steps[at + 1:]))
                    started.add(bank_no)
                    if bank_order and kt == kts - 1 and nt == 1 and i == 2:
                        last.then_inc(half_done, 1)
                last.then_inc(unit_done, 1)

            def product_tok(n, hi, lo):
                start_unit(n, None)
                wh = w_hi[:, n % RING, :].rearrange("p (k n) -> p k n", k=KT)
                wl = w_lo[:, n % RING, :].rearrange("p (k n) -> p k n", k=KT)
                for kt in range(KT):
                    for tt in range(TT):
                        for i, (a, b) in enumerate(((hi, wh), (lo, wh), (hi, wl))):
                            last = mm(lin[lin_bank[n]][:, tt * T:tt * T + T], a[:, kt, tt * P:tt * P + P], b[:, kt, :],
                                      kt == 0 and tt == 0 and i == 0, kt == KT - 1 and i == 2)
                last.then_inc(unit_done, 1)

            def ada_row_unit(a):
                slot = slot_of["a", a]
                tiles = w_raw[:, slot, :].rearrange("p (k n) -> p k n", k=KT)
                pe.wait_ge(raw_full[slot], value_of["a", a])
                if a % 2 == 0 and a:
                    pe.wait_ge(ada_copied, a // 2)
                for kt in range(KT):
                    last = mm(ps_ada[0:1, (a % 2) * T:(a % 2) * T + T], vec[:, V_C + kt:V_C + kt + 1], tiles[:, kt, :],
                              kt == 0 and a % 2 == 0, kt == KT - 1)
                last.then_inc(ada_used, 1)

            def ada_columns(a):
                for nt in range(2):
                    last = mm(ps_ada[:, 2 * a + nt:2 * a + nt + 1], ada_row[:, 256 * a + nt * P:256 * a + nt * P + P],
                              ones[0:1, 0:1], True, True)
                last.then_inc(ada_done, 1)

            def ada_unit(a):
                pe.wait_ge(ada_part_sum, a - ADA_FIRST + 1)
                if a == ADA_FIRST:
                    pe.wait_ge(ada_ready, 1)
                for nt in range(2):
                    last = mm(ps_ada[:, 2 * a + nt:2 * a + nt + 1], ada_late[:, a % 2, nt * P:nt * P + P], ones[:, 0:1],
                              True, True)
                last.then_inc(ada_done, 1)

            def add_squares(s, q):
                if q == 0:
                    into_misc(f"sum{s}")
                pe.wait_ge(sq_ready, 4 * (s - 1) + q + 1)
                for i in range(2):
                    for tt in range(TT):
                        last = mm(ps_misc[:, tt:tt + 1], probs[:, q % 2, i * T + tt * P:i * T + tt * P + P], ones[:, 0:1],
                                  q == 0 and i == 0 and tt == 0, q == 3 and i == 1)
                last.then_inc(misc_full if q == 3 else sq_used, 1)

            def spread_sum(s, bank):
                name = f"sum{s}"
                pe.wait_ge(root_ready, power_no[name] + 1)
                if bank is ps_ada:
                    pe.wait_ge(spread_read, spread_no[name])
                for tt in range(TT):
                    at = root_at[name] + tt
                    last = mm(bank[:, tt * P:tt * P + P], root[:, at:at + 1].to_broadcast([P, P]), ident, True, True)
                last.then_inc(spread_full, 1)

            def qk_squares(name, n):
                into_misc("qk." + name)
                pe.wait_ge(evac_a, evac_value[n])
                for tt in range(TT):
                    for a in range(2):
                        c0, at = a * T + tt * P, 4 * tt + 2 * a
                        last = mm(ps_misc[:, at:at + 2], probs[:, qk_no["qk." + name] % 2, c0:c0 + P], head_ones, True, True)
                last.then_inc(misc_full, 1)

            def spread_qk(name, bank):
                name = "qk." + name
                pe.wait_ge(root_ready, power_no[name] + 1)
                if bank is ps_ada:
                    pe.wait_ge(spread_read, spread_no[name])
                for a in range(2):
                    for tt in range(TT):
                        for h in range(2):
                            at = root_at[name] + 4 * tt + 2 * a + h
                            last = mm(bank[HD * h:HD * h + HD, a * T + tt * P:a * T + tt * P + P],
                                      root[:, at:at + 1].to_broadcast([P, HD]), ident, True, True)
                last.then_inc(spread_full, 1)

            def rotate(name, src):
                into_misc("rope." + name)
                pe.wait_ge(qk_normed, qk_no["qk." + name] + 1)
                mm(ps_misc[:, :], perm, src, True, True).then_inc(misc_full, 1)

            def to_T(dst_banks, src, sem_done, wait_q=None):
                for q, dst in enumerate(dst_banks):
                    if wait_q:
                        wait_q(q)
                    for i in range(2):
                        for tt in range(TT):
                            c0 = (2 * q + i) * P
                            last = pe.transpose(dst[:, i * T + tt * P:i * T + tt * P + P], src[:, tt, c0:c0 + P], ident)
                    last.then_inc(sem_done, 1)

            def scores(q_tile, k_tile, span):
                for odd in range(2):
                    base = HD * odd
                    for tt, (c0, c1) in enumerate(span):
                        last = mm(acc[odd][:, c0:c1], q_tile[base:base + HD, tt * P:tt * P + P],
                                  k_tile[base:base + HD, 0:c1 - c0], True, True)
                    last.then_inc(score_mm, 1)

            def attention(name, n_pairs, q_tile, k_tile, values, blocks, span, filler):
                scores(q_tile(0), k_tile(0), span)
                for g in range(n_pairs):
                    filler(g)
                    G = pairs.up() - 1
                    for odd in range(2):
                        h = 2 * G + odd
                        pe.wait_ge(exp_done, h + 1)
                        if h >= 2:
                            pe.wait_ge(turned_copied, h - 1)
                        for _, _, c0 in blocks:
                            last = pe.transpose(acc[2 + odd][:, c0:c0 + P], probs[:, odd, c0:c0 + P], ident)
                        last.then_inc(turned, 1)
                    if g + 1 < n_pairs:
                        scores(q_tile(g + 1), k_tile(g + 1), span)
                    into_misc(f"{name}{g}")
                    for odd in range(2):
                        pe.wait_ge(turned_copied, 2 * G + odd + 1)
                        for tt in range(TT):
                            mine = [(s, c0) for t, s, c0 in blocks if t == tt]
                            for i, (s, c0) in enumerate(mine):
                                at = (2 * odd + tt) * HD
                                last = mm(ps_misc[:, at:at + HD], probsT[:, odd, c0:c0 + P], values(2 * g + odd, s),
                                          i == 0, i == len(mine) - 1)
                    last.then_inc(misc_full, 1)

            pe.wait_ge(consts_in, 16)
            pe.wait_ge(rows_in, 16 * 19)
            pe.transpose(ps_misc[:, 0:P], rows[:, 0:P], ident)
            pe.transpose(ps_misc[:, P:2 * P], rows[:, P:2 * P], ident).then_inc(misc_full, 1)
            pe.wait_ge(mem_scaled, 2)
            to_T(acc, mem_tok, mem_turned)
            pe.wait_ge(vec_ready, 1)
            product(0, u_hi, u_lo, job=J_MEM)
            ada_row_unit(0)
            product_tok(1, u_hi, u_lo)
            qk_squares("mem0", 0)
            ada_row_unit(1)
            pe.wait_ge(x_in, 16)
            to_T(acc, x_tok, x_turned, lambda q: pe.wait_ge(fresh_ready, q + 1))
            ada_row_unit(2)
            add_squares(1, 0)
            add_squares(1, 1)
            product(2, u_hi, u_lo)
            add_squares(1, 2)
            add_squares(1, 3)
            for a in range(3, 6):
                ada_row_unit(a)
            spread_sum(1, acc[0])
            for a in range(6, ADA_FIRST):
                ada_row_unit(a)
            pe.wait_ge(ada_copied, 4)
            for a in range(ADA_FIRST):
                ada_columns(a)
            product_tok(3, u_hi, u_lo)
            qk_squares("mem1", 2)
            for n in range(N_IDX, N_GF):
                if n < 10:
                    product(n, h_hi, h_lo, job=J_H1 if n == N_IDX else None)
                else:
                    product_tok(n, h_hi, h_lo)
                if n in ada_after:
                    ada_unit(ada_after[n])
                if n == 4:
                    spread_qk("mem0", acc[1])
                    spread_qk("mem1", acc[2])
                if n == 5:
                    into_misc("wi")
                    pe.wait_ge(evac_a, evac_value[4])
                    for tt in range(TT):
                        last = pe.transpose(ps_misc[:, tt * P:tt * P + P], f_raw[:, tt * P:tt * P + P], ident)
                    last.then_inc(misc_full, 1)
                if n == 6:
                    pe.wait_ge(evac_a, evac_value[5])
                    pe.wait_ge(spread_read, 3)
                    for h in range(IDX_HEADS):
                        base = HD * (h % 2)
                        for tt, (c0, c1) in enumerate(CAUSAL_SPAN):
                            last = mm(acc[h][:, c0:c1], qi[base:base + HD, h // 2, tt * P:tt * P + P],
                                      ki[base:base + HD, 0:c1 - c0], True, True)
                        last.then_inc(idx_mm, 1)
                if n == 8:
                    pe.wait_ge(f_ready, 1)
                    pe.wait_ge(sel_ready, 1)
                    pe.wait_ge(idx_relu, IDX_HEADS)
                    for h in range(HEADS):
                        last = mm(acc[h // 2][:, (h % 2) * T:(h % 2) * T + T], head_bias[:, h, 0:P], f_cum, True, True)
                        if h % 2:
                            last.then_inc(f_bc, 1)
                if n == 9:
                    into_misc("row")
                    pe.wait_ge(small_in, 48)
                    mm(ps_misc[0:HEADS, 0:384], rel[0:33, :], buckets[0:33, :], True, True).then_inc(misc_full, 1)

            def with_ada(n, multiply):
                multiply(n, h_hi, h_lo)
                if n in ada_after:
                    ada_unit(ada_after[n])

            pe.wait_ge(f_copied, 4)
            pe.wait_ge(evac_a, evac_value[11])
            attention("fox", 4, lambda g: qk[:, g, :], lambda g: qk[:, 4 + g, :],
                      lambda h, s: v_tok[:, s, h * HD:h * HD + HD], CAUSAL_BLOCKS, CAUSAL_SPAN,
                      lambda g: with_ada(N_GF + g, product))
            with_ada(N_DSA, product)
            pe.wait_ge(misc_read, misc_no["fox3"] + 1)
            to_T(acc[0:2], y_tok, y_turned)
            for n in range(N_DSA + 1, N_GD):
                with_ada(n, product if n < N_DSA + 4 else product_tok)
            pe.wait_ge(fresh_ready, J_DSA)
            pe.wait_ge(evac_a, evac_value[N_GD - 1])
            attention("dsa", 4, lambda g: qk[:, g, :], lambda g: qk[:, 4 + g, :],
                      lambda h, s: v_tok[:, s, h * HD:h * HD + HD], CAUSAL_BLOCKS, CAUSAL_SPAN,
                      lambda g: with_ada(N_GD + g, product))
            product(N_BR, u_hi, u_lo, 0, acc[0:2], job=J_FOX)
            product(N_BR + 1, u_hi, u_lo, 0, acc[2:4])
            pe.wait_ge(misc_read, misc_no["dsa3"] + 1)
            to_T(acc[0:2], y_tok, y_turned, lambda q: pe.wait_ge(branch_done, q + 1))
            pe.wait_ge(fresh_ready, J_MERGED)
            product(N_BR + 2, u_hi, u_lo, 4, acc[0:2], job=J_DSA)
            pe.wait_ge(branch_done, 4)
            product(N_BR + 3, u_hi, u_lo, 4, acc[2:4])
            for i in range(4):
                product(N_OUT + i, h_hi, h_lo, job=J_MERGED if i == 0 else None)
                if i >= 1:
                    add_squares(2, i - 1)
            add_squares(2, 3)

            def mlp(n0, s, job_h, job_u):
                def up(n, turn=None, job=None):
                    product(n, h_hi, h_lo, turn=turn, job=job)
                    product(n + 1, h_hi, h_lo, turn=turn)

                def down(n, step, turn=None, last=False):
                    ready = job_u + 2 * step + 2
                    pe.wait_ge(fresh_lo, ready if turn is None else turn * 4 + ready)
                    for half in range(2):
                        product(n + half, u_hi, u_lo, 4 * (step % 2), acc[2 * half:2 * half + 2], start=step == 0,
                                turn=turn, bank_order=last)

                spread_sum(s, ps_ada)
                up(n0, job=job_h)
                up(n0 + 2)
                down(n0 + 4, 0)
                with pe.Fori(0, MLP_LOOPS) as turn:
                    for k in range(2):
                        up(n0 + 6 + 4 * k, turn)
                        down(n0 + 8 + 4 * k, 1 + k, turn)
                down(n0 + 30, FF_STEPS - 1, last=True)

            pe.wait_ge(fresh_ready, J_H2)
            mlp(N_MLP0, 2, J_H2, J_MLP0)
            for s in (3, 4):
                for q in range(4):
                    add_squares(s, q)
                spread_sum(s, ps_ada)
            product(N_QM0, h_hi, h_lo, job=J_H4)
            product(N_CONV, h_hi, h_lo)
            qk_squares("qm0", N_QM0)
            product(N_CONV + 1, h_hi, h_lo)
            spread_qk("qm0", ps_ada)
            product(N_CONV + 2, h_hi, h_lo)
            pe.wait_ge(qk_normed, qk_no["qk.qm0"] + 1)
            attention("mem0.", 2, lambda g: qi[:, g, :], lambda g: mem_k[:, 0, g, :],
                      lambda h, s: mem_v[:, 0, s, h * HD:h * HD + HD], FULL_BLOCKS, FULL_SPAN,
                      lambda g: product(N_CONV + 3 + g, h_hi, h_lo))
            product(N_CONV + 5, h_hi, h_lo)
            pe.wait_ge(misc_read, misc_no["mem0.1"] + 1)
            to_T(acc[0:1], y_tok, y_turned)
            for n in range(N_CONV + 6, N_O0):
                product(n, h_hi, h_lo)
            for i in range(4):
                product(N_O0 + i, u_hi, u_lo, job=J_YM0 if i == 0 else None, tiles_first=6)
                if i >= 1:
                    add_squares(5, i - 1)
            add_squares(5, 3)
            mlp(N_MLP1, 5, J_H5, J_MLP1)
            for q in range(4):
                add_squares(6, q)
            spread_sum(6, ps_ada)
            product(N_K, h_hi, h_lo, job=J_KV)
            product(N_K + 1, h_hi, h_lo)
            qk_squares("k0", N_K)
            product(N_K + 2, h_hi, h_lo)
            qk_squares("k1", N_K + 1)
            spread_qk("k0", ps_ada)
            pe.wait_ge(late_in, 48)
            product(N_Q, u_hi, u_lo, job=J_MIX1)
            qk_squares("k2", N_K + 2)
            spread_qk("k1", ps_ada)
            rotate("k0", flat(qk, 0, 2))
            product(N_Q + 1, u_hi, u_lo)
            qk_squares("qm1", N_Q)
            spread_qk("k2", ps_ada)
            rotate("k1", flat(qk, 2, 4))
            product(N_Q + 2, u_hi, u_lo)
            qk_squares("q0", N_Q + 1)
            spread_qk("qm1", ps_ada)
            rotate("k2", flat(qk, 4, 6))
            product(N_Q + 3, u_hi, u_lo)
            qk_squares("q1", N_Q + 2)
            spread_qk("q0", ps_ada)
            product_tok(N_V, h_hi, h_lo)
            qk_squares("q2", N_Q + 3)
            spread_qk("q1", ps_ada)
            rotate("q0", flat(big, 10, 12))

            def values_unit(g):
                product_tok(N_V + 1 + g, h_hi, h_lo)
                if g == 0:
                    spread_qk("q2", ps_ada)
                    rotate("q1", flat(big, 12, 14))
                else:
                    rotate("q2", flat(big, 14, 16))

            attention("mem1.", 2, lambda g: qi[:, g, :], lambda g: mem_k[:, 1, g, :],
                      lambda h, s: mem_v[:, 1, s, h * HD:h * HD + HD], FULL_BLOCKS, FULL_SPAN, values_unit)
            pe.wait_ge(misc_read, misc_no["mem1.1"] + 1)
            to_T(acc[0:1], y_tok, y_turned)

            def d_scores(h):
                base, odd = HD * (h % 2), h % 2
                for m in range(2):
                    for tt, (c0, c1) in enumerate(CAUSAL_SPAN):
                        last = mm(acc[2 * odd + m][:, c0:c1], diff_q[base:base + HD, 3 * m + h // 2, tt * P:tt * P + P],
                                  qk[base:base + HD, 3 * m + h // 2, 0:c1 - c0], True, True)
                last.then_inc(d_score, 1)

            def turn_o(h):
                into_misc(f"oT{h}")
                pe.wait_ge(o_scaled, h + 1)
                for tt in range(TT):
                    last = pe.transpose(ps_misc[:, tt * P:tt * P + P], y_tok[:, tt, (h % 2) * P:(h % 2) * P + P], ident)
                last.then_inc(misc_full, 1)

            pe.wait_ge(rope_done, len(ROPES))
            pe.wait_ge(spread_read, spread_no["qk.q2"] + 1)
            pe.wait_ge(fresh_ready, J_YM1 + 1)
            pe.wait_ge(evac_a, evac_value[N_V + 2])
            d_scores(0)
            for h in range(DIFF_HEADS):
                if h + 1 < DIFF_HEADS:
                    if h >= 1:
                        pe.wait_ge(d_max, h)
                    d_scores(h + 1)
                pe.wait_ge(mixed, h + 1)
                if h >= 1:
                    pe.wait_ge(d_copied, h)
                for _, _, c0 in CAUSAL_BLOCKS:
                    last = pe.transpose(ps_ada[:, c0:c0 + P], head_bias[:, 2 * (h % 2), c0:c0 + P], ident)
                last.then_inc(d_turned, 1)
                into_misc(f"pv{h}")
                pe.wait_ge(d_copied, h + 1)
                for tt in range(TT):
                    mine = [(s, c0) for t, s, c0 in CAUSAL_BLOCKS if t == tt]
                    for i, (s, c0) in enumerate(mine):
                        last = mm(ps_misc[:, tt * P:tt * P + P], probsT[:, h % 2, c0:c0 + P], diff_v[:, s, h * P:h * P + P],
                                  i == 0, i == len(mine) - 1)
                last.then_inc(misc_full, 1)
                if h >= 1:
                    turn_o(h - 1)
            turn_o(DIFF_HEADS - 1)
            for i in range(4):
                product(N_O1 + i, u_hi, u_lo, job=J_YM1 if i == 0 else None, tiles_first=6)
                if i >= 1:
                    add_squares(7, i - 1)
            add_squares(7, 3)
            mlp(N_MLP2, 7, J_H7, J_MLP2)
            for tt in range(TT):
                for q in range(2):
                    pe.wait_ge(xt_ready, 24 + 2 * q + 2)
                    if tt == 1 and q == 0:
                        pe.wait_ge(spread_read, len(SPREAD))
                    if tt == 0 and q == 0:
                        pe.wait_ge(evac_a, emptied["a"])
                    dst = (lin[0], lin[1], ps_ada, ps_misc)[2 * tt + q]
                    for i in range(4):
                        last = pe.transpose(dst[:, i * P:i * P + P], xT[:, 4 * q + i, tt * P:tt * P + P], ident)
                    last.then_inc(out_turned, 1)

        @block.scalar
        def _(act):
            def link(ins):
                ins.then_inc(chain_a, 1)
                act.wait_ge(chain_a, 1)

            def scale_ada(a):
                slot = slot_of["a", a]
                tiles = w_raw[:, slot, :].rearrange("p (k n) -> p k n", k=KT)
                act.wait_ge(raw_full[slot], value_of["a", a])
                for k in range(KT):
                    last = act.activation(tiles[:, k, :], tiles[:, k, :], ACT.Copy, scale=vec[:, V_C + k:V_C + k + 1])
                last.then_inc(ada_scaled, 1)

            def split_w(n, turn=None):
                if n >= N_UNITS:
                    return
                at = lambda value, per: value if turn is None else turn * per + value
                slot = slot_of["w", n]
                act.wait_ge(raw_full[slot], at(value_of["w", n], 32))
                if n >= RING:
                    act.wait_ge(unit_done, at(n - RING + 1, BODY))
                act.activation(w_hi[:, n % RING, :], w_raw[:, slot, :], ACT.Copy).then_inc(hi_w, 1)
                if n in ada_after:
                    scale_ada(ada_after[n])

            def split_h(job, hi, tile, turn=None, free=None):
                at = lambda value, per: value if turn is None else turn * per + value
                act.wait_ge(fresh_ready, at(job + 1, 4))
                if free:
                    act.wait_ge(unit_done, at(free, BODY))
                act.activation(flat(hi, tile, tile + 2), fresh[:, job % 2, :], ACT.Copy).then_inc(fresh_hi, 1)

            def evac(n, dst, func=ACT.Copy, scale=1.0):
                act.wait_ge(unit_done, n + 1)
                act.activation(dst, lin[lin_bank[n]][:, :], func, scale=scale).then_inc(evac_a, 1)

            def evac_qk(name, n, dst):
                act.wait_ge(unit_done, n + 1)
                act.activation(dst, lin[lin_bank[n]][:, :], ACT.Copy)
                i = qk_no["qk." + name]
                if i >= 2:
                    act.wait_ge(misc_full, misc_no[QK_NORMS[i - 2]] + 1)
                act.activation(probs[:, i % 2, :], lin[lin_bank[n]][:, :], ACT.Square).then_inc(evac_a, 1)

            def square_pair(s, q, src):
                if q >= 2:
                    act.wait_ge(sq_used, 3 * (s - 1) + q - 1)
                elif s > 1:
                    act.wait_ge(misc_full, misc_no[f"sum{s - 1}"] + 1)
                act.activation(probs[:, q % 2, :], src, ACT.Square).then_inc(sq_ready, 1)

            def square_x(s):
                for q in range(4):
                    act.wait_ge(xt_ready, 4 * (s - 2) + q + 1)
                    square_pair(s, q, flat(xT, 2 * q, 2 * q + 2))

            def exps(G, span, from_bank=False):
                for odd in range(2):
                    h = 2 * G + odd
                    act.wait_ge(score_max, h + 1)
                    if from_bank and h >= 2:
                        act.wait_ge(turned, h - 1)
                    for tt, (c0, c1) in enumerate(span):
                        at = 2 * odd + tt
                        last = act.activation(probs[:, odd, c0:c1], (acc[odd] if from_bank else probs[:, odd, :])[:, c0:c1],
                                              ACT.Exp, bias=stat[:, S_NMAX + at:S_NMAX + at + 1],
                                              accum_out=stat[:, S_SUM + 4 * (G % 2) + at:S_SUM + 4 * (G % 2) + at + 1])
                    last.then_inc(exp_done, 1)

            def copy_turned(name, g, G, width):
                before_me = misc_no[f"{name}{g}"]
                for odd in range(2):
                    h = 2 * G + odd
                    act.wait_ge(turned, h + 1)
                    if g >= 1:
                        act.wait_ge(misc_full, before_me)
                    act.activation(probsT[:, odd, 0:width], acc[2 + odd][:, 0:width], ACT.Copy).then_inc(turned_copied, 1)

            def sigmoid_unit(n, tile):
                evac(n, flat(big, tile, tile + 2), ACT.Tanh, 0.5)

            act.wait_ge(filled, 1)
            at = 0
            for name, count in (("c", 8), ("b_ada", 48), ("g_norm1", 8), ("g_norm2", 8), ("g_final", 8),
                                ("norm_mix", 16), ("norm_mlp", 16), ("kv_norm", 8), ("mem_norm", 8)):
                act.dma_start(rows[at:at + count, 0:P], vectors[name].rearrange("(r p) -> r p", p=P)).then_inc(rows_in, 16)
                at += count
            act.dma_start(rows[0:18, P:2 * P], vectors["a_conv"].rearrange("(r p) -> r p", p=P)).then_inc(rows_in, 16)
            act.dma_start(rows[18:19, P:2 * P], vectors["b_subln"].rearrange("(r p) -> r p", p=P)).then_inc(rows_in, 16)
            at = 19
            for name, count in (("b_q_norm", 1), ("k_norm", 1), ("mem_q_norm", 2), ("mem_k_norm", 2)):
                for side in range(2):
                    act.dma_start(rows[at:at + count, P + HD * side:P + HD * side + HD],
                                 vectors[name].rearrange("(r p) -> r p", p=HD)).then_inc(rows_in, 16)
                at += count
            act.wait_ge(mem_in, 16)
            for tt in range(TT):
                last = act.activation(flat(xT, 4 * tt, 4 * tt + 4), mem_tok[:, tt, :], ACT.Square,
                                      accum_out=stat[:, S_MEM + tt:S_MEM + tt + 1])
            last.then_inc(mem_sq, 1)

            def copy_ada(i):
                act.wait_ge(ada_used, 2 * i + 2)
                act.activation(ada_row[:, 512 * i:512 * i + 512], ps_ada[0:1, :], ACT.Copy).then_inc(ada_copied, 1)

            split_w(0)
            for q in range(4):
                split_h(J_MEM + q, u_hi, 2 * q)
            split_w(1)
            evac_qk("mem0", 0, flat(mem_k[:, 0], 0, 2))
            evac(1, flat(mem_v[:, 0], 0, 2))
            copy_ada(0)
            act.wait_ge(misc_full, misc_no["qk.mem0"] + 1)
            act.wait_ge(mem_turned, 4)
            for q in range(4):
                act.wait_ge(x_turned, q + 1)
                act.activation(flat(xT, 2 * q, 2 * q + 2), acc[q][:, :], ACT.Copy)
                square_pair(1, q, acc[q][:, :])
                if q == 1:
                    split_w(2)
            for i in range(1, 4):
                copy_ada(i)
            split_w(3)
            split_w(4)
            act.wait_ge(misc_full, misc_no["sum1"] + 1)
            evac_qk("mem1", 2, flat(mem_k[:, 1], 0, 2))
            for q in range(4):
                split_h(J_H1 + q, h_hi, 2 * q)
            split_w(5)
            evac(3, flat(mem_v[:, 1], 0, 2))
            split_w(6)
            split_w(7)
            act.wait_ge(unit_done, 5)
            act.wait_ge(misc_full, misc_no["vec"] + 1)
            act.activation(ki, lin[lin_bank[4]][:, 0:T], ACT.Copy)
            act.activation(f_raw, lin[lin_bank[4]][:, T:2 * T], ACT.Copy).then_inc(evac_a, 1)
            split_w(8)
            evac(5, v_tok[:, 0, :], scale=HD ** -0.5)
            act.wait_ge(f_in, 1)
            link(act.activation(f_low[64:64 + HEADS, :], f_low[64:64 + HEADS, :], ACT.Exp))
            act.activation(f_low[64:64 + HEADS, :], f_low[64:64 + HEADS, :], ACT.Ln, bias=1.0).then_inc(f_ln, 1)
            split_w(9)
            evac(6, flat(qk, 0, 2), scale=HD ** -0.5)
            act.wait_ge(misc_full, misc_no["qk.mem1"] + 1)
            for h in range(IDX_HEADS):
                act.wait_ge(idx_mm, h + 1)
                if h >= 2:
                    act.wait_ge(idx_added, h - 1)
                act.activation(probs[:, h % 2, 0:384], acc[h][:, 0:384], ACT.Relu).then_inc(idx_relu, 1)
            split_w(10)
            evac(7, flat(qk, 2, 4), scale=HD ** -0.5)
            split_w(11)
            evac(8, flat(qk, 4, 6))
            for q in range(4):
                act.wait_ge(f_bc, 4)
                act.activation(head_bias[:, 2 * q:2 * q + 2, 128:384], acc[q][:, :].rearrange("p (h s) -> p h s", h=2),
                               ACT.Copy, scale=-1.0).then_inc(f_copied, 1)
            split_w(12)
            evac(9, flat(qk, 6, 8))
            for n in (10, 11):
                split_w(n + AHEAD)
                act.wait_ge(unit_done, n + 1)
                c0 = 256 * (n - 10)
                act.activation(v_tok[:, :, c0:c0 + 256], lin[lin_bank[n]][:, :].rearrange("p (t c) -> p t c", t=TT),
                               ACT.Copy).then_inc(evac_a, 1)
            act.wait_ge(bias_out, 16)
            for g in range(4):
                exps(G_FOX + g, CAUSAL_SPAN)
                split_w(N_GF + g + AHEAD)
                sigmoid_unit(N_GF + g, 2 * g)
                copy_turned("fox", g, G_FOX + g, 384)
            split_w(N_DSA + AHEAD)
            act.wait_ge(misc_full, misc_no["fox3"] + 1)
            evac(N_DSA, flat(qk, 0, 2), scale=HD ** -0.5)
            for q in range(2):
                split_h(J_FOX + q, u_hi, 2 * q)
            for i in range(1, 4):
                split_w(N_DSA + i + AHEAD)
                evac(N_DSA + i, flat(qk, 2 * i, 2 * i + 2), scale=HD ** -0.5 if i < 2 else 1.0)
            for i in range(4, 6):
                n = N_DSA + i
                split_w(n + AHEAD)
                act.wait_ge(unit_done, n + 1)
                c0 = 256 * (i - 4)
                act.activation(v_tok[:, :, c0:c0 + 256], lin[lin_bank[n]][:, :].rearrange("p (t c) -> p t c", t=TT),
                               ACT.Copy).then_inc(evac_a, 1)
            for g in range(4):
                exps(G_DSA + g, CAUSAL_SPAN)
                split_w(N_GD + g + AHEAD)
                sigmoid_unit(N_GD + g, 8 + 2 * g)
                copy_turned("dsa", g, G_DSA + g, 384)
            split_w(N_BR + AHEAD)
            split_w(N_BR + 1 + AHEAD)
            for q in range(2):
                split_h(J_DSA + q, u_hi, 4 + 2 * q)
            split_w(N_BR + 2 + AHEAD)
            for q in range(4):
                if q == 2:
                    split_w(N_BR + 3 + AHEAD)
                split_h(J_MERGED + q, h_hi, 2 * q)
            for i in range(4):
                split_w(N_OUT + i + AHEAD)
                act.wait_ge(xt_ready, i + 1)
                square_pair(2, i, flat(xT, 2 * i, 2 * i + 2))
            for q in range(4):
                split_h(J_H2 + q, h_hi, 2 * q)

            def mlp(n0, job_u, ahead=AHEAD):
                def up_step(n, step, turn=None, first=0):
                    at = lambda value, per: value if turn is None else turn * per + value
                    job = job_u + 2 * step
                    free = n0 + 6 + 4 * (step - 2) if step >= 2 else None
                    for half in range(2):
                        split_w(n + half + ahead, turn)
                        if half:
                            split_h(job, u_hi, 4 * (step % 2), turn, free)
                        act.wait_ge(unit_done, at(n + half + 1, BODY))
                        act.wait_ge(fresh_lo, at(job + half - 1, 4))
                        act.activation(fresh[:, half, :], lin[half][:, :], ACT.Relu).then_inc(evac_a, 1)

                def down_step(n, step, turn=None, pending=None):
                    for half in range(2):
                        split_w(n + half + ahead, turn)
                        if half == 0 and pending is not None:
                            free = n0 + 6 + 4 * (pending - 2) if pending >= 2 else None
                            split_h(job_u + 2 * pending + 1, u_hi, 4 * (pending % 2) + 2, turn, free)

                up_step(n0, 0)
                split_h(job_u + 1, u_hi, 2)
                up_step(n0 + 2, 1)
                down_step(n0 + 4, 0, pending=1)
                with act.Fori(0, MLP_LOOPS) as turn:
                    for k in range(2):
                        up_step(n0 + 6 + 4 * k, 2 + k, turn)
                        down_step(n0 + 8 + 4 * k, 1 + k, turn, pending=2 + k)
                down_step(n0 + 30, FF_STEPS - 1)

            mlp(N_MLP0, J_MLP0)
            square_x(3)
            square_x(4)
            for q in range(4):
                split_h(J_H4 + q, h_hi, 2 * q)
            split_w(N_QM0 + AHEAD)
            act.wait_ge(misc_full, misc_no["sum4"] + 1)
            evac_qk("qm0", N_QM0, v_tok[:, 0, :])
            for i in range(3):
                split_w(N_CONV + i + AHEAD)
                evac(N_CONV + i, flat(big, 2 * i, 2 * i + 2))
            act.wait_ge(misc_full, misc_no["qk.qm0"] + 1)
            for g in range(2):
                exps(G_M0 + g, FULL_SPAN, from_bank=True)
                split_w(N_CONV + 3 + g + AHEAD)
                copy_turned("mem0.", g, G_M0 + g, 512)
            split_w(N_CONV + 5 + AHEAD)
            split_h(J_YM0, u_hi, 6)
            for i in range(3):
                split_w(N_CONV + 6 + i + AHEAD)
                split_h(J_CONV + i, u_hi, 2 * i)
            for i in range(4):
                split_w(N_O0 + i + AHEAD)
                act.wait_ge(xt_ready, 12 + i + 1)
                square_pair(5, i, flat(xT, 2 * i, 2 * i + 2))
            for q in range(4):
                split_h(J_H5 + q, h_hi, 2 * q)
            mlp(N_MLP1, J_MLP1)
            square_x(6)
            for q in range(4):
                split_h(J_KV + q, h_hi, 2 * q)
            for q in range(4):
                split_h(J_MIX1 + q, u_hi, 2 * q)
            act.wait_ge(misc_full, misc_no["sum6"] + 1)
            for i in range(3):
                split_w(N_K + i + AHEAD)
                evac_qk(f"k{i}", N_K + i, flat(qk, 2 * i, 2 * i + 2))
            split_w(N_Q + AHEAD)
            evac_qk("qm1", N_Q, v_tok[:, 0, :])
            for i in range(3):
                split_w(N_Q + 1 + i + AHEAD)
                evac_qk(f"q{i}", N_Q + 1 + i, flat(big, 10 + 2 * i, 12 + 2 * i))
            act.wait_ge(lam_dots, 1)
            act.activation(stat[:, S_LAM:S_LAM + 2], stat[:, S_DOT:S_DOT + 2], ACT.Exp).then_inc(lam_exp, 1)

            def evac_v_unit(i):
                act.wait_ge(unit_done, N_V + i + 1)
                act.activation(diff_v[:, :, 256 * i:256 * i + 256],
                               lin[lin_bank[N_V + i]][:, :].rearrange("p (t c) -> p t c", t=TT), ACT.Copy).then_inc(evac_a, 1)

            split_w(N_V + AHEAD)
            evac_v_unit(0)
            act.wait_ge(misc_full, misc_no["qk.q2"] + 1)
            for g in range(2):
                exps(G_M1 + g, FULL_SPAN, from_bank=True)
                split_w(N_V + 1 + g + AHEAD)
                evac_v_unit(1 + g)
                copy_turned("mem1.", g, G_M1 + g, 512)
            def d_exps(h):
                act.wait_ge(d_max, h + 1)
                for m in range(2):
                    p = head_bias[:, 2 * (h % 2) + m, :]
                    for tt, (c0, c1) in enumerate(CAUSAL_SPAN):
                        at = 4 * (h % 2) + 2 * m + tt
                        last = act.activation(p[:, c0:c1], p[:, c0:c1], ACT.Exp, bias=stat[:, S_DNMAX + at:S_DNMAX + at + 1],
                                              accum_out=stat[:, S_DSUM + at:S_DSUM + at + 1])
                last.then_inc(d_exp, 1)

            d_exps(0)
            split_h(J_YM1, u_hi, 6)
            for h in range(DIFF_HEADS):
                act.wait_ge(d_turned, h + 1)
                if h >= 2:
                    act.wait_ge(misc_full, misc_no[f"pv{h - 2}"] + 1)
                act.activation(probsT[:, h % 2, 0:384], ps_ada[:, 0:384], ACT.Copy).then_inc(d_copied, 1)
                if h + 1 < DIFF_HEADS:
                    d_exps(h + 1)
                act.wait_ge(o_copied, h + 1)
                for tt in range(TT):
                    at = S_OSS + 2 * (h % 2) + tt
                    last = act.activation(probs[:, h % 2, tt * P:tt * P + P], y_tok[:, tt, (h % 2) * P:(h % 2) * P + P],
                                          ACT.Square, accum_out=stat[:, at:at + 1])
                last.then_inc(o_sq, 1)
                if h >= 2 and h % 2 == 0:
                    split_h(J_DIFF + h // 2 - 1, u_hi, h - 2)
            split_h(J_DIFF + 2, u_hi, 4)
            for i in range(4):
                if i < 3:
                    split_w(N_O1 + i + AHEAD)
                act.wait_ge(xt_ready, 20 + i + 1)
                square_pair(7, i, flat(xT, 2 * i, 2 * i + 2))
            for q in range(4):
                split_h(J_H7 + q, h_hi, 2 * q)
            mlp(N_MLP2, J_MLP2, AHEAD - 1)
            for i in range(4):
                act.wait_ge(out_turned, i + 1)
                tt, q = i // 2, i % 2
                act.activation(out_tok[:, tt, 512 * q:512 * q + 512], (lin[0], lin[1], ps_ada, ps_misc)[i][:, :], ACT.Copy)\
                    .then_inc(out_copied, 1)

        @block.gpsimd
        def _(pool):
            def split_h(job, lo, hi, tile, turn=None):
                pool.wait_ge(fresh_hi, job + 1 if turn is None else turn * 4 + (job + 1))
                pool.tensor_tensor(flat(lo, tile, tile + 2), fresh[:, job % 2, :], flat(hi, tile, tile + 2).bitcast(F32),
                                   ALU.subtract).then_inc(fresh_lo, 1)

            def power(name):
                pool.wait_ge(misc_read, misc_no[name] + 1)
                at, width = root_at[name], 2 if name.startswith("sum") else 8
                pool.tensor_tensor(root[:, at:at + width], root[:, at:at + width],
                                   minus_half[:, 0:1].to_broadcast([P, width]), ALU.pow).then_inc(root_ready, 1)

            def cos_part(name, src):
                i = rope_no["rope." + name]
                pool.wait_ge(qk_normed, qk_no["qk." + name] + 1)
                if i >= 2:
                    pool.wait_ge(rope_done, i - 1)
                for a in range(2):
                    last = pool.tensor_tensor(rope_cosines[:, i % 2, a * T:a * T + T], src[:, a * T:a * T + T], cosT, ALU.mult)
                last.then_inc(rope_cos, 1)

            chain = Count()

            def link(ins):
                ins.then_inc(chain_g, 1)
                pool.wait_ge(chain_g, chain.up())

            def ada_unit(a):
                tiles = w_raw[:, slot_of["a", a], :].rearrange("p (k n) -> p k n", k=KT)
                pool.wait_ge(ada_scaled, a - ADA_FIRST + 1)
                for half in (4, 2):
                    link(pool.tensor_tensor(tiles[:, 0:half, :], tiles[:, 0:half, :], tiles[:, half:2 * half, :], ALU.add))
                if a >= ADA_FIRST + 2:
                    pool.wait_ge(ada_done, a - 1)
                pool.tensor_tensor(ada_late[:, a % 2, :], tiles[:, 0, :], tiles[:, 1, :], ALU.add).then_inc(ada_part_sum, 1)

            pool.memset(minus_half[:, :], -0.5)
            pool.memset(rel[:, :], 1.0)
            pool.memset(rows, 0.0).then_inc(filled, 1)
            pool.memset(f_cum, 0.0)
            pool.wait_ge(mem_var, 1)
            pool.tensor_tensor(stat[:, S_MEM:S_MEM + 2], stat[:, S_MEM:S_MEM + 2], minus_half[:, 0:1].to_broadcast([P, 2]),
                               ALU.pow).then_inc(mem_rstd, 1)
            for q in range(4):
                split_h(J_MEM + q, u_lo, u_hi, 2 * q)
            power("qk.mem0")
            pool.wait_ge(x_turned, 4)
            pool.tensor_copy(head_bias[:, :, 0:P], ident[:, 64:64 + HEADS].unsqueeze(2).to_broadcast([P, HEADS, P]))\
                .then_inc(sel_ready, 1)
            power("sum1")
            for q in range(4):
                split_h(J_H1 + q, h_lo, h_hi, 2 * q)
            power("qk.mem1")
            for a in range(ADA_FIRST, 14):
                ada_unit(a)
            pool.wait_ge(f_copied, 4)
            mask = causal.unsqueeze(1).to_broadcast([P, HEADS, P])
            pool.tensor_tensor(head_bias[:, :, 0:P], head_bias[:, :, P:2 * P], mask, ALU.add)
            pool.tensor_tensor(head_bias[:, :, 2 * P:3 * P], head_bias[:, :, 2 * P:3 * P], mask, ALU.add).then_inc(fox_bias, 1)
            for a in range(14, 20):
                ada_unit(a)
            for q in range(2):
                split_h(J_FOX + q, u_lo, u_hi, 2 * q)
            pool.wait_ge(bias_in, 16)
            pool.wait_ge(picked, 1)
            pool.wait_ge(score_max, HEADS)
            pool.tensor_tensor(head_bias[:, :, 0:P], toeplitz[:, :, P:2 * P], idx[:, 0:P].unsqueeze(1).to_broadcast([P, HEADS, P]),
                               ALU.add)
            pool.tensor_tensor(head_bias[:, :, P:3 * P], toeplitz, idx[:, P:3 * P].unsqueeze(1).to_broadcast([P, HEADS, 2 * P]),
                               ALU.add).then_inc(dsa_bias, 1)
            for a in range(20, ADA_UNITS):
                ada_unit(a)
            for q in range(2):
                split_h(J_DSA + q, u_lo, u_hi, 4 + 2 * q)
            for q in range(4):
                split_h(J_MERGED + q, h_lo, h_hi, 2 * q)

            def norm(s, job=None):
                power(f"sum{s}")
                if job is not None:
                    for q in range(4):
                        split_h(job + q, h_lo, h_hi, 2 * q)

            def mlp(job_u):
                for i in range(4):
                    split_h(job_u + i, u_lo, u_hi, 2 * (i % 4))
                with pool.Fori(0, MLP_LOOPS) as turn:
                    for i in range(4):
                        split_h(job_u + 4 + i, u_lo, u_hi, 2 * (i % 4), turn)

            norm(2, J_H2)
            mlp(J_MLP0)
            norm(3)
            norm(4, J_H4)
            power("qk.qm0")
            split_h(J_YM0, u_lo, u_hi, 6)
            for i in range(3):
                split_h(J_CONV + i, u_lo, u_hi, 2 * i)
            norm(5, J_H5)
            mlp(J_MLP1)
            norm(6, J_KV)
            for q in range(4):
                split_h(J_MIX1 + q, u_lo, u_hi, 2 * q)
            pool.wait_ge(late_in, 48)
            power("qk.k0")
            power("qk.k1")
            cos_part("k0", flat(qk, 0, 2))
            power("qk.k2")
            cos_part("k1", flat(qk, 2, 4))
            power("qk.qm1")
            cos_part("k2", flat(qk, 4, 6))
            power("qk.q0")
            power("qk.q1")
            cos_part("q0", flat(big, 10, 12))
            power("qk.q2")
            cos_part("q1", flat(big, 12, 14))
            cos_part("q2", flat(big, 14, 16))
            split_h(J_YM1, u_lo, u_hi, 6)
            for h in range(DIFF_HEADS):
                pool.wait_ge(o_var, h + 1)
                at = S_ORSTD + 2 * (h % 2)
                pool.tensor_tensor(stat[:, at:at + 2], stat[:, at:at + 2], minus_half[:, 0:1].to_broadcast([P, 2]), ALU.pow)\
                    .then_inc(o_rstd, 1)
                if h >= 2 and h % 2 == 0:
                    split_h(J_DIFF + h // 2 - 1, u_lo, u_hi, h - 2)
            split_h(J_DIFF + 2, u_lo, u_hi, 4)
            norm(7, J_H7)
            mlp(J_MLP2)

        @block.vector
        def _(dve):
            chain = Count()

            def link(ins):
                ins.then_inc(chain_v, 1)
                dve.wait_ge(chain_v, chain.up())

            def split_w(n, turn=None):
                if n >= N_UNITS:
                    return
                dve.wait_ge(hi_w, n + 1 if turn is None else turn * BODY + (n + 1))
                dve.tensor_tensor(w_lo[:, n % RING, :], w_raw[:, slot_of["w", n], :], w_hi[:, n % RING, :].bitcast(F32),
                                  ALU.subtract).then_inc(lo_w, 1)

            def from_misc(name):
                dve.wait_ge(misc_full, misc_no[name] + 1)

            def mean_square(name, eps=EPS):
                from_misc(name)
                width, count = (2, D) if name.startswith("sum") else (8, HD)
                dve.tensor_scalar(root[:, root_at[name]:root_at[name] + width], ps_misc[:, 0:width], 1.0 / count, eps,
                                  ALU.mult, ALU.add).then_inc(misc_read, 1)

            def fresh_slot(job):
                if job >= 2:
                    dve.wait_ge(fresh_lo, job - 1)
                return fresh[:, job % 2, :]

            def normed(job, gains, rstd, shift=None):
                for q in range(4):
                    dst = fresh_slot(job + q)
                    for i in range(2):
                        k = 2 * q + i
                        last = dve.scalar_tensor_tensor(out=dst[:, i * T:i * T + T], in0=xT[:, k, :], scalar=gains[:, k:k + 1],
                                                        in1=rstd[:, 0:T], op0=ALU.mult, op1=ALU.mult)
                    if shift is not None:
                        link(last)
                        for i in range(2):
                            k = 2 * q + i
                            last = dve.tensor_scalar(dst[:, i * T:i * T + T], dst[:, i * T:i * T + T], shift[:, k:k + 1], None,
                                                     ALU.add)
                    last.then_inc(fresh_ready, 1)

            def rstd_read():
                dve.drain().then_inc(spread_read, 1)

            def qk_scale(name, dst, gain, bank):
                dve.wait_ge(spread_full, spread_no["qk." + name] + 1)
                dve.scalar_tensor_tensor(out=dst, in0=dst, scalar=vec[:, gain:gain + 1], in1=bank[:, :],
                                         op0=ALU.mult, op1=ALU.mult).then_inc(qk_normed, 1)
                rstd_read()

            def rope_add(name, dst):
                from_misc("rope." + name)
                for a in range(2):
                    last = dve.tensor_tensor(rope_sin[:, a * T:a * T + T], ps_misc[:, a * T:a * T + T], sinT, ALU.mult)
                last.then_inc(misc_read, 1)
                dve.wait_ge(misc_read, misc_no["rope." + name] + 1)
                i = rope_no["rope." + name]
                dve.wait_ge(rope_cos, i + 1)
                dve.tensor_tensor(dst, rope_sin, rope_cosines[:, i % 2, :], ALU.add).then_inc(rope_done, 1)

            def maxima(G, span, biased):
                for odd in range(2):
                    h = 2 * G + odd
                    dve.wait_ge(score_mm, h + 1)
                    if h >= 2:
                        dve.wait_ge(turned, h - 1)
                    at = 2 * odd
                    if biased is not None:
                        for tt, (c0, c1) in enumerate(span):
                            last = dve.tensor_tensor_reduce(probs[:, odd, c0:c1], acc[odd][:, c0:c1],
                                                            head_bias[:, (2 * (G - biased)) + odd, c0:c1], 1.0, PICKED,
                                                            ALU.add, ALU.max, stat[:, S_MAX + at + tt:S_MAX + at + tt + 1])
                        link(last)
                    else:
                        link(dve.tensor_reduce(stat[:, S_MAX + at:S_MAX + at + 2],
                                               acc[odd][:, :].rearrange("p (t s) -> p t s", t=TT), AX.X, ALU.max))
                    dve.tensor_scalar(stat[:, S_NMAX + at:S_NMAX + at + 2], stat[:, S_MAX + at:S_MAX + at + 2], -1.0, None,
                                      ALU.mult).then_inc(score_max, 1)

            def attended(name, g, G, y_free=None):
                s0 = S_SUM + 4 * (G % 2)
                dve.wait_ge(exp_done, 2 * G + 2)
                link(dve.reciprocal(stat[:, S_INV:S_INV + 4], stat[:, s0:s0 + 4]))
                from_misc(f"{name}{g}")
                for odd in range(2):
                    for tt in range(TT):
                        at, c0 = 2 * odd + tt, (2 * g + odd) * HD
                        last = dve.tensor_scalar(y_tok[:, tt, c0:c0 + HD], ps_misc[:, at * HD:at * HD + HD],
                                                 stat[:, S_INV + at:S_INV + at + 1], None, ALU.mult)
                last.then_inc(misc_read, 1)

            def y_copy(job, bank_no, y_no):
                dve.wait_ge(y_turned, y_no)
                dve.tensor_copy(fresh_slot(job), acc[bank_no][:, :]).then_inc(fresh_ready, 1)

            from_misc("vec")
            dve.tensor_copy(vec[:, :], ps_misc[:, 0:2 * P]).then_inc(misc_read, 1)
            dve.wait_ge(misc_read, 1)
            dve.tensor_scalar(vec[:, V_BQ:V_BQ + 1], vec[:, V_BQ:V_BQ + 1], HD ** -0.5, None, ALU.mult)
            dve.tensor_scalar(vec[:, V_SUBLN:V_SUBLN + 1], vec[:, V_SUBLN:V_SUBLN + 1], 1.0 - LAM_INIT, None, ALU.mult)
            dve.tensor_scalar(vec[:, V_MQ:V_MQ + 2], vec[:, V_MQ:V_MQ + 2], HD ** -0.5, None, ALU.mult).then_inc(vec_ready, 1)
            dve.wait_ge(mem_sq, 1)
            dve.tensor_scalar(stat[:, S_MEM:S_MEM + 2], stat[:, S_MEM:S_MEM + 2], 1.0 / D, EPS, ALU.mult, ALU.add)\
                .then_inc(mem_var, 1)
            dve.wait_ge(mem_rstd, 1)
            for tt in range(TT):
                dve.tensor_scalar(mem_tok[:, tt, :], mem_tok[:, tt, :], stat[:, S_MEM + tt:S_MEM + tt + 1], None, ALU.mult)\
                    .then_inc(mem_scaled, 1)
            dve.wait_ge(vec_ready, 1)
            split_w(0)
            for q in range(4):
                dst = fresh_slot(J_MEM + q)
                dve.wait_ge(mem_turned, q + 1)
                for i in range(2):
                    k = 2 * q + i
                    last = dve.tensor_scalar(dst[:, i * T:i * T + T], acc[q][:, i * T:i * T + T], vec[:, V_MEM + k:V_MEM + k + 1],
                                             None, ALU.mult)
                last.then_inc(fresh_ready, 1)
            split_w(1)
            mean_square("qk.mem0")
            split_w(2)
            mean_square("sum1")
            split_w(3)
            dve.wait_ge(ada_done, ADA_FIRST)
            dve.tensor_tensor(ada[:, 0:16], ps_ada[:, 0:16], vec[:, V_ADA:V_ADA + 16], ALU.add).then_inc(ada_ready, 1)
            dve.wait_ge(ada_ready, 1)
            link(dve.scalar_tensor_tensor(out=gs[:, 0, :], in0=ada[:, 8:16], scalar=1.0, in1=vec[:, V_G1:V_G1 + 8],
                                          op0=ALU.add, op1=ALU.mult))
            dve.wait_ge(spread_full, spread_no["sum1"] + 1)
            normed(J_H1, gs[:, 0, :], acc[0], ada[:, 0:8])
            rstd_read()
            split_w(4)
            mean_square("qk.mem1")
            split_w(5)
            split_w(6)
            split_w(7)
            qk_scale("mem0", flat(mem_k[:, 0], 0, 2), V_MK, acc[1])
            qk_scale("mem1", flat(mem_k[:, 1], 0, 2), V_MK + 1, acc[2])
            z, low = idx[64:64 + HEADS, 0:T], f_low[64:64 + HEADS, :]
            dve.wait_ge(evac_a, evac_value[4])
            dve.wait_ge(small_in, 48)
            link(dve.tensor_scalar(z, f_raw[64:64 + HEADS, :], rel[64:64 + HEADS, 0:1], None, ALU.add))
            link(dve.tensor_scalar(low, z, -1.0, None, ALU.mult))
            dve.tensor_tensor(low, low, z, ALU.min).then_inc(f_in, 1)
            split_w(8)
            from_misc("wi")
            for tt in range(TT):
                last = dve.tensor_scalar(stat[:, S_WI + 4 * tt:S_WI + 4 * tt + 4], ps_misc[:, tt * P:tt * P + 4],
                                         IDX_HEADS ** -0.5, None, ALU.mult)
            last.then_inc(misc_read, 1)
            dve.wait_ge(f_ln, 1)
            link(dve.scalar_tensor_tensor(out=z, in0=z, scalar=0.0, in1=low, op0=ALU.min, op1=ALU.subtract))
            dve.tensor_tensor_scan(f_cum[64:64 + HEADS, :], ones[64:64 + HEADS, 0:1].to_broadcast([HEADS, T]), z, 0.0,
                                   ALU.mult, ALU.add).then_inc(f_ready, 1)
            dve.wait_ge(f_ready, 1)
            split_w(9)
            for h in range(IDX_HEADS):
                dve.wait_ge(idx_relu, h + 1)
                if h:
                    dve.wait_ge(idx_added, h)
                for tt, (c0, c1) in enumerate(CAUSAL_SPAN):
                    wi = stat[:, S_WI + 4 * tt + h:S_WI + 4 * tt + h + 1]
                    if h == 0:
                        dve.wait_ge(misc_read, misc_no["wi"] + 1)
                        last = dve.tensor_scalar(idx[:, c0:c1], probs[:, 0, c0:c1], wi, None, ALU.mult)
                    else:
                        last = dve.scalar_tensor_tensor(out=idx[:, c0:c1], in0=probs[:, h % 2, c0:c1], scalar=wi,
                                                        in1=idx[:, c0:c1], op0=ALU.mult, op1=ALU.add)
                last.then_inc(idx_added, 1)
            dve.wait_ge(idx_added, IDX_HEADS)
            dve.tensor_tensor(idx[:, 0:P], idx[:, 0:P], causal, ALU.add)
            link(dve.tensor_tensor(idx[:, 2 * P:3 * P], idx[:, 2 * P:3 * P], causal, ALU.add))

            def pick_eight():
                for tt, (c0, c1) in enumerate(CAUSAL_SPAN):
                    last = dve.max(top8[:, tt, :], idx[:, c0:c1])
                link(last)
                for tt, (c0, c1) in enumerate(CAUSAL_SPAN):
                    last = dve.match_replace(out=idx[:, c0:c1], in_to_replace=top8[:, tt, :], in_values=idx[:, c0:c1],
                                             imm_value=PICKED)
                link(last)

            pick_eight()
            for n in (10, 11):
                split_w(n)
                pick_eight()
            split_w(12)
            pick_eight()
            from_misc("row")
            dve.tensor_copy(bias_row[0:HEADS, :], ps_misc[0:HEADS, 0:384]).then_inc(misc_read, 1)
            split_w(13)
            pick_eight()
            split_w(14)
            pick_eight()
            dve.wait_ge(fox_bias, 1)

            def sigmoid(n, tile):
                dve.wait_ge(evac_a, evac_value[n])
                gate = flat(big, tile, tile + 2)
                dve.tensor_scalar(gate, gate, 0.5, 0.5, ALU.mult, ALU.add)

            for g in range(4):
                maxima(G_FOX + g, CAUSAL_SPAN, G_FOX)
                split_w(N_GF + g + AHEAD)
                if g < 2:
                    pick_eight()
                if g == 2:
                    dve.tensor_scalar(idx[:, :], idx[:, :], PICKED, MASKED, ALU.not_equal, ALU.mult).then_inc(picked, 1)
                sigmoid(N_GF + g, 2 * g)
                attended("fox", g, G_FOX + g)
            split_w(N_DSA + AHEAD)
            for q in range(2):
                y_copy(J_FOX + q, q, q + 1)
            for i in range(1, 6):
                split_w(N_DSA + i + AHEAD)
            dve.wait_ge(dsa_bias, 1)
            for g in range(4):
                maxima(G_DSA + g, CAUSAL_SPAN, G_DSA)
                split_w(N_GD + g + AHEAD)
                sigmoid(N_GD + g, 8 + 2 * g)
                attended("dsa", g, G_DSA + g)
            for half in range(2):
                split_w(N_BR + half + AHEAD)
                dve.wait_ge(unit_done, N_BR + half + 1)
                for q in (2 * half, 2 * half + 1):
                    gate = flat(big, 2 * q, 2 * q + 2)
                    dve.tensor_tensor(gate, gate, acc[q][:, :], ALU.mult).then_inc(branch_done, 1)
            for q in range(2):
                y_copy(J_DSA + q, q, 2 + q + 1)
            for half in range(2):
                split_w(N_BR + 2 + half + AHEAD)
                dve.wait_ge(unit_done, N_BR + 2 + half + 1)
                for q in (2 * half, 2 * half + 1):
                    gate = flat(big, 8 + 2 * q, 8 + 2 * q + 2)
                    link(dve.tensor_tensor(gate, gate, acc[q][:, :], ALU.mult))
                    dve.tensor_tensor(fresh_slot(J_MERGED + q), gate, flat(big, 2 * q, 2 * q + 2), ALU.add)\
                        .then_inc(fresh_ready, 1)
            dve.wait_ge(ada_done, ADA_UNITS)
            link(dve.tensor_tensor(ada[:, 16:48], ps_ada[:, 16:48], vec[:, V_ADA + 16:V_ADA + 48], ALU.add))
            dve.scalar_tensor_tensor(out=gs[:, 1, :], in0=ada[:, 32:40], scalar=1.0, in1=vec[:, V_G2:V_G2 + 8],
                                     op0=ALU.add, op1=ALU.mult)
            for i in range(4):
                n = N_OUT + i
                split_w(n + AHEAD)
                dve.wait_ge(unit_done, n + 1)
                for j in range(2):
                    k = 2 * i + j
                    last = dve.scalar_tensor_tensor(out=xT[:, k, :], in0=lin[lin_bank[n]][:, j * T:j * T + T],
                                                    scalar=ada[:, 16 + k:17 + k], in1=xT[:, k, :], op0=ALU.mult, op1=ALU.add)
                    if j == 0:
                        continue
                    last.then_inc(evac_v, 1)
                dve.drain().then_inc(xt_ready, 1)
            mean_square("sum2")
            dve.wait_ge(spread_full, spread_no["sum2"] + 1)
            normed(J_H2, gs[:, 1, :], ps_ada, ada[:, 24:32])
            rstd_read()

            halves = Count()

            def mlp(n0, job_u, gate=None, ahead=AHEAD):
                def up_step(n, step, turn=None):
                    at = lambda value, per: value if turn is None else turn * per + value
                    for half in range(2):
                        split_w(n + half + ahead, turn)
                        dve.wait_ge(evac_a, at(evac_value[n + half], 4))
                        dve.tensor_tensor(fresh[:, half, :], fresh[:, half, :], fresh[:, half, :], ALU.mult)\
                            .then_inc(fresh_ready, 1)

                def down_step(n, turn=None):
                    for half in range(2):
                        split_w(n + half + ahead, turn)

                up_step(n0, 0)
                up_step(n0 + 2, 1)
                down_step(n0 + 4)
                with dve.Fori(0, MLP_LOOPS) as turn:
                    for k in range(2):
                        up_step(n0 + 6 + 4 * k, 2 + k, turn)
                        down_step(n0 + 8 + 4 * k, turn)
                down_step(n0 + 30)
                for q in range(4):
                    if q % 2 == 0:
                        dve.wait_ge(half_done, halves.up())
                    else:
                        dve.wait_ge(unit_done, n0 + 30 + q // 2 + 1)
                    if gate is None:
                        pair = flat(xT, 2 * q, 2 * q + 2)
                        dve.tensor_tensor(pair, acc[q][:, :], pair, ALU.add).then_inc(xt_ready, 1)
                    else:
                        for j in range(2):
                            k = 2 * q + j
                            last = dve.scalar_tensor_tensor(out=xT[:, k, :], in0=acc[q][:, j * T:j * T + T],
                                                            scalar=gate[:, k:k + 1], in1=xT[:, k, :], op0=ALU.mult, op1=ALU.add)
                        last.then_inc(xt_ready, 1)

            mlp(N_MLP0, J_MLP0, ada[:, 40:48])
            mean_square("sum3")
            dve.wait_ge(spread_full, spread_no["sum3"] + 1)
            for q in range(4):
                for j in range(2):
                    k = 2 * q + j
                    last = dve.scalar_tensor_tensor(out=xT[:, k, :], in0=xT[:, k, :], scalar=vec[:, V_GF + k:V_GF + k + 1],
                                                    in1=ps_ada[:, 0:T], op0=ALU.mult, op1=ALU.mult)
                last.then_inc(xt_ready, 1)
            rstd_read()
            mean_square("sum4")
            dve.wait_ge(spread_full, spread_no["sum4"] + 1)
            dve.wait_ge(xt_ready, 12)
            normed(J_H4, vec[:, V_MIX:V_MIX + 8], ps_ada)
            rstd_read()
            split_w(N_QM0 + AHEAD)
            split_w(N_CONV + AHEAD)
            mean_square("qk.qm0")
            split_w(N_CONV + 1 + AHEAD)
            qk_scale("qm0", v_tok[:, 0, :], V_MQ, ps_ada)
            split_w(N_CONV + 2 + AHEAD)

            def conv(i):
                n = N_CONV + 3 + i
                dve.wait_ge(unit_done, n + 1)
                dve.wait_ge(evac_a, evac_value[N_CONV + i])
                c = flat(big, 2 * i, 2 * i + 2)
                dve.tensor_tensor(c, c, lin[lin_bank[n]][:, :], ALU.mult).then_inc(evac_v, 1)
                dve.wait_ge(evac_v, evac_value[n])
                for tap, back in ((V_CONV + 12, 0), (V_CONV + 6, 1), (V_CONV, 2)):
                    for j in range(2):
                        k = 2 * i + j
                        u, y, tap_w = big[:, k, :], big[:, 6 + k, :], vec[:, tap + k:tap + k + 1]
                        if back == 0:
                            last = dve.tensor_scalar(y, u, tap_w, None, ALU.mult)
                        else:
                            last = dve.scalar_tensor_tensor(out=y[:, back:T], in0=u[:, 0:T - back], scalar=tap_w,
                                                            in1=y[:, back:T], op0=ALU.mult, op1=ALU.add)
                    link(last)

            for g in range(2):
                maxima(G_M0 + g, FULL_SPAN, None)
                split_w(N_CONV + 3 + g + AHEAD)
                conv(g)
                attended("mem0.", g, G_M0 + g)
            split_w(N_CONV + 5 + AHEAD)
            conv(2)
            y_copy(J_YM0, 0, 5)
            for i in range(3):
                n = N_CONV + 6 + i
                split_w(n + AHEAD)
                dve.wait_ge(unit_done, n + 1)
                dst = fresh_slot(J_CONV + i)
                dve.tensor_tensor(dst, flat(big, 6 + 2 * i, 8 + 2 * i), lin[lin_bank[n]][:, :], ALU.mult).then_inc(evac_v, 1)
                dve.drain().then_inc(fresh_ready, 1)

            def residual(n0, splits=4):
                for i in range(4):
                    n = n0 + i
                    if i < splits:
                        split_w(n + AHEAD)
                    dve.wait_ge(unit_done, n + 1)
                    pair = flat(xT, 2 * i, 2 * i + 2)
                    dve.tensor_tensor(pair, lin[lin_bank[n]][:, :], pair, ALU.add).then_inc(evac_v, 1)
                    dve.drain().then_inc(xt_ready, 1)

            residual(N_O0)
            mean_square("sum5")
            dve.wait_ge(spread_full, spread_no["sum5"] + 1)
            normed(J_H5, vec[:, V_MLP:V_MLP + 8], ps_ada)
            rstd_read()
            mlp(N_MLP1, J_MLP1)
            mean_square("sum6")
            dve.wait_ge(spread_full, spread_no["sum6"] + 1)
            normed(J_KV, vec[:, V_KV:V_KV + 8], ps_ada)
            normed(J_MIX1, vec[:, V_MIX + 8:V_MIX + 16], ps_ada)
            rstd_read()
            dve.wait_ge(late_in, 48)
            split_w(N_K + AHEAD)
            dve.tensor_tensor_reduce(lam_in[:, 0, :], lam_in[:, 0, :], lam_in[:, 1, :], 1.0, 0.0, ALU.mult, ALU.add,
                                     stat[:, S_DOT:S_DOT + 1])
            dve.tensor_tensor_reduce(lam_in[:, 2, :], lam_in[:, 2, :], lam_in[:, 3, :], 1.0, 0.0, ALU.mult, ALU.add,
                                     stat[:, S_DOT + 1:S_DOT + 2]).then_inc(lam_dots, 1)
            split_w(N_K + 1 + AHEAD)
            k_pair = [flat(qk, 2 * i, 2 * i + 2) for i in range(3)]
            q_pair = [flat(big, 10 + 2 * i, 12 + 2 * i) for i in range(3)]
            mean_square("qk.k0")
            split_w(N_K + 2 + AHEAD)
            mean_square("qk.k1")
            qk_scale("k0", k_pair[0], V_K, ps_ada)
            split_w(N_Q + AHEAD)
            mean_square("qk.k2")
            qk_scale("k1", k_pair[1], V_K, ps_ada)
            rope_add("k0", k_pair[0])
            split_w(N_Q + 1 + AHEAD)
            mean_square("qk.qm1")
            qk_scale("k2", k_pair[2], V_K, ps_ada)
            rope_add("k1", k_pair[1])
            split_w(N_Q + 2 + AHEAD)
            mean_square("qk.q0")
            qk_scale("qm1", v_tok[:, 0, :], V_MQ + 1, ps_ada)
            rope_add("k2", k_pair[2])
            split_w(N_Q + 3 + AHEAD)
            mean_square("qk.q1")
            qk_scale("q0", q_pair[0], V_BQ, ps_ada)
            split_w(N_V + AHEAD)
            mean_square("qk.q2")
            qk_scale("q1", q_pair[1], V_BQ, ps_ada)
            rope_add("q0", q_pair[0])
            dve.wait_ge(lam_exp, 1)
            link(dve.tensor_tensor(stat[:, S_NLAM:S_NLAM + 1], stat[:, S_LAM + 1:S_LAM + 2], stat[:, S_LAM:S_LAM + 1],
                                   ALU.subtract))
            dve.tensor_scalar(stat[:, S_NLAM:S_NLAM + 1], stat[:, S_NLAM:S_NLAM + 1], -LAM_INIT, None, ALU.add)
            for g in range(2):
                maxima(G_M1 + g, FULL_SPAN, None)
                split_w(N_V + 1 + g + AHEAD)
                if g == 0:
                    qk_scale("q2", q_pair[2], V_BQ, ps_ada)
                    rope_add("q1", q_pair[1])
                else:
                    rope_add("q2", q_pair[2])
                attended("mem1.", g, G_M1 + g)

            def d_maxima(h):
                dve.wait_ge(d_score, h + 1)
                if h >= 2:
                    dve.wait_ge(d_turned, h - 1)
                for m in range(2):
                    for tt, (c0, c1) in enumerate(CAUSAL_SPAN):
                        at = 4 * (h % 2) + 2 * m + tt
                        last = dve.tensor_tensor_reduce(head_bias[:, 2 * (h % 2) + m, c0:c1], acc[2 * (h % 2) + m][:, c0:c1],
                                                        chunk_mask[:, c0:c1], 1.0, PICKED, ALU.add, ALU.max,
                                                        stat[:, S_DMAX + at:S_DMAX + at + 1])
                link(last)
                at = 4 * (h % 2)
                dve.tensor_scalar(stat[:, S_DNMAX + at:S_DNMAX + at + 4], stat[:, S_DMAX + at:S_DMAX + at + 4], -1.0, None,
                                  ALU.mult).then_inc(d_max, 1)

            def mix(h):
                dve.wait_ge(d_exp, h + 1)
                at = 4 * (h % 2)
                inv = stat[:, S_DINV + at:S_DINV + at + 4]
                link(dve.reciprocal(inv, stat[:, S_DSUM + at:S_DSUM + at + 4]))
                link(dve.tensor_scalar(inv[:, 2:4], inv[:, 2:4], stat[:, S_NLAM:S_NLAM + 1], None, ALU.mult))
                p1, p2 = head_bias[:, 2 * (h % 2), :], head_bias[:, 2 * (h % 2) + 1, :]
                for tt, (c0, c1) in enumerate(CAUSAL_SPAN):
                    last = dve.tensor_scalar(p2[:, c0:c1], p2[:, c0:c1], inv[:, 2 + tt:3 + tt], None, ALU.mult)
                link(last)
                for tt, (c0, c1) in enumerate(CAUSAL_SPAN):
                    last = dve.scalar_tensor_tensor(out=p1[:, c0:c1], in0=p1[:, c0:c1], scalar=inv[:, tt:tt + 1],
                                                    in1=p2[:, c0:c1], op0=ALU.mult, op1=ALU.add)
                last.then_inc(mixed, 1)

            def o_copy(h):
                from_misc(f"pv{h}")
                c0 = (h % 2) * P
                for tt in range(TT):
                    last = dve.tensor_copy(y_tok[:, tt, c0:c0 + P], ps_misc[:, tt * P:tt * P + P])
                last.then_inc(misc_read, 1)
                dve.drain().then_inc(o_copied, 1)

            def o_mean(h):
                dve.wait_ge(o_sq, h + 1)
                at = 2 * (h % 2)
                dve.tensor_scalar(stat[:, S_ORSTD + at:S_ORSTD + at + 2], stat[:, S_OSS + at:S_OSS + at + 2], 1.0 / (2 * HD),
                                  SUBLN_EPS, ALU.mult, ALU.add).then_inc(o_var, 1)

            def o_scale(h):
                dve.wait_ge(o_rstd, h + 1)
                c0 = (h % 2) * P
                for tt in range(TT):
                    at = S_ORSTD + 2 * (h % 2) + tt
                    last = dve.tensor_scalar(y_tok[:, tt, c0:c0 + P], y_tok[:, tt, c0:c0 + P], stat[:, at:at + 1], None, ALU.mult)
                last.then_inc(o_scaled, 1)

            def o_take(h):
                job = J_DIFF + h // 2
                from_misc(f"oT{h}")
                dst = fresh_slot(job)[:, (h % 2) * T:(h % 2) * T + T]
                dve.tensor_scalar(dst, ps_misc[:, 0:T], vec[:, V_SUBLN:V_SUBLN + 1], None, ALU.mult).then_inc(misc_read, 1)
                if h % 2:
                    dve.drain().then_inc(fresh_ready, 1)

            y_copy(J_YM1, 0, 6)
            d_maxima(0)
            for h in range(DIFF_HEADS):
                mix(h)
                if h >= 2:
                    o_take(h - 2)
                if h >= 1:
                    o_mean(h - 1)
                if h + 1 < DIFF_HEADS:
                    d_maxima(h + 1)
                if h >= 1:
                    o_scale(h - 1)
                o_copy(h)
            o_mean(DIFF_HEADS - 1)
            o_take(DIFF_HEADS - 2)
            o_scale(DIFF_HEADS - 1)
            o_take(DIFF_HEADS - 1)
            residual(N_O1, 3)
            mean_square("sum7")
            dve.wait_ge(spread_full, spread_no["sum7"] + 1)
            normed(J_H7, vec[:, V_MLP + 8:V_MLP + 16], ps_ada)
            rstd_read()
            mlp(N_MLP2, J_MLP2, ahead=AHEAD - 1)


_WEIGHTS = {"w_ada": "w_ada", "w_in": "w_in", "w_branch_fox": "w_branch_fox", "w_branch_dsa": "w_branch_dsa",
            "w_out": "w_out", "w_mlp1": "w_mlp1", "w_mlp2": "w_mlp2", "a_w_in": "a_w_in_2", "b_w_q": "b_w_q_2",
            "w_kv": "w_kv_2", "w_mem_kv": "w_mem_kv_2", "w_o": "w_o_2", "w_up": "w_up_2", "w_down": "w_down_2"}
_VECTORS = {"c": "c", "b_ada": "b_ada", "g_norm1": "g_norm1", "g_norm2": "g_norm2", "g_final": "g_final",
            "norm_mix": "norm_mix_2", "norm_mlp": "norm_mlp_2", "kv_norm": "kv_norm_2", "mem_norm": "mem_norm_2",
            "a_conv": "a_conv_2", "b_subln": "b_subln_2", "b_q_norm": "b_q_norm_2", "k_norm": "k_norm_2",
            "mem_q_norm": "mem_q_norm_2", "mem_k_norm": "mem_k_norm_2", "rel_bias": "rel_bias",
            "b_forget": "b_forget", "b_lam": "b_lam_2"}


def kernel(**inputs):
    import numpy as _np
    import concourse.bacc as _bacc
    from concourse import mybir as _mybir
    from concourse.bass_utils import run_bass_kernel_spmd as _run

    nc = _bacc.Bacc("TRN2", target_bir_lowering=False, num_devices=1)
    arrays = {}

    def give(name, a):
        a = _np.ascontiguousarray(a)
        arrays[f"in_{name}"] = a
        return nc.dram_tensor(f"in_{name}", a.shape, _mybir.dt.from_np(a.dtype), kind="ExternalInput").ap()

    x = give("x", _np.asarray(inputs["x"]).reshape(T, D))
    w = {name: give(name, inputs[key]) for name, key in _WEIGHTS.items()}
    vectors = {name: give(name, _np.asarray(inputs[key]).reshape(-1)) for name, key in _VECTORS.items()}
    vectors["mem"] = give("mem", _np.asarray(inputs["mem_2"]).reshape(T, D))
    tables = {name: give(name, table) for name, table in host_tables().items()}
    out = nc.dram_tensor("out_dram", (1, T, D), _mybir.dt.float32, kind="ExternalOutput").ap()
    two_blocks(nc, x, w, vectors, tables, out.rearrange("b t d -> (b t) d"))
    r = _run(nc, [arrays], core_ids=[0])
    return r.results[0]["out_dram"]
```

```python
from contextlib import ExitStack

import numpy as np

import concourse.bass as bass
from concourse import mybir

F32 = mybir.dt.float32
F32R = mybir.dt.float32r
ALU = mybir.AluOpType
ACT = mybir.ActivationFunctionType
AX = mybir.AxisListType

P = 128
T = 256
TT = T // P
D = 1024
KT = D // P
HD = 64
HEADS = 8
IDX_HEADS = 4
TOPK = T // 4
FF = 4 * D
MEM_HEADS = 4
MEM_W = MEM_HEADS * HD
MAIN_W = D - MEM_W
CT = MAIN_W // P
DIFF_HEADS = MAIN_W // (2 * HD)
EPS = 1e-6
SUBLN_EPS = 1e-5
LAM_INIT = 0.8 - 0.6 * float(np.exp(-0.3 * 1))
MASKED = -1e30
PICKED = -3e38

C_QF, C_KF, C_VF, C_F = 0, 512, 1024, 1536
C_QD, C_KD, C_VD = 1544, 2056, 2568
C_QI, C_KI, C_WI = 3080, 3336, 3400
C_GF, C_GD = 3404, 4428

V_C, V_ADA, V_G1, V_G2, V_GF, V_MIX, V_MLP, V_KV, V_MEM = 0, 8, 56, 64, 72, 80, 96, 112, 120
V_CONV, V_SUBLN, V_BQ, V_K, V_MQ, V_MK = 128, 146, 147, 148, 149, 151
V_COLUMNS = 153

RING = 4
AHEAD = 3
FF_STEPS = FF // 512
MLP_LOOPS = 3
BODY = 8


ADA_UNITS = 24
ADA_FIRST = 8


def plan_loads():
    order = [("w", 0), ("a", 0), ("w", 1), ("a", 1), ("a", 2), ("w", 2)] + [("a", a) for a in range(3, ADA_FIRST)]
    order += [("w", 3), ("w", 4)]
    a = ADA_FIRST
    for n in range(5, N_UNITS):
        order.append(("w", n))
        if a < ADA_UNITS and n % 5 != 4:
            order.append(("a", a))
            a += 1
    return order


def plan_units(w):
    units = []

    def n_unit(name, src, col, user, pieces=None):
        cols = src.rearrange("(k p) n -> p k n", p=P)
        pieces = pieces or [(0, col, 256)]
        units.append(("N", name, [(at, cols[:, :, c:c + width]) for at, c, width in pieces], user))

    def k_unit(name, src, row, col, user=None):
        rows = src[row:row + 512, col:col + 512].rearrange("(k p) n -> p k n", p=P)
        units.append(("K", name, [(0, rows)], user))

    def mlp(name, up, down):
        for j in range(FF_STEPS + 1):
            if j < FF_STEPS:
                n_unit(f"{name}.up", up, 512 * j, "a")
                n_unit(f"{name}.up", up, 512 * j + 256, "a")
            if j >= 1:
                k_unit(f"{name}.down", down, 512 * (j - 1), 0)
                k_unit(f"{name}.down", down, 512 * (j - 1), 512)

    for l in range(2):
        n_unit(f"mem{l}.k", w["w_mem_kv"][l], 0, "a")
        n_unit(f"mem{l}.v", w["w_mem_kv"][l], MEM_W, "a")
    w_in = w["w_in"]
    n_unit("idx.k", w_in, 0, "a", [(0, C_KI, 64), (64, C_KI, 128), (192, C_F, 64)])
    n_unit("idx.q", w_in, C_QI, "a")
    for c in (C_QF, C_KF, C_VF):
        n_unit("fox", w_in, c, "a")
        n_unit("fox", w_in, c + 256, "a")
    for i in range(4):
        n_unit("gate.fox", w_in, C_GF + 256 * i, "a")
    for c in (C_QD, C_KD, C_VD):
        n_unit("dsa", w_in, c, "a")
        n_unit("dsa", w_in, c + 256, "a")
    for i in range(4):
        n_unit("gate.dsa", w_in, C_GD + 256 * i, "a")
    for name in ("w_branch_fox", "w_branch_dsa"):
        k_unit("branch", w[name], 0, 0)
        k_unit("branch", w[name], 0, 512)
    for i in range(4):
        n_unit("out", w["w_out"], 256 * i, "v")
    mlp("mlp0", w["w_mlp1"], w["w_mlp2"])
    a_in = w["a_w_in"][0]
    n_unit("qm0", a_in, 3 * MAIN_W, "a")
    for c, user in ((MAIN_W, "a"), (2 * MAIN_W, "v"), (0, "v")):
        for i in range(3):
            n_unit("conv", a_in, c + 256 * i, user)
    for i in range(4):
        n_unit("o0", w["w_o"][0], 256 * i, "v")
    mlp("mlp1", w["w_up"][0], w["w_down"][0])
    for i in range(3):
        n_unit("k", w["w_kv"], 256 * i, "a")
    for i in (3, 0, 1, 2):
        n_unit("q", w["b_w_q"][0], 256 * i, "a")
    for i in range(3):
        n_unit("v", w["w_kv"], MAIN_W + 256 * i, "a")
    for i in range(4):
        n_unit("o1", w["w_o"][1], 256 * i, "v")
    mlp("mlp2", w["w_up"][1], w["w_down"][1])
    return units


N_MEM, N_IDX, N_FOX, N_GF, N_DSA, N_GD, N_BR, N_OUT, N_MLP0 = 0, 4, 6, 12, 16, 22, 26, 30, 34
N_QM0, N_CONV, N_O0, N_MLP1, N_K, N_Q, N_V, N_O1, N_MLP2 = 66, 67, 76, 80, 112, 115, 119, 122, 126
N_UNITS = 158

MISC = (["sum0", "sum1", "qk.mem0", "row", "qk.mem1", "wi"] + [f"fox{g}" for g in range(4)]
        + [f"dsa{g}" for g in range(4)] + ["sum2", "sum3", "qk.qm0", "mem0.0", "mem0.1", "sum5", "sum6",
           "qk.k0", "qk.k1", "qk.k2", "rope.k0", "qk.qm1", "rope.k1", "qk.q0", "rope.k2", "qk.q1", "qk.q2", "rope.q0",
           "rope.q1", "mem1.0", "rope.q2", "mem1.1", "pv0"]
        + [f"{what}{h - (what == 'oT')}" for h in range(1, DIFF_HEADS) for what in ("pv", "oT")] + ["oT5", "sum7"])
POWERS = [m for m in MISC if m[:3] in ("sum", "qk.")]
POWERS.insert(POWERS.index("sum3") + 1, "sum4")
QK_NORMS = [m for m in MISC if m.startswith("qk.")]
ROPES = [m for m in MISC if m.startswith("rope.")]
SPREAD = POWERS

J_MEM, J_H1, J_FOX, J_DSA, J_MERGED, J_H2, J_MLP0 = 0, 4, 8, 10, 12, 16, 20
J_H4, J_YM0, J_CONV, J_H5, J_MLP1 = 36, 40, 41, 44, 48
J_KV, J_MIX1, J_YM1, J_DIFF, J_H7, J_MLP2 = 64, 68, 72, 73, 76, 80
G_FOX, G_DSA, G_M0, G_M1 = 0, 4, 8, 10


class Count:

    def __init__(self):
        self.n, self.turn, self.per = 0, None, 0

    def up(self, k=1):
        self.n += k
        return self.now()

    def now(self, off=0):
        v = self.n + off
        return v if self.turn is None else self.turn * self.per + v

    def enter(self, turn, per):
        self.turn, self.per, self.entered = turn, per, self.n

    def leave(self, turns):
        assert self.n - self.entered == self.per, (self.n - self.entered, self.per)
        self.n = self.entered + self.per * turns
        self.turn = None


def host_tables():
    t = np.arange(P)
    ident = np.eye(P, dtype=np.float32)
    ones = np.ones((P, P), np.float32)
    heads2 = (t[:, None] // HD == t[None, :] // HD).astype(np.float32)
    causal = np.where(t[None, :] <= t[:, None], 0, MASKED).astype(np.float32)
    chunk = np.where(t[None, :] // 64 <= t[:, None] // 64, 0, MASKED).astype(np.float32)
    consts = np.concatenate([ident, ones, heads2, causal], 1)
    chunks = np.concatenate([chunk, np.zeros((P, P), np.float32), chunk], 1)
    half = 8
    inv = (1.0 / (np.float32(500000.0) ** (np.arange(0, 2 * half, 2, dtype=np.float32) / np.float32(2 * half))))
    ang = np.arange(T, dtype=np.float32)[None, :] * inv.astype(np.float32)[:, None]
    cos, sin = np.ones((P, T), np.float32), np.zeros((P, T), np.float32)
    perm = np.zeros((P, P), np.float32)
    for base in (0, HD):
        for i in range(half):
            cos[base + i] = cos[base + half + i] = np.cos(ang[i])
            sin[base + i] = sin[base + half + i] = np.sin(ang[i])
            perm[base + half + i, base + i] = -1.0
            perm[base + i, base + half + i] = 1.0
    rope = np.concatenate([cos, sin, perm], 1)
    dist = 255 - np.arange(384)
    n = np.maximum(dist, 0)
    large = 16 + (np.log(np.maximum(n, 1).astype(np.float32) / np.float32(16)) / np.float32(np.log(8.0))
                  * np.float32(16)).astype(np.int32)
    bucket = np.where(n < 16, n, np.minimum(large, 31))
    buckets = np.zeros((33, 384), np.float32)
    buckets[bucket, np.arange(384)] = dist >= 0
    buckets[32] = np.where(dist >= 0, 0, MASKED)
    return {"consts": consts, "chunks": chunks, "rope": rope, "buckets": buckets}


def two_blocks(nc, x, mem, w, vectors, tables, out):
    units = plan_units(w)
    assert len(units) == N_UNITS
    loads = plan_loads()
    slot_of, value_of, slot_count = {}, {}, [0] * RING
    for i, (kind, n) in enumerate(loads):
        slot_count[i % RING] += 16 * (len(units[n][2]) if kind == "w" else 1)
        slot_of[kind, n], value_of[kind, n] = i % RING, slot_count[i % RING]
    assert all(slot_of["w", n] == n % RING for n in range(N_MLP0, N_UNITS))
    lin_bank, before, evac_value = [], [], []
    emptied, order = {"a": 0, "v": 0}, []
    for n, (_, _, _, user) in enumerate(units):
        lin_bank.append(len(order) % 2 if user else None)
        before.append(order[-2] if user and len(order) >= 2 else None)
        if user:
            emptied[user] += 1
            order.append((user, emptied[user]))
        evac_value.append(emptied[user] if user else None)

    misc_no = {name: i for i, name in enumerate(MISC)}
    misc_no["sum4"] = misc_no["sum3"]
    power_no = {name: i for i, name in enumerate(POWERS)}
    spread_no = {name: i for i, name in enumerate(SPREAD)}
    root_at, root_columns = {}, 0
    for name in POWERS:
        root_at[name] = root_columns
        root_columns += 2 if name.startswith("sum") else 8
    qk_no = {name: i for i, name in enumerate(QK_NORMS)}
    rope_no = {name: i for i, name in enumerate(ROPES)}

    ctx = ExitStack()
    with ctx:
        def sb(name, shape, dt=F32):
            return ctx.enter_context(nc.sbuf_tensor(name, shape, dt))

        def sem(name):
            return ctx.enter_context(nc.semaphore(name))

        w_raw = sb("w_raw", [P, RING, 2048])
        w_hi = sb("w_hi", [P, RING, 2048], F32R)
        w_lo = sb("w_lo", [P, RING, 2048], F32R)
        xT = sb("xT", [P, KT, T])
        h_hi = sb("h_hi", [P, KT, T], F32R)
        h_lo = sb("h_lo", [P, KT, T], F32R)
        u_hi = sb("u_hi", [P, KT, T], F32R)
        u_lo = sb("u_lo", [P, KT, T], F32R)
        fresh = sb("fresh", [P, 2, 512])
        qk = sb("qk", [P, 8, T])
        v_tok = sb("v_tok", [P, TT, 512])
        big = sb("big", [P, 16, T])
        head_bias = sb("head_bias", [P, HEADS, 384])
        idx = sb("idx", [P, 384])
        probs = sb("probs", [P, 2, 512])
        probsT = sb("probsT", [P, 2, 512])
        y_tok = sb("y_tok", [P, TT, 512])
        mem_k = sb("mem_k", [P, 2, 2, T])
        mem_v = sb("mem_v", [P, 2, TT, MEM_W])
        consts = sb("consts", [P, 4 * P])
        vec = sb("vec", [P, V_COLUMNS])
        ada = sb("ada", [P, 48])
        gs = sb("gs", [P, 2, KT])
        root = sb("root", [P, root_columns])
        ada_late = sb("ada_late", [P, 2, T])
        stat = sb("stat", [P, 96])
        top8 = sb("top8", [P, 2, 8])
        minus_half = sb("minus_half", [P, 1])
        rel = sb("rel", [P, 8])

        def flat(t, a, b):
            return t[:, a:b, :].rearrange("p a n -> p (a n)")

        ident, ones, heads2, causal = (consts[:, i * P:i * P + P] for i in range(4))
        sq_sum = ada_late
        ada_row = flat(big, 0, 4)[0:1, :]
        memT = qk
        qi, ki = v_tok[:, 0, :].rearrange("p (a n) -> p a n", a=2), v_tok[:, 1, 0:T]
        f_cum, f_raw, f_low = y_tok[:, 0, 0:T], y_tok[:, 1, 0:T], y_tok[:, 1, T:2 * T]
        buckets, bias_row = probsT[:, 0, 0:384], probsT[:, 1, 0:384]
        toeplitz = big[:, 8:16, :]
        cosT, sinT, perm = big[:, 6, :], big[:, 7, :], big[:, 8, 0:P]
        lam_in = big[:, 9, :].rearrange("p (a d) -> p a d", a=4)
        diff_v = flat(big, 0, 6).rearrange("p (t n) -> p t n", t=TT)
        diff_q = big[:, 10:16, :]
        chunk_mask = head_bias[:, 4, :]
        rope_sin = flat(head_bias, 0, 2)[:, 0:2 * T]
        rope_cosines = flat(head_bias, 5, 8)[:, 0:4 * T].rearrange("p (a n) -> p a n", a=2)
        head_ones = heads2.rearrange("p (h d) -> p h d", d=HD)[:, :, 0]
        S_WI, S_MAX, S_NMAX, S_SUM, S_INV, S_DOT, S_LAM, S_NLAM = 8, 16, 20, 24, 32, 36, 38, 40
        S_DMAX, S_DNMAX, S_DSUM, S_DINV, S_OSS, S_ORSTD = 44, 52, 60, 68, 76, 80

        bank = [ctx.enter_context(nc.psum_tensor(f"bank{i}", [P, 512], F32)) for i in range(8)]
        lin, acc, ps_ada, ps_misc = bank[0:2], bank[2:6], bank[6], bank[7]
        SKEW = 384 + 1
        bias_dram = nc.dram_tensor("bias_rows", (HEADS, P * SKEW), F32, kind="Internal").ap()

        raw_full = [sem(f"raw_full{s}") for s in range(RING)]
        consts_in, vec_in, x_in, small_in = (sem(s) for s in ("consts_in", "vec_in", "x_in", "small_in"))
        mem_in = [sem(f"mem_in{i}") for i in range(2)]
        bias_out, bias_in, late_in, y_out = (sem(s) for s in ("bias_out", "bias_in", "late_in", "y_out"))
        hi_w, lo_w, unit_done, evac_a, evac_v = (sem(s) for s in ("hi_w", "lo_w", "unit_done", "evac_a", "evac_v"))
        fresh_ready, fresh_hi, fresh_lo = sem("fresh_ready"), sem("fresh_hi"), sem("fresh_lo")
        chain_v, chain_a, chain_g = sem("chain_v"), sem("chain_a"), sem("chain_g")
        misc_full, misc_read = sem("misc_full"), sem("misc_read")
        vec_ready, sq_summed = sem("vec_ready"), sem("sq_summed")
        ada_used, ada_copied, ada_vector, ada_scaled, ada_part_sum = (sem(s) for s in (
            "ada_used", "ada_copied", "ada_vector", "ada_scaled", "ada_part_sum"))
        ada_done, ada_ready = sem("ada_done"), sem("ada_ready")
        xt_ready, sq_ready, sq_used, root_ready, spread_full, spread_read = (sem(s) for s in (
            "xt_ready", "sq_ready", "sq_used", "root_ready", "spread_full", "spread_read"))
        qk_normed, rope_cos, rope_done = (sem(s) for s in ("qk_normed", "rope_cos", "rope_done"))
        f_in, f_exp, f_ln, f_ready, sel_ready, f_bc, f_copied, fox_bias = (sem(s) for s in (
            "f_in", "f_exp", "f_ln", "f_ready", "sel_ready", "f_bc", "f_copied", "fox_bias"))
        idx_mm, idx_relu, idx_added, picked, dsa_bias = (sem(s) for s in (
            "idx_mm", "idx_relu", "idx_added", "picked", "dsa_bias"))
        score_mm, score_max, exp_done, turned, turned_copied, y_turned, y_copied = (sem(s) for s in (
            "score_mm", "score_max", "exp_done", "turned", "turned_copied", "y_turned", "y_copied"))
        branch_done, half_done = sem("branch_done"), sem("half_done")
        lam_dots, lam_exp = sem("lam_dots"), sem("lam_exp")
        d_score, d_max, d_exp, mixed, d_turned, d_copied, o_copied, o_sq, o_var, o_rstd, o_scaled = (sem(s) for s in (
            "d_score", "d_max", "d_exp", "mixed", "d_turned", "d_copied", "o_copied", "o_sq", "o_var", "o_rstd", "o_scaled"))

        CAUSAL_BLOCKS, CAUSAL_SPAN = [(0, 0, 0), (1, 0, 128), (1, 1, 256)], [(0, 128), (128, 384)]
        FULL_BLOCKS, FULL_SPAN = [(0, 0, 0), (0, 1, 128), (1, 0, 256), (1, 1, 384)], [(0, 256), (256, 512)]

        ada_after = {loads[i - 1][1]: a for i, (kind, a) in enumerate(loads) if kind == "a" and a >= ADA_FIRST}

        block = ctx.enter_context(nc.Block())

        @block.sync
        def _(sp):
            def slot_view(n, at, width):
                slot = w_raw[:, slot_of["w", n], :]
                if units[n][0] == "N":
                    return slot.rearrange("p (k n) -> p k n", k=KT)[:, :, at:at + width]
                return slot.rearrange("p (k n) -> p k n", k=4)

            position = {what: i for i, what in enumerate(loads)}

            def slot_free(kind, n):
                i = position[kind, n] - RING
                if i < 0:
                    return
                kind, m = loads[i]
                if kind == "w":
                    sp.wait_ge(lo_w, m + 1)
                elif m < ADA_FIRST:
                    sp.wait_ge(ada_vector if m % 2 else ada_used, m // 2 + 1)
                else:
                    sp.wait_ge(ada_part_sum, m - ADA_FIRST + 1)

            def load_unit(n):
                slot_free("w", n)
                for at, src in units[n][2]:
                    sp.dma_start(slot_view(n, at, src.shape[-1]), src).then_inc(raw_full[slot_of["w", n]], 16)

            def load_ada(a):
                slot_free("a", a)
                s = slot_of["a", a]
                cols = w["w_ada"].rearrange("(k p) n -> p k n", p=P)[:, :, 256 * a:256 * a + 256]
                sp.dma_start(w_raw[:, s, :].rearrange("p (k n) -> p k n", k=KT), cols).then_inc(raw_full[s], 16)

            def load(first, last):
                for kind, n in loads[position[first]:position[last] + 1]:
                    (load_unit if kind == "w" else load_ada)(n)

            def load_mlp(n0, up, down):
                up_cols = up.rearrange("(k p) n -> p k n", p=P)
                down_rows = down.rearrange("(j k p) n -> p j k n", j=FF_STEPS, p=P)
                for n in range(n0, n0 + 6):
                    load_unit(n)
                with sp.Fori(0, MLP_LOOPS) as turn:
                    for k in range(BODY):
                        n = n0 + 6 + k
                        is_up = k % 4 < 2
                        step = 2 + k // 4 if is_up else 1 + k // 4
                        at = sp.snap(turn * 1024 + (512 * step + 256 * (k % 2))) if is_up else sp.snap(turn * 2 + step)
                        free = sp.snap(turn * BODY + (n - RING + 1))
                        sp.wait_ge(lo_w, free)
                        if is_up:
                            sp.dma_start(slot_view(n, 0, 256), up_cols[:, :, bass.ds(at, 256)])\
                                .then_inc(raw_full[n % RING], 16)
                        else:
                            c0 = 512 * (k % 2)
                            sp.dma_start(w_raw[:, n % RING, :].rearrange("p (j k n) -> p j k n", j=1, k=4),
                                         down_rows[:, bass.ds(at, 1), :, c0:c0 + 512]).then_inc(raw_full[n % RING], 16)
                for n in range(n0 + 30, n0 + 32):
                    load_unit(n)

            sp.dma_start(consts[:, :], tables["consts"]).then_inc(consts_in, 16)
            for half in range(2):
                sp.dma_start(memT[:, 4 * half:4 * half + 4, :], mem[:, 4 * half:4 * half + 4, :]).then_inc(mem_in[half], 16)
            sp.dma_start(vec[:, :], tables["vec"]).then_inc(vec_in, 16)
            load(("w", 0), ("a", 0))
            sp.dma_start(xT[:, :, :], x).then_inc(x_in, 16)
            load(("w", 1), ("w", 2))
            sp.dma_start(rel[0:32, :], vectors["rel_bias"].rearrange("(b h) -> b h", h=HEADS)).then_inc(small_in, 16)
            sp.dma_start(rel[64:64 + HEADS, 0:1], vectors["b_forget"].rearrange("(h o) -> h o", o=1)).then_inc(small_in, 16)
            sp.dma_start(buckets[0:33, :], tables["buckets"]).then_inc(small_in, 16)
            load(("a", 3), ("a", 5))
            sp.wait_ge(misc_read, misc_no["row"] + 1)
            sp.dma_start(bass.AP(bias_dram.tensor, bias_dram.offset, [[P * SKEW, HEADS], [SKEW, P], [1, 384]]),
                         bias_row[0:HEADS, :].unsqueeze(1).to_broadcast([HEADS, P, 384])).then_inc(bias_out, 16)
            load(("a", 6), ("w", 6))
            sp.wait_ge(bias_out, 16)
            sp.wait_ge(ada_ready, 1)
            sp.dma_start(toeplitz, bass.AP(bias_dram.tensor, bias_dram.offset + P - 1, [[SKEW - 1, P], [P * SKEW, HEADS], [1, T]]))\
                .then_inc(bias_in, 16)
            load(("a", 9), ("w", 15))
            load(loads[position["w", 15] + 1], ("w", N_MLP0 - 1))
            load_mlp(N_MLP0, w["w_mlp1"], w["w_mlp2"])
            for n in range(N_QM0, N_MLP1):
                load_unit(n)
            load_mlp(N_MLP1, w["w_up"][0], w["w_down"][0])
            sp.dma_start(flat(big, 6, 9)[:, 0:2 * T + P], tables["rope"]).then_inc(late_in, 16)
            sp.dma_start(big[:, 9, :], vectors["b_lam"].partition_broadcast(P)).then_inc(late_in, 16)
            sp.dma_start(chunk_mask, tables["chunks"]).then_inc(late_in, 16)
            for n in range(N_K, N_MLP2):
                load_unit(n)
            load_mlp(N_MLP2, w["w_up"][1], w["w_down"][1])
            for q in range(4):
                sp.wait_ge(xt_ready, 24 + q + 1)
                sp.dma_start(out[:, 2 * q:2 * q + 2, :], xT[:, 2 * q:2 * q + 2, :]).then_inc(y_out, 16)
            sp.wait_ge(y_out, 64)

        @block.tensor
        def _(pe):
            pairs = Count()

            def mm(dst, lhsT, rhs, start, stop):
                return pe.matmul(dst, lhsT, rhs, start=start, stop=stop, skip_group_check=True)

            def into_misc(name):
                if misc_no[name]:
                    pe.wait_ge(misc_read, misc_no[name])

            def start_unit(n, turn):
                pe.wait_ge(lo_w, n + 1 if turn is None else turn * BODY + (n + 1))
                if before[n]:
                    user, value = before[n]
                    pe.wait_ge(evac_a if user == "a" else evac_v, value if turn is None else turn * 4 + value)

            def product(n, hi, lo, first_tile=0, banks=None, start=True, turn=None, bank_order=False, job=None):
                start_unit(n, turn)
                banks = banks or [lin[lin_bank[n]]]
                kts, nts = (KT, 2) if units[n][0] == "N" else (4, 4)
                wh = w_hi[:, n % RING, :].rearrange("p (k n) -> p k n", k=kts)
                wl = w_lo[:, n % RING, :].rearrange("p (k n) -> p k n", k=kts)
                order = [(kt, nt) for kt in range(kts) for nt in range(nts)]
                if bank_order:
                    order = [(kt, 2 * b + i) for b in range(nts // 2) for kt in range(kts) for i in range(2)]
                steps = [(kt, nt, i) for kt, nt in order for i in range(3)]
                if job is not None:
                    steps = [(kt, nt, i) for kt, nt in order for i in (0, 2)] + [(kt, nt, 1) for kt, nt in order]
                parts, started = ((wh, hi), (wh, lo), (wl, hi)), set()
                for at, (kt, nt, i) in enumerate(steps):
                    if job is not None and kt % 2 == 0 and nt == 0 and i != 2:
                        pe.wait_ge(fresh_lo if i == 1 else fresh_hi, job + kt // 2 + 1)
                    a, b = parts[i]
                    bank_no = nt // 2
                    last = mm(banks[bank_no][:, (nt % 2) * T:(nt % 2) * T + T], a[:, kt, nt * P:nt * P + P],
                              b[:, first_tile + kt, :], start and bank_no not in started,
                              all(n != nt for _, n, _ in steps[at + 1:]))
                    started.add(bank_no)
                    if bank_order and kt == kts - 1 and nt == 1 and i == 2:
                        last.then_inc(half_done, 1)
                last.then_inc(unit_done, 1)

            def part(n, pair, hi, lo, first=False, last=False, products="hl"):
                wh, wl = (t[:, n % RING, :].rearrange("p (k n) -> p k n", k=KT) for t in (w_hi, w_lo))
                which = [(w, x) for w, x, kind in ((wh, hi, "h"), (wl, hi, "h"), (wh, lo, "l")) if kind in products]
                for kt in (2 * pair, 2 * pair + 1):
                    for nt in range(2):
                        for i, (w, x) in enumerate(which):
                            ins = mm(lin[lin_bank[n]][:, nt * T:nt * T + T], w[:, kt, nt * P:nt * P + P], x[:, kt, :],
                                     first and kt % 2 == 0 and nt == 0 and i == 0,
                                     last and kt % 2 == 1 and i == len(which) - 1)
                if last:
                    ins.then_inc(unit_done, 1)

            def product_two(n, hi, lo, pairs, early=0):
                start_unit(n, None)
                for at, (pair, job) in enumerate(pairs[:early]):
                    pe.wait_ge(fresh_hi, job + 1)
                    part(n, pair, hi, lo, first=at == 0, products="h")
                for at, (pair, job) in enumerate(pairs[:early]):
                    if at == 0:
                        start_unit(n + 1, None)
                    part(n + 1, pair, hi, lo, first=at == 0, products="h")
                for at, (pair, job) in enumerate(pairs):
                    if at < early:
                        continue
                    pe.wait_ge(fresh_hi, job + 1)
                    for m in range(2):
                        if at == 0 and m == 1:
                            start_unit(n + 1, None)
                        part(n + m, pair, hi, lo, first=at == 0, products="h")
                for m in range(2):
                    for at, (pair, job) in enumerate(pairs):
                        pe.wait_ge(fresh_lo, job + 1)
                        part(n + m, pair, hi, lo, last=at == 3, products="l")

            def in_order(job):
                return [(pair, job + pair) for pair in range(4)]

            def product_tok(n, hi, lo):
                start_unit(n, None)
                wh = w_hi[:, n % RING, :].rearrange("p (k n) -> p k n", k=KT)
                wl = w_lo[:, n % RING, :].rearrange("p (k n) -> p k n", k=KT)
                for kt in range(KT):
                    for tt in range(TT):
                        for i, (a, b) in enumerate(((hi, wh), (lo, wh), (hi, wl))):
                            last = mm(lin[lin_bank[n]][:, tt * T:tt * T + T], a[:, kt, tt * P:tt * P + P], b[:, kt, :],
                                      kt == 0 and tt == 0 and i == 0, kt == KT - 1 and i == 2)
                last.then_inc(unit_done, 1)

            def ada_row_unit(j):
                slot = slot_of["a", 2 * j]
                tiles = w_raw[:, slot, :].rearrange("p (k n) -> p k n", k=KT)
                pe.wait_ge(raw_full[slot], value_of["a", 2 * j])
                if j == 2:
                    pe.wait_ge(ada_copied, 1)
                for kt in range(KT):
                    last = mm(ps_ada[0:1, (j % 2) * T:(j % 2) * T + T], vec[:, V_C + kt:V_C + kt + 1], tiles[:, kt, :],
                              kt == 0 and j % 2 == 0, kt == KT - 1)
                last.then_inc(ada_used, 1)

            def ada_columns(a, part, over):
                for nt in range(2):
                    last = mm(ps_ada[:, 2 * a + nt:2 * a + nt + 1], part[:, nt * P:nt * P + P], over, True, True)
                last.then_inc(ada_done, 1)

            def ada_unit(a):
                pe.wait_ge(ada_part_sum, a - ADA_FIRST + 1)
                if a == ADA_FIRST:
                    pe.wait_ge(ada_ready, 1)
                ada_columns(a, ada_late[:, a % 2, :], ones[:, 0:1])

            def add_squares(s, q):
                if q == 0:
                    into_misc(f"sum{s}")
                pe.wait_ge(sq_ready, 4 * s + q + 1)
                for i in range(2):
                    for tt in range(TT):
                        last = mm(ps_misc[:, tt:tt + 1], probs[:, q % 2, i * T + tt * P:i * T + tt * P + P], ones[:, 0:1],
                                  q == 0 and i == 0 and tt == 0, q == 3 and i == 1)
                last.then_inc(misc_full if q == 3 else sq_used, 1)

            def spread_sum(s, bank):
                name = f"sum{s}"
                pe.wait_ge(root_ready, power_no[name] + 1)
                if bank is ps_ada:
                    pe.wait_ge(spread_read, spread_no[name])
                for tt in range(TT):
                    at = root_at[name] + tt
                    last = mm(bank[:, tt * P:tt * P + P], root[:, at:at + 1].to_broadcast([P, P]), ident, True, True)
                last.then_inc(spread_full, 1)

            def qk_squares(name, n):
                into_misc("qk." + name)
                pe.wait_ge(evac_a, evac_value[n])
                for tt in range(TT):
                    for a in range(2):
                        c0, at = a * T + tt * P, 4 * tt + 2 * a
                        last = mm(ps_misc[:, at:at + 2], probs[:, qk_no["qk." + name] % 2, c0:c0 + P], head_ones, True, True)
                last.then_inc(misc_full, 1)

            def spread_qk(name, bank):
                name = "qk." + name
                pe.wait_ge(root_ready, power_no[name] + 1)
                if bank is ps_ada:
                    pe.wait_ge(spread_read, spread_no[name])
                for a in range(2):
                    for tt in range(TT):
                        for h in range(2):
                            at = root_at[name] + 4 * tt + 2 * a + h
                            last = mm(bank[HD * h:HD * h + HD, a * T + tt * P:a * T + tt * P + P],
                                      root[:, at:at + 1].to_broadcast([P, HD]), ident, True, True)
                last.then_inc(spread_full, 1)

            def rotate(name, src):
                into_misc("rope." + name)
                pe.wait_ge(qk_normed, qk_no["qk." + name] + 1)
                mm(ps_misc[:, :], perm, src, True, True).then_inc(misc_full, 1)

            def to_T(dst_banks, src, sem_done, wait_q=None):
                for q, dst in enumerate(dst_banks):
                    if wait_q:
                        wait_q(q)
                    for i in range(2):
                        for tt in range(TT):
                            c0 = (2 * q + i) * P
                            last = pe.transpose(dst[:, i * T + tt * P:i * T + tt * P + P], src[:, tt, c0:c0 + P], ident)
                    last.then_inc(sem_done, 1)

            def scores(q_tile, k_tile, span):
                for odd in range(2):
                    base = HD * odd
                    for tt, (c0, c1) in enumerate(span):
                        last = mm(acc[odd][:, c0:c1], q_tile[base:base + HD, tt * P:tt * P + P],
                                  k_tile[base:base + HD, 0:c1 - c0], True, True)
                    last.then_inc(score_mm, 1)

            def attention(name, n_pairs, q_tile, k_tile, values, blocks, span, filler):
                scores(q_tile(0), k_tile(0), span)
                for g in range(n_pairs):
                    filler(g)
                    G = pairs.up() - 1
                    for odd in range(2):
                        h = 2 * G + odd
                        pe.wait_ge(exp_done, h + 1)
                        if h >= 2:
                            pe.wait_ge(turned_copied, h - 1)
                        for _, _, c0 in blocks:
                            last = pe.transpose(acc[2 + odd][:, c0:c0 + P], probs[:, odd, c0:c0 + P], ident)
                        last.then_inc(turned, 1)
                    if g + 1 < n_pairs:
                        scores(q_tile(g + 1), k_tile(g + 1), span)
                    into_misc(f"{name}{g}")
                    for odd in range(2):
                        pe.wait_ge(turned_copied, 2 * G + odd + 1)
                        for tt in range(TT):
                            mine = [(s, c0) for t, s, c0 in blocks if t == tt]
                            for i, (s, c0) in enumerate(mine):
                                at = (2 * odd + tt) * HD
                                last = mm(ps_misc[:, at:at + HD], probsT[:, odd, c0:c0 + P], values(2 * g + odd, s),
                                          i == 0, i == len(mine) - 1)
                    last.then_inc(misc_full, 1)

            def finish_stream(n, hi, lo, s):
                product(n + 2, hi, lo)
                add_squares(s, 0)
                add_squares(s, 1)
                product(n + 3, hi, lo)
                add_squares(s, 2)
                add_squares(s, 3)

            pe.wait_ge(consts_in, 16)
            for q in range(4):
                add_squares(0, q)
            spread_sum(0, acc[0])
            pe.wait_ge(vec_ready, 1)
            product(0, u_hi, u_lo, job=J_MEM)
            ada_row_unit(0)
            for q in range(4):
                add_squares(1, q)
            product_tok(1, u_hi, u_lo)
            qk_squares("mem0", 0)
            spread_sum(1, acc[3])
            ada_row_unit(1)
            into_misc("row")
            pe.wait_ge(small_in, 48)
            mm(ps_misc[0:HEADS, 0:384], rel[0:33, :], buckets[0:33, :], True, True).then_inc(misc_full, 1)
            product(2, u_hi, u_lo)
            ada_row_unit(2)
            ada_row_unit(3)
            pe.wait_ge(ada_copied, 2)
            for j in range(4):
                ada_columns(2 * j, ada_row[:, 256 * j:256 * j + 256], ones[0:1, 0:1])
                pe.wait_ge(ada_vector, j + 1)
                ada_columns(2 * j + 1, big[:, 8 + j, :], ones[:, 0:1])
            product_tok(3, u_hi, u_lo)
            qk_squares("mem1", 2)
            for n in range(N_IDX, N_GF):
                if n < 10:
                    product(n, h_hi, h_lo, job=J_H1 if n == N_IDX else None)
                else:
                    product_tok(n, h_hi, h_lo)
                if n in ada_after:
                    ada_unit(ada_after[n])
                if n == 4:
                    spread_qk("mem0", acc[1])
                    spread_qk("mem1", acc[2])
                if n == 5:
                    into_misc("wi")
                    pe.wait_ge(evac_a, evac_value[4])
                    for tt in range(TT):
                        last = pe.transpose(ps_misc[:, tt * P:tt * P + P], f_raw[:, tt * P:tt * P + P], ident)
                    last.then_inc(misc_full, 1)
                if n == 6:
                    pe.wait_ge(evac_a, evac_value[5])
                    pe.wait_ge(spread_read, 4)
                    for h in range(IDX_HEADS):
                        base = HD * (h % 2)
                        for tt, (c0, c1) in enumerate(CAUSAL_SPAN):
                            last = mm(acc[h][:, c0:c1], qi[base:base + HD, h // 2, tt * P:tt * P + P],
                                      ki[base:base + HD, 0:c1 - c0], True, True)
                        last.then_inc(idx_mm, 1)
                if n == 8:
                    pe.wait_ge(f_ready, 1)
                    pe.wait_ge(sel_ready, 1)
                    pe.wait_ge(idx_relu, IDX_HEADS)
                    for h in range(HEADS):
                        last = mm(acc[h // 2][:, (h % 2) * T:(h % 2) * T + T], head_bias[:, h, 0:P], f_cum, True, True)
                        if h % 2:
                            last.then_inc(f_bc, 1)

            def with_ada(n, multiply):
                multiply(n, h_hi, h_lo)
                if n in ada_after:
                    ada_unit(ada_after[n])

            pe.wait_ge(f_copied, 4)
            pe.wait_ge(evac_a, evac_value[11])
            attention("fox", 4, lambda g: qk[:, g, :], lambda g: qk[:, 4 + g, :],
                      lambda h, s: v_tok[:, s, h * HD:h * HD + HD], CAUSAL_BLOCKS, CAUSAL_SPAN,
                      lambda g: with_ada(N_GF + g, product))
            with_ada(N_DSA, product)
            pe.wait_ge(misc_read, misc_no["fox3"] + 1)
            to_T(acc[0:2], y_tok, y_turned)
            for n in range(N_DSA + 1, N_GD):
                with_ada(n, product if n < N_DSA + 4 else product_tok)
            pe.wait_ge(fresh_ready, J_DSA)
            pe.wait_ge(evac_a, evac_value[N_GD - 1])
            attention("dsa", 4, lambda g: qk[:, g, :], lambda g: qk[:, 4 + g, :],
                      lambda h, s: v_tok[:, s, h * HD:h * HD + HD], CAUSAL_BLOCKS, CAUSAL_SPAN,
                      lambda g: with_ada(N_GD + g, product))
            product(N_BR, u_hi, u_lo, 0, acc[0:2], job=J_FOX)
            product(N_BR + 1, u_hi, u_lo, 0, acc[2:4])
            pe.wait_ge(misc_read, misc_no["dsa3"] + 1)
            to_T(acc[0:2], y_tok, y_turned, lambda q: pe.wait_ge(branch_done, q + 1))
            pe.wait_ge(fresh_ready, J_MERGED)
            product(N_BR + 2, u_hi, u_lo, 4, acc[0:2], job=J_DSA)
            pe.wait_ge(branch_done, 4)
            product(N_BR + 3, u_hi, u_lo, 4, acc[2:4], bank_order=True)
            product_two(N_OUT, h_hi, h_lo, in_order(J_MERGED), early=2)
            finish_stream(N_OUT, h_hi, h_lo, 2)

            def mlp(n0, s, job_h, job_u):
                def up(n, turn=None):
                    product(n, h_hi, h_lo, turn=turn)
                    product(n + 1, h_hi, h_lo, turn=turn)

                def down(n, step, turn=None, last=False):
                    ready = job_u + 2 * step + 2
                    pe.wait_ge(fresh_lo, ready if turn is None else turn * 4 + ready)
                    for half in range(2):
                        product(n + half, u_hi, u_lo, 4 * (step % 2), acc[2 * half:2 * half + 2], start=step == 0,
                                turn=turn, bank_order=last)

                spread_sum(s, ps_ada)
                product_two(n0, h_hi, h_lo, in_order(job_h))
                up(n0 + 2)
                down(n0 + 4, 0)
                with pe.Fori(0, MLP_LOOPS) as turn:
                    for k in range(2):
                        up(n0 + 6 + 4 * k, turn)
                        down(n0 + 8 + 4 * k, 1 + k, turn)
                down(n0 + 30, FF_STEPS - 1, last=True)

            pe.wait_ge(fresh_ready, J_H2)
            mlp(N_MLP0, 2, J_H2, J_MLP0)
            into_misc("sum3")
            pe.wait_ge(sq_summed, 1)
            for j in range(2):
                for tt in range(TT):
                    last = mm(ps_misc[:, 2 * j + tt:2 * j + tt + 1], sq_sum[:, j, tt * P:tt * P + P], ones[:, 0:1], True, True)
            last.then_inc(misc_full, 1)
            pe.wait_ge(root_ready, power_no["sum4"] + 1)
            pe.wait_ge(spread_read, spread_no["sum3"])
            for j, name in enumerate(("sum3", "sum4")):
                for tt in range(TT):
                    at = root_at[name] + tt
                    last = mm(ps_ada[:, j * T + tt * P:j * T + tt * P + P], root[:, at:at + 1].to_broadcast([P, P]), ident,
                              True, True)
            last.then_inc(spread_full, 2)
            product_two(N_QM0, h_hi, h_lo, in_order(J_H4))
            qk_squares("qm0", N_QM0)
            product(N_CONV + 1, h_hi, h_lo)
            spread_qk("qm0", ps_ada)
            product(N_CONV + 2, h_hi, h_lo)
            pe.wait_ge(qk_normed, qk_no["qk.qm0"] + 1)
            attention("mem0.", 2, lambda g: qi[:, g, :], lambda g: mem_k[:, 0, g, :],
                      lambda h, s: mem_v[:, 0, s, h * HD:h * HD + HD], FULL_BLOCKS, FULL_SPAN,
                      lambda g: product(N_CONV + 3 + g, h_hi, h_lo))
            product(N_CONV + 5, h_hi, h_lo)
            pe.wait_ge(misc_read, misc_no["mem0.1"] + 1)
            to_T(acc[0:1], y_tok, y_turned)
            for n in range(N_CONV + 6, N_O0):
                product(n, h_hi, h_lo)
            product_two(N_O0, u_hi, u_lo, [(3, J_YM0)] + [(i, J_CONV + i) for i in range(3)], early=3)
            finish_stream(N_O0, u_hi, u_lo, 5)
            mlp(N_MLP1, 5, J_H5, J_MLP1)
            for q in range(4):
                add_squares(6, q)
            spread_sum(6, ps_ada)
            product_two(N_K, h_hi, h_lo, in_order(J_KV))
            qk_squares("k0", N_K)
            product(N_K + 2, h_hi, h_lo)
            qk_squares("k1", N_K + 1)
            spread_qk("k0", ps_ada)
            pe.wait_ge(late_in, 48)
            product(N_Q, u_hi, u_lo, job=J_MIX1)
            qk_squares("k2", N_K + 2)
            spread_qk("k1", ps_ada)
            rotate("k0", flat(qk, 0, 2))
            product(N_Q + 1, u_hi, u_lo)
            qk_squares("qm1", N_Q)
            spread_qk("k2", ps_ada)
            rotate("k1", flat(qk, 2, 4))
            product(N_Q + 2, u_hi, u_lo)
            qk_squares("q0", N_Q + 1)
            spread_qk("qm1", ps_ada)
            rotate("k2", flat(qk, 4, 6))
            product(N_Q + 3, u_hi, u_lo)
            qk_squares("q1", N_Q + 2)
            spread_qk("q0", ps_ada)
            product_tok(N_V, h_hi, h_lo)
            qk_squares("q2", N_Q + 3)
            spread_qk("q1", ps_ada)
            rotate("q0", flat(big, 10, 12))

            def values_unit(g):
                product_tok(N_V + 1 + g, h_hi, h_lo)
                if g == 0:
                    spread_qk("q2", ps_ada)
                    rotate("q1", flat(big, 12, 14))
                else:
                    rotate("q2", flat(big, 14, 16))

            attention("mem1.", 2, lambda g: qi[:, g, :], lambda g: mem_k[:, 1, g, :],
                      lambda h, s: mem_v[:, 1, s, h * HD:h * HD + HD], FULL_BLOCKS, FULL_SPAN, values_unit)
            pe.wait_ge(misc_read, misc_no["mem1.1"] + 1)
            to_T(acc[0:1], y_tok, y_turned)

            def d_scores(h):
                base, odd = HD * (h % 2), h % 2
                for m in range(2):
                    for tt, (c0, c1) in enumerate(CAUSAL_SPAN):
                        last = mm(acc[2 * odd + m][:, c0:c1], diff_q[base:base + HD, 3 * m + h // 2, tt * P:tt * P + P],
                                  qk[base:base + HD, 3 * m + h // 2, 0:c1 - c0], True, True)
                last.then_inc(d_score, 1)

            def turn_o(h):
                into_misc(f"oT{h}")
                pe.wait_ge(o_scaled, h + 1)
                for tt in range(TT):
                    last = pe.transpose(ps_misc[:, tt * P:tt * P + P], y_tok[:, tt, (h % 2) * P:(h % 2) * P + P], ident)
                last.then_inc(misc_full, 1)

            pe.wait_ge(rope_done, len(ROPES))
            pe.wait_ge(spread_read, spread_no["qk.q2"] + 1)
            pe.wait_ge(fresh_ready, J_YM1 + 1)
            pe.wait_ge(evac_a, evac_value[N_V + 2])
            d_scores(0)
            for h in range(DIFF_HEADS):
                if h + 1 < DIFF_HEADS:
                    if h >= 1:
                        pe.wait_ge(d_max, h)
                    d_scores(h + 1)
                pe.wait_ge(mixed, h + 1)
                if h >= 1:
                    pe.wait_ge(d_copied, h)
                for _, _, c0 in CAUSAL_BLOCKS:
                    last = pe.transpose(ps_ada[:, c0:c0 + P], head_bias[:, 2 * (h % 2), c0:c0 + P], ident)
                last.then_inc(d_turned, 1)
                into_misc(f"pv{h}")
                pe.wait_ge(d_copied, h + 1)
                for tt in range(TT):
                    mine = [(s, c0) for t, s, c0 in CAUSAL_BLOCKS if t == tt]
                    for i, (s, c0) in enumerate(mine):
                        last = mm(ps_misc[:, tt * P:tt * P + P], probsT[:, h % 2, c0:c0 + P], diff_v[:, s, h * P:h * P + P],
                                  i == 0, i == len(mine) - 1)
                last.then_inc(misc_full, 1)
                if h >= 1:
                    turn_o(h - 1)
                if h in (1, 2):
                    start_unit(N_O1 + h - 1, None)
                    pe.wait_ge(fresh_lo, J_YM1 + 1)
                    part(N_O1 + h - 1, 3, u_hi, u_lo, first=True)
                if h in (4, 5):
                    pe.wait_ge(fresh_lo, J_DIFF + 1)
                    part(N_O1 + h - 4, 0, u_hi, u_lo)
            pe.wait_ge(fresh_lo, J_DIFF + 2)
            for m in range(2):
                part(N_O1 + m, 1, u_hi, u_lo)
            turn_o(DIFF_HEADS - 1)
            pe.wait_ge(fresh_hi, J_DIFF + 3)
            for m in range(2):
                part(N_O1 + m, 2, u_hi, u_lo, products="h")
            pe.wait_ge(fresh_lo, J_DIFF + 3)
            for m in range(2):
                part(N_O1 + m, 2, u_hi, u_lo, last=True, products="l")
            finish_stream(N_O1, u_hi, u_lo, 7)
            mlp(N_MLP2, 7, J_H7, J_MLP2)

        @block.scalar
        def _(act):
            def link(ins):
                ins.then_inc(chain_a, 1)
                act.wait_ge(chain_a, 1)

            def scale_ada(a):
                slot = slot_of["a", a]
                tiles = w_raw[:, slot, :].rearrange("p (k n) -> p k n", k=KT)
                act.wait_ge(raw_full[slot], value_of["a", a])
                for k in range(KT):
                    last = act.activation(tiles[:, k, :], tiles[:, k, :], ACT.Copy, scale=vec[:, V_C + k:V_C + k + 1])
                last.then_inc(ada_scaled, 1)

            def split_w(n, turn=None, late=False):
                if n >= N_UNITS:
                    return
                at = lambda value, per: value if turn is None else turn * per + value
                slot = slot_of["w", n]
                act.wait_ge(raw_full[slot], at(value_of["w", n], 32))
                if n >= RING:
                    act.wait_ge(unit_done, at(n - RING + 1, BODY))
                act.activation(w_hi[:, n % RING, :], w_raw[:, slot, :], ACT.Copy).then_inc(hi_w, 1)
                if n in ada_after and not late:
                    scale_ada(ada_after[n])

            def split_h(job, hi, tile, turn=None, free=None):
                at = lambda value, per: value if turn is None else turn * per + value
                act.wait_ge(fresh_ready, at(job + 1, 4))
                if free:
                    act.wait_ge(unit_done, at(free, BODY))
                act.activation(flat(hi, tile, tile + 2), fresh[:, job % 2, :], ACT.Copy).then_inc(fresh_hi, 1)

            def evac(n, dst, func=ACT.Copy, scale=1.0):
                act.wait_ge(unit_done, n + 1)
                act.activation(dst, lin[lin_bank[n]][:, :], func, scale=scale).then_inc(evac_a, 1)

            def evac_qk(name, n, dst):
                act.wait_ge(unit_done, n + 1)
                act.activation(dst, lin[lin_bank[n]][:, :], ACT.Copy)
                i = qk_no["qk." + name]
                if i >= 2:
                    act.wait_ge(misc_full, misc_no[QK_NORMS[i - 2]] + 1)
                act.activation(probs[:, i % 2, :], lin[lin_bank[n]][:, :], ACT.Square).then_inc(evac_a, 1)

            def square_pair(s, q, src):
                if q >= 2:
                    act.wait_ge(sq_used, 3 * s + q - 1)
                elif s:
                    act.wait_ge(misc_full, misc_no[f"sum{s - 1}"] + 1)
                act.activation(probs[:, q % 2, :], src, ACT.Square).then_inc(sq_ready, 1)

            def square_x(s):
                for q in range(4):
                    act.wait_ge(xt_ready, 4 * (s - 2) + q + 1)
                    square_pair(s, q, flat(xT, 2 * q, 2 * q + 2))

            def exps(G, span, from_bank=False):
                for odd in range(2):
                    h = 2 * G + odd
                    act.wait_ge(score_max, h + 1)
                    if from_bank and h >= 2:
                        act.wait_ge(turned, h - 1)
                    for tt, (c0, c1) in enumerate(span):
                        at = 2 * odd + tt
                        last = act.activation(probs[:, odd, c0:c1], (acc[odd] if from_bank else probs[:, odd, :])[:, c0:c1],
                                              ACT.Exp, bias=stat[:, S_NMAX + at:S_NMAX + at + 1],
                                              accum_out=stat[:, S_SUM + 4 * (G % 2) + at:S_SUM + 4 * (G % 2) + at + 1])
                    last.then_inc(exp_done, 1)

            def copy_turned(name, g, G, width):
                before_me = misc_no[f"{name}{g}"]
                for odd in range(2):
                    h = 2 * G + odd
                    act.wait_ge(turned, h + 1)
                    if g >= 1:
                        act.wait_ge(misc_full, before_me)
                    act.activation(probsT[:, odd, 0:width], acc[2 + odd][:, 0:width], ACT.Copy).then_inc(turned_copied, 1)

            def sigmoid_unit(n, tile):
                evac(n, flat(big, tile, tile + 2), ACT.Tanh, 0.5)

            for q in range(4):
                act.wait_ge(mem_in[q // 2], 16)
                square_pair(0, q, flat(memT, 2 * q, 2 * q + 2))

            def copy_ada(i):
                act.wait_ge(ada_used, 2 * i + 2)
                act.activation(ada_row[:, 512 * i:512 * i + 512], ps_ada[0:1, :], ACT.Copy).then_inc(ada_copied, 1)

            split_w(0)
            for q in range(4):
                split_h(J_MEM + q, u_hi, 2 * q)
            split_w(1)
            act.wait_ge(x_in, 16)
            for q in range(4):
                square_pair(1, q, flat(xT, 2 * q, 2 * q + 2))
            act.wait_ge(misc_full, misc_no["sum1"] + 1)
            evac_qk("mem0", 0, flat(mem_k[:, 0], 0, 2))
            split_w(2)
            evac(1, flat(mem_v[:, 0], 0, 2))
            copy_ada(0)
            copy_ada(1)
            split_w(3)
            split_w(4)
            evac_qk("mem1", 2, flat(mem_k[:, 1], 0, 2))
            for q in range(4):
                split_h(J_H1 + q, h_hi, 2 * q)
            split_w(5)
            evac(3, flat(mem_v[:, 1], 0, 2))
            split_w(6)
            split_w(7)
            act.wait_ge(unit_done, 5)
            act.activation(ki, lin[lin_bank[4]][:, 0:T], ACT.Copy)
            act.activation(f_raw, lin[lin_bank[4]][:, T:2 * T], ACT.Copy).then_inc(evac_a, 1)
            split_w(8)
            evac(5, v_tok[:, 0, :], scale=HD ** -0.5)
            act.wait_ge(f_in, 1)
            link(act.activation(f_low[64:64 + HEADS, :], f_low[64:64 + HEADS, :], ACT.Exp))
            act.activation(f_low[64:64 + HEADS, :], f_low[64:64 + HEADS, :], ACT.Ln, bias=1.0).then_inc(f_ln, 1)
            split_w(9)
            evac(6, flat(qk, 0, 2), scale=HD ** -0.5)
            act.wait_ge(misc_full, misc_no["qk.mem1"] + 1)
            for h in range(IDX_HEADS):
                act.wait_ge(idx_mm, h + 1)
                if h >= 2:
                    act.wait_ge(idx_added, h - 1)
                act.activation(probs[:, h % 2, 0:384], acc[h][:, 0:384], ACT.Relu).then_inc(idx_relu, 1)
            split_w(10)
            evac(7, flat(qk, 2, 4), scale=HD ** -0.5)
            split_w(11)
            evac(8, flat(qk, 4, 6))
            for q in range(4):
                act.wait_ge(f_bc, 4)
                act.activation(head_bias[:, 2 * q:2 * q + 2, 128:384], acc[q][:, :].rearrange("p (h s) -> p h s", h=2),
                               ACT.Copy, scale=-1.0).then_inc(f_copied, 1)
            split_w(12)
            evac(9, flat(qk, 6, 8))
            for n in (10, 11):
                split_w(n + AHEAD)
                act.wait_ge(unit_done, n + 1)
                c0 = 256 * (n - 10)
                act.activation(v_tok[:, :, c0:c0 + 256], lin[lin_bank[n]][:, :].rearrange("p (t c) -> p t c", t=TT),
                               ACT.Copy).then_inc(evac_a, 1)
            act.wait_ge(bias_out, 16)
            for g in range(4):
                exps(G_FOX + g, CAUSAL_SPAN)
                split_w(N_GF + g + AHEAD, late=True)
                copy_turned("fox", g, G_FOX + g, 384)
                sigmoid_unit(N_GF + g, 2 * g)
                if N_GF + g + AHEAD in ada_after:
                    scale_ada(ada_after[N_GF + g + AHEAD])
            split_w(N_DSA + AHEAD)
            act.wait_ge(misc_full, misc_no["fox3"] + 1)
            evac(N_DSA, flat(qk, 0, 2), scale=HD ** -0.5)
            for q in range(2):
                split_h(J_FOX + q, u_hi, 2 * q)
            for i in range(1, 4):
                split_w(N_DSA + i + AHEAD)
                evac(N_DSA + i, flat(qk, 2 * i, 2 * i + 2), scale=HD ** -0.5 if i < 2 else 1.0)
            for i in range(4, 6):
                n = N_DSA + i
                split_w(n + AHEAD)
                act.wait_ge(unit_done, n + 1)
                c0 = 256 * (i - 4)
                act.activation(v_tok[:, :, c0:c0 + 256], lin[lin_bank[n]][:, :].rearrange("p (t c) -> p t c", t=TT),
                               ACT.Copy).then_inc(evac_a, 1)
            for g in range(4):
                exps(G_DSA + g, CAUSAL_SPAN)
                split_w(N_GD + g + AHEAD)
                copy_turned("dsa", g, G_DSA + g, 384)
                sigmoid_unit(N_GD + g, 8 + 2 * g)
            split_w(N_BR + AHEAD)
            split_w(N_BR + 1 + AHEAD)
            for q in range(2):
                split_h(J_DSA + q, u_hi, 4 + 2 * q)
            split_w(N_BR + 2 + AHEAD)
            for q in range(4):
                if q == 2:
                    split_w(N_BR + 3 + AHEAD)
                split_h(J_MERGED + q, h_hi, 2 * q)
            for i in range(4):
                split_w(N_OUT + i + AHEAD)
                act.wait_ge(xt_ready, i + 1)
                square_pair(2, i, flat(xT, 2 * i, 2 * i + 2))
            for q in range(4):
                split_h(J_H2 + q, h_hi, 2 * q)

            def mlp(n0, job_u, ahead=AHEAD):
                def up_step(n, step, turn=None, first=0):
                    at = lambda value, per: value if turn is None else turn * per + value
                    job = job_u + 2 * step
                    free = n0 + 6 + 4 * (step - 2) if step >= 2 else None
                    for half in range(2):
                        split_w(n + half + ahead, turn)
                        if half:
                            split_h(job, u_hi, 4 * (step % 2), turn, free)
                        act.wait_ge(unit_done, at(n + half + 1, BODY))
                        act.wait_ge(fresh_lo, at(job + half - 1, 4))
                        act.activation(fresh[:, half, :], lin[half][:, :], ACT.Relu).then_inc(evac_a, 1)

                def down_step(n, step, turn=None, pending=None):
                    for half in range(2):
                        split_w(n + half + ahead, turn)
                        if half == 0 and pending is not None:
                            free = n0 + 6 + 4 * (pending - 2) if pending >= 2 else None
                            split_h(job_u + 2 * pending + 1, u_hi, 4 * (pending % 2) + 2, turn, free)

                up_step(n0, 0)
                split_h(job_u + 1, u_hi, 2)
                up_step(n0 + 2, 1)
                down_step(n0 + 4, 0, pending=1)
                with act.Fori(0, MLP_LOOPS) as turn:
                    for k in range(2):
                        up_step(n0 + 6 + 4 * k, 2 + k, turn)
                        down_step(n0 + 8 + 4 * k, 1 + k, turn, pending=2 + k)
                down_step(n0 + 30, FF_STEPS - 1)

            mlp(N_MLP0, J_MLP0)
            for q in range(4):
                act.wait_ge(xt_ready, 4 + q + 1)
                if q >= 2:
                    act.wait_ge(sq_used, 3 * 3 + 2 * (q - 1))
                act.activation(probs[:, q % 2, :], flat(xT, 2 * q, 2 * q + 2), ACT.Square).then_inc(sq_ready, 1)
                for j in range(2):
                    k = 2 * q + j
                    last = act.activation(probsT[:, q % 2, j * T:j * T + T], xT[:, k, :], ACT.Square,
                                          scale=vec[:, V_GF + k:V_GF + k + 1])
                last.then_inc(sq_ready, 1)
            for q in range(4):
                split_h(J_H4 + q, h_hi, 2 * q)
            split_w(N_QM0 + AHEAD)
            act.wait_ge(misc_full, misc_no["sum4"] + 1)
            evac_qk("qm0", N_QM0, v_tok[:, 0, :])
            for i in range(3):
                split_w(N_CONV + i + AHEAD)
                evac(N_CONV + i, flat(big, 2 * i, 2 * i + 2))
            act.wait_ge(misc_full, misc_no["qk.qm0"] + 1)
            for g in range(2):
                exps(G_M0 + g, FULL_SPAN, from_bank=True)
                split_w(N_CONV + 3 + g + AHEAD)
                copy_turned("mem0.", g, G_M0 + g, 512)
            split_w(N_CONV + 5 + AHEAD)
            split_h(J_YM0, u_hi, 6)
            for i in range(3):
                split_w(N_CONV + 6 + i + AHEAD)
                split_h(J_CONV + i, u_hi, 2 * i)
            for i in range(4):
                split_w(N_O0 + i + AHEAD)
                act.wait_ge(xt_ready, 12 + i + 1)
                square_pair(5, i, flat(xT, 2 * i, 2 * i + 2))
            for q in range(4):
                split_h(J_H5 + q, h_hi, 2 * q)
            mlp(N_MLP1, J_MLP1)
            square_x(6)
            for q in range(4):
                split_h(J_KV + q, h_hi, 2 * q)
            for q in range(4):
                split_h(J_MIX1 + q, u_hi, 2 * q)
            act.wait_ge(misc_full, misc_no["sum6"] + 1)
            for i in range(3):
                split_w(N_K + i + AHEAD)
                evac_qk(f"k{i}", N_K + i, flat(qk, 2 * i, 2 * i + 2))
            split_w(N_Q + AHEAD)
            evac_qk("qm1", N_Q, v_tok[:, 0, :])
            for i in range(3):
                split_w(N_Q + 1 + i + AHEAD)
                evac_qk(f"q{i}", N_Q + 1 + i, flat(big, 10 + 2 * i, 12 + 2 * i))
            act.wait_ge(lam_dots, 1)
            act.activation(stat[:, S_LAM:S_LAM + 2], stat[:, S_DOT:S_DOT + 2], ACT.Exp).then_inc(lam_exp, 1)

            def evac_v_unit(i):
                act.wait_ge(unit_done, N_V + i + 1)
                act.activation(diff_v[:, :, 256 * i:256 * i + 256],
                               lin[lin_bank[N_V + i]][:, :].rearrange("p (t c) -> p t c", t=TT), ACT.Copy).then_inc(evac_a, 1)

            split_w(N_V + AHEAD)
            evac_v_unit(0)
            act.wait_ge(misc_full, misc_no["qk.q2"] + 1)
            for g in range(2):
                exps(G_M1 + g, FULL_SPAN, from_bank=True)
                split_w(N_V + 1 + g + AHEAD)
                evac_v_unit(1 + g)
                copy_turned("mem1.", g, G_M1 + g, 512)
            def d_exps(h):
                act.wait_ge(d_max, h + 1)
                for m in range(2):
                    p = head_bias[:, 2 * (h % 2) + m, :]
                    for tt, (c0, c1) in enumerate(CAUSAL_SPAN):
                        at = 4 * (h % 2) + 2 * m + tt
                        last = act.activation(p[:, c0:c1], p[:, c0:c1], ACT.Exp, bias=stat[:, S_DNMAX + at:S_DNMAX + at + 1],
                                              accum_out=stat[:, S_DSUM + at:S_DSUM + at + 1])
                last.then_inc(d_exp, 1)

            split_w(N_O1 + AHEAD)
            d_exps(0)
            split_h(J_YM1, u_hi, 6)
            for h in range(DIFF_HEADS):
                act.wait_ge(d_turned, h + 1)
                if h >= 2:
                    act.wait_ge(misc_full, misc_no[f"pv{h - 2}"] + 1)
                act.activation(probsT[:, h % 2, 0:384], ps_ada[:, 0:384], ACT.Copy).then_inc(d_copied, 1)
                if h + 1 < DIFF_HEADS:
                    d_exps(h + 1)
                if h >= 3 and h % 2:
                    split_h(J_DIFF + h // 2 - 1, u_hi, h - 3)
                act.wait_ge(o_copied, h + 1)
                for tt in range(TT):
                    at = S_OSS + 2 * (h % 2) + tt
                    last = act.activation(probs[:, h % 2, tt * P:tt * P + P], y_tok[:, tt, (h % 2) * P:(h % 2) * P + P],
                                          ACT.Square, accum_out=stat[:, at:at + 1])
                last.then_inc(o_sq, 1)
            split_h(J_DIFF + 2, u_hi, 4)
            for i in range(4):
                if i in (1, 2):
                    split_w(N_O1 + i + AHEAD)
                act.wait_ge(xt_ready, 20 + i + 1)
                square_pair(7, i, flat(xT, 2 * i, 2 * i + 2))
            for q in range(4):
                split_h(J_H7 + q, h_hi, 2 * q)
            mlp(N_MLP2, J_MLP2, AHEAD - 1)

        @block.gpsimd
        def _(pool):
            def split_h(job, lo, hi, tile, turn=None):
                pool.wait_ge(fresh_hi, job + 1 if turn is None else turn * 4 + (job + 1))
                pool.tensor_tensor(flat(lo, tile, tile + 2), fresh[:, job % 2, :], flat(hi, tile, tile + 2).bitcast(F32),
                                   ALU.subtract).then_inc(fresh_lo, 1)

            def power(name):
                pool.wait_ge(misc_read, misc_no[name] + 1)
                at, width = root_at[name], 2 if name.startswith("sum") else 8
                pool.tensor_tensor(root[:, at:at + width], root[:, at:at + width],
                                   minus_half[:, 0:1].to_broadcast([P, width]), ALU.pow).then_inc(root_ready, 1)

            def cos_part(name, src):
                i = rope_no["rope." + name]
                pool.wait_ge(qk_normed, qk_no["qk." + name] + 1)
                if i >= 2:
                    pool.wait_ge(rope_done, i - 1)
                for a in range(2):
                    last = pool.tensor_tensor(rope_cosines[:, i % 2, a * T:a * T + T], src[:, a * T:a * T + T], cosT, ALU.mult)
                last.then_inc(rope_cos, 1)

            chain = Count()

            def link(ins):
                ins.then_inc(chain_g, 1)
                pool.wait_ge(chain_g, chain.up())

            def ada_unit(a):
                tiles = w_raw[:, slot_of["a", a], :].rearrange("p (k n) -> p k n", k=KT)
                pool.wait_ge(ada_scaled, a - ADA_FIRST + 1)
                for half in (4, 2):
                    link(pool.tensor_tensor(tiles[:, 0:half, :], tiles[:, 0:half, :], tiles[:, half:2 * half, :], ALU.add))
                if a >= ADA_FIRST + 2:
                    pool.wait_ge(ada_done, a - 1)
                pool.tensor_tensor(ada_late[:, a % 2, :], tiles[:, 0, :], tiles[:, 1, :], ALU.add).then_inc(ada_part_sum, 1)

            pool.memset(minus_half[:, :], -0.5)
            pool.memset(rel[:, :], 1.0)
            link(pool.memset(f_cum, 0.0))
            pool.wait_ge(consts_in, 16)
            pool.tensor_copy(head_bias[:, :, 0:P], ident[:, 64:64 + HEADS].unsqueeze(2).to_broadcast([P, HEADS, P]))\
                .then_inc(sel_ready, 1)
            power("sum0")
            for q in range(4):
                split_h(J_MEM + q, u_lo, u_hi, 2 * q)
            power("sum1")
            power("qk.mem0")
            for q in range(4):
                split_h(J_H1 + q, h_lo, h_hi, 2 * q)
            power("qk.mem1")
            for a in range(ADA_FIRST, 14):
                ada_unit(a)
            pool.wait_ge(f_copied, 4)
            mask = causal.unsqueeze(1).to_broadcast([P, HEADS, P])
            pool.tensor_tensor(head_bias[:, :, 0:P], head_bias[:, :, P:2 * P], mask, ALU.add)
            pool.tensor_tensor(head_bias[:, :, 2 * P:3 * P], head_bias[:, :, 2 * P:3 * P], mask, ALU.add).then_inc(fox_bias, 1)
            for a in range(14, 20):
                ada_unit(a)
            for q in range(2):
                split_h(J_FOX + q, u_lo, u_hi, 2 * q)
            pool.wait_ge(bias_in, 16)
            pool.wait_ge(picked, 1)
            pool.wait_ge(score_max, HEADS)
            pool.tensor_tensor(head_bias[:, :, 0:P], toeplitz[:, :, P:2 * P], idx[:, 0:P].unsqueeze(1).to_broadcast([P, HEADS, P]),
                               ALU.add)
            pool.tensor_tensor(head_bias[:, :, P:3 * P], toeplitz, idx[:, P:3 * P].unsqueeze(1).to_broadcast([P, HEADS, 2 * P]),
                               ALU.add).then_inc(dsa_bias, 1)
            for a in range(20, ADA_UNITS):
                ada_unit(a)
            for q in range(2):
                split_h(J_DSA + q, u_lo, u_hi, 4 + 2 * q)
            for q in range(4):
                split_h(J_MERGED + q, h_lo, h_hi, 2 * q)

            def norm(s, job=None):
                power(f"sum{s}")
                if job is not None:
                    for q in range(4):
                        split_h(job + q, h_lo, h_hi, 2 * q)

            def mlp(job_u):
                for i in range(4):
                    split_h(job_u + i, u_lo, u_hi, 2 * (i % 4))
                with pool.Fori(0, MLP_LOOPS) as turn:
                    for i in range(4):
                        split_h(job_u + 4 + i, u_lo, u_hi, 2 * (i % 4), turn)

            norm(2, J_H2)
            mlp(J_MLP0)
            power("sum3")
            pool.wait_ge(root_ready, power_no["sum3"] + 1)
            at = root_at["sum3"]
            for _ in range(2):
                link(pool.tensor_tensor(root[:, at + 2:at + 4], root[:, at + 2:at + 4], root[:, at:at + 2], ALU.mult))
            link(pool.tensor_scalar(root[:, at + 2:at + 4], root[:, at + 2:at + 4], EPS, None, ALU.add))
            power("sum4")
            for q in range(4):
                split_h(J_H4 + q, h_lo, h_hi, 2 * q)
            power("qk.qm0")
            split_h(J_YM0, u_lo, u_hi, 6)
            for i in range(3):
                split_h(J_CONV + i, u_lo, u_hi, 2 * i)
            norm(5, J_H5)
            mlp(J_MLP1)
            norm(6, J_KV)
            for q in range(4):
                split_h(J_MIX1 + q, u_lo, u_hi, 2 * q)
            pool.wait_ge(late_in, 48)
            power("qk.k0")
            power("qk.k1")
            cos_part("k0", flat(qk, 0, 2))
            power("qk.k2")
            cos_part("k1", flat(qk, 2, 4))
            power("qk.qm1")
            cos_part("k2", flat(qk, 4, 6))
            power("qk.q0")
            power("qk.q1")
            cos_part("q0", flat(big, 10, 12))
            power("qk.q2")
            cos_part("q1", flat(big, 12, 14))
            cos_part("q2", flat(big, 14, 16))
            split_h(J_YM1, u_lo, u_hi, 6)
            for h in range(DIFF_HEADS):
                if h >= 3 and h % 2:
                    split_h(J_DIFF + h // 2 - 1, u_lo, u_hi, h - 3)
                pool.wait_ge(o_var, h + 1)
                at = S_ORSTD + 2 * (h % 2)
                pool.tensor_tensor(stat[:, at:at + 2], stat[:, at:at + 2], minus_half[:, 0:1].to_broadcast([P, 2]), ALU.pow)\
                    .then_inc(o_rstd, 1)
            split_h(J_DIFF + 2, u_lo, u_hi, 4)
            norm(7, J_H7)
            mlp(J_MLP2)

        @block.vector
        def _(dve):
            chain, halves = Count(), Count()

            def link(ins):
                ins.then_inc(chain_v, 1)
                dve.wait_ge(chain_v, chain.up())

            def split_w(n, turn=None):
                if n >= N_UNITS:
                    return
                dve.wait_ge(hi_w, n + 1 if turn is None else turn * BODY + (n + 1))
                dve.tensor_tensor(w_lo[:, n % RING, :], w_raw[:, slot_of["w", n], :], w_hi[:, n % RING, :].bitcast(F32),
                                  ALU.subtract).then_inc(lo_w, 1)

            def ada_unit(a):
                slot = slot_of["a", a]
                tiles, part = w_raw[:, slot, :].rearrange("p (k n) -> p k n", k=KT), big[:, 8 + a // 2, :]
                dve.wait_ge(raw_full[slot], value_of["a", a])
                link(dve.tensor_scalar(part, tiles[:, 0, :], vec[:, V_C:V_C + 1], None, ALU.mult))
                for k in range(1, KT):
                    last = dve.scalar_tensor_tensor(out=part, in0=tiles[:, k, :], scalar=vec[:, V_C + k:V_C + k + 1], in1=part,
                                                    op0=ALU.mult, op1=ALU.add)
                    if k < KT - 1:
                        link(last)
                last.then_inc(ada_vector, 1)

            def from_misc(name):
                dve.wait_ge(misc_full, misc_no[name] + 1)

            def mean_square(name, eps=EPS):
                from_misc(name)
                width, count = (2, D) if name.startswith("sum") else (8, HD)
                dve.tensor_scalar(root[:, root_at[name]:root_at[name] + width], ps_misc[:, 0:width], 1.0 / count, eps,
                                  ALU.mult, ALU.add).then_inc(misc_read, 1)

            def fresh_slot(job):
                if job >= 2:
                    dve.wait_ge(fresh_lo, job - 1)
                return fresh[:, job % 2, :]

            def normed(job, gains, rstd, shift=None, src=xT):
                for q in range(4):
                    dst = fresh_slot(job + q)
                    for i in range(2):
                        k = 2 * q + i
                        last = dve.scalar_tensor_tensor(out=dst[:, i * T:i * T + T], in0=src[:, k, :], scalar=gains[:, k:k + 1],
                                                        in1=rstd[:, 0:T], op0=ALU.mult, op1=ALU.mult)
                    if shift is not None:
                        link(last)
                        for i in range(2):
                            k = 2 * q + i
                            last = dve.tensor_scalar(dst[:, i * T:i * T + T], dst[:, i * T:i * T + T], shift[:, k:k + 1], None,
                                                     ALU.add)
                    last.then_inc(fresh_ready, 1)

            def rstd_read():
                dve.drain().then_inc(spread_read, 1)

            def qk_scale(name, dst, gain, bank):
                dve.wait_ge(spread_full, spread_no["qk." + name] + 1)
                dve.scalar_tensor_tensor(out=dst, in0=dst, scalar=vec[:, gain:gain + 1], in1=bank[:, :],
                                         op0=ALU.mult, op1=ALU.mult).then_inc(qk_normed, 1)
                rstd_read()

            def rope_add(name, dst):
                from_misc("rope." + name)
                for a in range(2):
                    last = dve.tensor_tensor(rope_sin[:, a * T:a * T + T], ps_misc[:, a * T:a * T + T], sinT, ALU.mult)
                last.then_inc(misc_read, 1)
                dve.wait_ge(misc_read, misc_no["rope." + name] + 1)
                i = rope_no["rope." + name]
                dve.wait_ge(rope_cos, i + 1)
                dve.tensor_tensor(dst, rope_sin, rope_cosines[:, i % 2, :], ALU.add).then_inc(rope_done, 1)

            def maxima(G, span, biased):
                for odd in range(2):
                    h = 2 * G + odd
                    dve.wait_ge(score_mm, h + 1)
                    if h >= 2:
                        dve.wait_ge(turned, h - 1)
                    at = 2 * odd
                    if biased is not None:
                        for tt, (c0, c1) in enumerate(span):
                            last = dve.tensor_tensor_reduce(probs[:, odd, c0:c1], acc[odd][:, c0:c1],
                                                            head_bias[:, (2 * (G - biased)) + odd, c0:c1], 1.0, PICKED,
                                                            ALU.add, ALU.max, stat[:, S_MAX + at + tt:S_MAX + at + tt + 1])
                        link(last)
                    else:
                        link(dve.tensor_reduce(stat[:, S_MAX + at:S_MAX + at + 2],
                                               acc[odd][:, :].rearrange("p (t s) -> p t s", t=TT), AX.X, ALU.max))
                    dve.tensor_scalar(stat[:, S_NMAX + at:S_NMAX + at + 2], stat[:, S_MAX + at:S_MAX + at + 2], -1.0, None,
                                      ALU.mult).then_inc(score_max, 1)

            def attended(name, g, G, y_free=None):
                s0 = S_SUM + 4 * (G % 2)
                dve.wait_ge(exp_done, 2 * G + 2)
                link(dve.reciprocal(stat[:, S_INV:S_INV + 4], stat[:, s0:s0 + 4]))
                from_misc(f"{name}{g}")
                for odd in range(2):
                    for tt in range(TT):
                        at, c0 = 2 * odd + tt, (2 * g + odd) * HD
                        last = dve.tensor_scalar(y_tok[:, tt, c0:c0 + HD], ps_misc[:, at * HD:at * HD + HD],
                                                 stat[:, S_INV + at:S_INV + at + 1], None, ALU.mult)
                last.then_inc(misc_read, 1)

            def y_copy(job, bank_no, y_no):
                dve.wait_ge(y_turned, y_no)
                dve.tensor_copy(fresh_slot(job), acc[bank_no][:, :]).then_inc(fresh_ready, 1)

            dve.wait_ge(vec_in, 16)
            dve.tensor_scalar(vec[:, V_BQ:V_BQ + 1], vec[:, V_BQ:V_BQ + 1], HD ** -0.5, None, ALU.mult)
            dve.tensor_scalar(vec[:, V_SUBLN:V_SUBLN + 1], vec[:, V_SUBLN:V_SUBLN + 1], 1.0 - LAM_INIT, None, ALU.mult)
            dve.tensor_scalar(vec[:, V_MQ:V_MQ + 2], vec[:, V_MQ:V_MQ + 2], HD ** -0.5, None, ALU.mult).then_inc(vec_ready, 1)
            split_w(0)
            mean_square("sum0")
            dve.wait_ge(spread_full, spread_no["sum0"] + 1)
            dve.wait_ge(mem_in[1], 16)
            normed(J_MEM, vec[:, V_MEM:V_MEM + 8], acc[0], src=memT)
            rstd_read()
            split_w(1)
            ada_unit(1)
            mean_square("sum1")
            split_w(2)
            mean_square("qk.mem0")
            from_misc("row")
            dve.tensor_copy(bias_row[0:HEADS, :], ps_misc[0:HEADS, 0:384]).then_inc(misc_read, 1)
            for a in (3, 5, 7):
                ada_unit(a)
            split_w(3)
            dve.wait_ge(ada_done, ADA_FIRST)
            dve.tensor_tensor(ada[:, 0:16], ps_ada[:, 0:16], vec[:, V_ADA:V_ADA + 16], ALU.add).then_inc(ada_ready, 1)
            dve.wait_ge(ada_ready, 1)
            link(dve.scalar_tensor_tensor(out=gs[:, 0, :], in0=ada[:, 8:16], scalar=1.0, in1=vec[:, V_G1:V_G1 + 8],
                                          op0=ALU.add, op1=ALU.mult))
            dve.wait_ge(spread_full, spread_no["sum1"] + 1)
            normed(J_H1, gs[:, 0, :], acc[3], ada[:, 0:8])
            rstd_read()
            split_w(4)
            mean_square("qk.mem1")
            split_w(5)
            split_w(6)
            split_w(7)
            qk_scale("mem0", flat(mem_k[:, 0], 0, 2), V_MK, acc[1])
            qk_scale("mem1", flat(mem_k[:, 1], 0, 2), V_MK + 1, acc[2])
            z, low = idx[64:64 + HEADS, 0:T], f_low[64:64 + HEADS, :]
            dve.wait_ge(evac_a, evac_value[4])
            dve.wait_ge(small_in, 48)
            link(dve.tensor_scalar(z, f_raw[64:64 + HEADS, :], rel[64:64 + HEADS, 0:1], None, ALU.add))
            link(dve.tensor_scalar(low, z, -1.0, None, ALU.mult))
            dve.tensor_tensor(low, low, z, ALU.min).then_inc(f_in, 1)
            split_w(8)
            from_misc("wi")
            for tt in range(TT):
                last = dve.tensor_scalar(stat[:, S_WI + 4 * tt:S_WI + 4 * tt + 4], ps_misc[:, tt * P:tt * P + 4],
                                         IDX_HEADS ** -0.5, None, ALU.mult)
            last.then_inc(misc_read, 1)
            dve.wait_ge(f_ln, 1)
            link(dve.scalar_tensor_tensor(out=z, in0=z, scalar=0.0, in1=low, op0=ALU.min, op1=ALU.subtract))
            dve.tensor_tensor_scan(f_cum[64:64 + HEADS, :], ones[64:64 + HEADS, 0:1].to_broadcast([HEADS, T]), z, 0.0,
                                   ALU.mult, ALU.add).then_inc(f_ready, 1)
            dve.wait_ge(f_ready, 1)
            split_w(9)
            for h in range(IDX_HEADS):
                dve.wait_ge(idx_relu, h + 1)
                if h:
                    dve.wait_ge(idx_added, h)
                for tt, (c0, c1) in enumerate(CAUSAL_SPAN):
                    wi = stat[:, S_WI + 4 * tt + h:S_WI + 4 * tt + h + 1]
                    if h == 0:
                        dve.wait_ge(misc_read, misc_no["wi"] + 1)
                        last = dve.tensor_scalar(idx[:, c0:c1], probs[:, 0, c0:c1], wi, None, ALU.mult)
                    else:
                        last = dve.scalar_tensor_tensor(out=idx[:, c0:c1], in0=probs[:, h % 2, c0:c1], scalar=wi,
                                                        in1=idx[:, c0:c1], op0=ALU.mult, op1=ALU.add)
                last.then_inc(idx_added, 1)
            dve.wait_ge(idx_added, IDX_HEADS)
            dve.tensor_tensor(idx[:, 0:P], idx[:, 0:P], causal, ALU.add)
            link(dve.tensor_tensor(idx[:, 2 * P:3 * P], idx[:, 2 * P:3 * P], causal, ALU.add))

            def pick_eight():
                for tt, (c0, c1) in enumerate(CAUSAL_SPAN):
                    last = dve.max(top8[:, tt, :], idx[:, c0:c1])
                link(last)
                for tt, (c0, c1) in enumerate(CAUSAL_SPAN):
                    last = dve.match_replace(out=idx[:, c0:c1], in_to_replace=top8[:, tt, :], in_values=idx[:, c0:c1],
                                             imm_value=PICKED)
                link(last)

            pick_eight()
            for n in (10, 11):
                split_w(n)
                pick_eight()
            split_w(12)
            pick_eight()
            split_w(13)
            pick_eight()
            split_w(14)
            pick_eight()
            dve.wait_ge(fox_bias, 1)

            def sigmoid(n, tile):
                dve.wait_ge(evac_a, evac_value[n])
                gate = flat(big, tile, tile + 2)
                dve.tensor_scalar(gate, gate, 0.5, 0.5, ALU.mult, ALU.add)

            for g in range(4):
                maxima(G_FOX + g, CAUSAL_SPAN, G_FOX)
                split_w(N_GF + g + AHEAD)
                if g < 2:
                    pick_eight()
                if g == 2:
                    dve.tensor_scalar(idx[:, :], idx[:, :], PICKED, MASKED, ALU.not_equal, ALU.mult).then_inc(picked, 1)
                attended("fox", g, G_FOX + g)
                sigmoid(N_GF + g, 2 * g)
            split_w(N_DSA + AHEAD)
            for q in range(2):
                y_copy(J_FOX + q, q, q + 1)
            for i in range(1, 6):
                split_w(N_DSA + i + AHEAD)
            dve.wait_ge(dsa_bias, 1)
            for g in range(4):
                maxima(G_DSA + g, CAUSAL_SPAN, G_DSA)
                split_w(N_GD + g + AHEAD)
                attended("dsa", g, G_DSA + g)
                sigmoid(N_GD + g, 8 + 2 * g)
            for half in range(2):
                split_w(N_BR + half + AHEAD)
                dve.wait_ge(unit_done, N_BR + half + 1)
                for q in (2 * half, 2 * half + 1):
                    gate = flat(big, 2 * q, 2 * q + 2)
                    dve.tensor_tensor(gate, gate, acc[q][:, :], ALU.mult).then_inc(branch_done, 1)
            for q in range(2):
                y_copy(J_DSA + q, q, 2 + q + 1)
            for half in range(2):
                split_w(N_BR + 2 + half + AHEAD)
                if half == 0:
                    dve.wait_ge(unit_done, N_BR + 2 + 1)
                for q in (2 * half, 2 * half + 1):
                    if q == 2:
                        dve.wait_ge(half_done, halves.up())
                    if q == 3:
                        dve.wait_ge(unit_done, N_BR + 3 + 1)
                    gate = flat(big, 8 + 2 * q, 8 + 2 * q + 2)
                    link(dve.tensor_tensor(gate, gate, acc[q][:, :], ALU.mult))
                    dve.tensor_tensor(fresh_slot(J_MERGED + q), gate, flat(big, 2 * q, 2 * q + 2), ALU.add)\
                        .then_inc(fresh_ready, 1)
            dve.wait_ge(ada_done, ADA_UNITS)
            link(dve.tensor_tensor(ada[:, 16:48], ps_ada[:, 16:48], vec[:, V_ADA + 16:V_ADA + 48], ALU.add))
            dve.scalar_tensor_tensor(out=gs[:, 1, :], in0=ada[:, 32:40], scalar=1.0, in1=vec[:, V_G2:V_G2 + 8],
                                     op0=ALU.add, op1=ALU.mult)
            for i in range(4):
                n = N_OUT + i
                if i < 3:
                    split_w(n + AHEAD)
                dve.wait_ge(unit_done, n + 1)
                for j in range(2):
                    k = 2 * i + j
                    last = dve.scalar_tensor_tensor(out=xT[:, k, :], in0=lin[lin_bank[n]][:, j * T:j * T + T],
                                                    scalar=ada[:, 16 + k:17 + k], in1=xT[:, k, :], op0=ALU.mult, op1=ALU.add)
                    if j == 0:
                        continue
                    last.then_inc(evac_v, 1)
                dve.drain().then_inc(xt_ready, 1)
            split_w(N_OUT + 3 + AHEAD)
            mean_square("sum2")
            dve.wait_ge(spread_full, spread_no["sum2"] + 1)
            normed(J_H2, gs[:, 1, :], ps_ada, ada[:, 24:32])
            rstd_read()

            def mlp(n0, job_u, gate=None, ahead=AHEAD):
                def up_step(n, step, turn=None):
                    at = lambda value, per: value if turn is None else turn * per + value
                    for half in range(2):
                        split_w(n + half + ahead, turn)
                        dve.wait_ge(evac_a, at(evac_value[n + half], 4))
                        dve.tensor_tensor(fresh[:, half, :], fresh[:, half, :], fresh[:, half, :], ALU.mult)\
                            .then_inc(fresh_ready, 1)

                def down_step(n, turn=None):
                    for half in range(2):
                        split_w(n + half + ahead, turn)

                up_step(n0, 0)
                up_step(n0 + 2, 1)
                down_step(n0 + 4)
                with dve.Fori(0, MLP_LOOPS) as turn:
                    for k in range(2):
                        up_step(n0 + 6 + 4 * k, 2 + k, turn)
                        down_step(n0 + 8 + 4 * k, turn)
                down_step(n0 + 30)
                for q in range(4):
                    if q % 2 == 0:
                        dve.wait_ge(half_done, halves.up())
                    else:
                        dve.wait_ge(unit_done, n0 + 30 + q // 2 + 1)
                    if gate is None:
                        pair = flat(xT, 2 * q, 2 * q + 2)
                        dve.tensor_tensor(pair, acc[q][:, :], pair, ALU.add).then_inc(xt_ready, 1)
                    else:
                        for j in range(2):
                            k = 2 * q + j
                            last = dve.scalar_tensor_tensor(out=xT[:, k, :], in0=acc[q][:, j * T:j * T + T],
                                                            scalar=gate[:, k:k + 1], in1=xT[:, k, :], op0=ALU.mult, op1=ALU.add)
                        last.then_inc(xt_ready, 1)

            mlp(N_MLP0, J_MLP0, ada[:, 40:48])
            for q in range(4):
                dve.wait_ge(sq_ready, 4 * 3 + 2 * q + 2)
                if q:
                    dve.wait_ge(sq_used, 3 * 3 + 2 * q)
                for half in range(2):
                    cols = slice(half * T, half * T + T)
                    for j, squares in enumerate((probs, probsT)):
                        if q == 0 and half == 0:
                            last = dve.tensor_copy(sq_sum[:, j, :], squares[:, 0, cols])
                        else:
                            last = dve.tensor_tensor(sq_sum[:, j, :], sq_sum[:, j, :], squares[:, q % 2, cols], ALU.add)
                    if half == 0:
                        link(last)
                if q < 3:
                    last.then_inc(sq_used, 2)
                else:
                    last.then_inc(sq_summed, 1)
            from_misc("sum3")
            at = root_at["sum3"]
            dve.tensor_scalar(root[:, at:at + 2], ps_misc[:, 0:2], 1.0 / D, EPS, ALU.mult, ALU.add)
            dve.tensor_scalar(root[:, at + 2:at + 4], ps_misc[:, 2:4], 1.0 / D, None, ALU.mult).then_inc(misc_read, 1)
            dve.wait_ge(spread_full, spread_no["sum4"] + 1)
            for q in range(4):
                for j in range(2):
                    k = 2 * q + j
                    last = dve.scalar_tensor_tensor(out=xT[:, k, :], in0=xT[:, k, :], scalar=vec[:, V_GF + k:V_GF + k + 1],
                                                    in1=ps_ada[:, 0:T], op0=ALU.mult, op1=ALU.mult)
                last.then_inc(xt_ready, 1)
                dst = fresh_slot(J_H4 + q)
                dve.wait_ge(xt_ready, 8 + q + 1)
                for j in range(2):
                    k = 2 * q + j
                    last = dve.scalar_tensor_tensor(out=dst[:, j * T:j * T + T], in0=xT[:, k, :],
                                                    scalar=vec[:, V_MIX + k:V_MIX + k + 1], in1=ps_ada[:, T:2 * T],
                                                    op0=ALU.mult, op1=ALU.mult)
                last.then_inc(fresh_ready, 1)
            dve.wait_ge(fresh_ready, J_H4 + 4)
            dve.drain().then_inc(spread_read, 2)
            split_w(N_QM0 + AHEAD)
            split_w(N_CONV + AHEAD)
            mean_square("qk.qm0")
            split_w(N_CONV + 1 + AHEAD)
            qk_scale("qm0", v_tok[:, 0, :], V_MQ, ps_ada)
            split_w(N_CONV + 2 + AHEAD)

            def conv(i):
                n = N_CONV + 3 + i
                dve.wait_ge(unit_done, n + 1)
                dve.wait_ge(evac_a, evac_value[N_CONV + i])
                c = flat(big, 2 * i, 2 * i + 2)
                dve.tensor_tensor(c, c, lin[lin_bank[n]][:, :], ALU.mult).then_inc(evac_v, 1)
                dve.wait_ge(evac_v, evac_value[n])
                for tap, back in ((V_CONV + 12, 0), (V_CONV + 6, 1), (V_CONV, 2)):
                    for j in range(2):
                        k = 2 * i + j
                        u, y, tap_w = big[:, k, :], big[:, 6 + k, :], vec[:, tap + k:tap + k + 1]
                        if back == 0:
                            last = dve.tensor_scalar(y, u, tap_w, None, ALU.mult)
                        else:
                            last = dve.scalar_tensor_tensor(out=y[:, back:T], in0=u[:, 0:T - back], scalar=tap_w,
                                                            in1=y[:, back:T], op0=ALU.mult, op1=ALU.add)
                    link(last)

            for g in range(2):
                maxima(G_M0 + g, FULL_SPAN, None)
                split_w(N_CONV + 3 + g + AHEAD)
                conv(g)
                attended("mem0.", g, G_M0 + g)
            split_w(N_CONV + 5 + AHEAD)
            conv(2)
            y_copy(J_YM0, 0, 5)
            for i in range(3):
                n = N_CONV + 6 + i
                split_w(n + AHEAD)
                dve.wait_ge(unit_done, n + 1)
                dst = fresh_slot(J_CONV + i)
                dve.tensor_tensor(dst, flat(big, 6 + 2 * i, 8 + 2 * i), lin[lin_bank[n]][:, :], ALU.mult).then_inc(evac_v, 1)
                dve.drain().then_inc(fresh_ready, 1)

            def residual(n0, splits):
                for i in range(4):
                    n = n0 + i
                    if i in splits and i < 3:
                        split_w(n + AHEAD)
                    dve.wait_ge(unit_done, n + 1)
                    pair = flat(xT, 2 * i, 2 * i + 2)
                    dve.tensor_tensor(pair, lin[lin_bank[n]][:, :], pair, ALU.add).then_inc(evac_v, 1)
                    dve.drain().then_inc(xt_ready, 1)
                if 3 in splits:
                    split_w(n0 + 3 + AHEAD)

            residual(N_O0, (0, 1, 2, 3))
            mean_square("sum5")
            dve.wait_ge(spread_full, spread_no["sum5"] + 1)
            normed(J_H5, vec[:, V_MLP:V_MLP + 8], ps_ada)
            rstd_read()
            mlp(N_MLP1, J_MLP1)
            mean_square("sum6")
            dve.wait_ge(spread_full, spread_no["sum6"] + 1)
            normed(J_KV, vec[:, V_KV:V_KV + 8], ps_ada)
            normed(J_MIX1, vec[:, V_MIX + 8:V_MIX + 16], ps_ada)
            rstd_read()
            dve.wait_ge(late_in, 48)
            split_w(N_K + AHEAD)
            dve.tensor_tensor_reduce(lam_in[:, 0, :], lam_in[:, 0, :], lam_in[:, 1, :], 1.0, 0.0, ALU.mult, ALU.add,
                                     stat[:, S_DOT:S_DOT + 1])
            dve.tensor_tensor_reduce(lam_in[:, 2, :], lam_in[:, 2, :], lam_in[:, 3, :], 1.0, 0.0, ALU.mult, ALU.add,
                                     stat[:, S_DOT + 1:S_DOT + 2]).then_inc(lam_dots, 1)
            split_w(N_K + 1 + AHEAD)
            k_pair = [flat(qk, 2 * i, 2 * i + 2) for i in range(3)]
            q_pair = [flat(big, 10 + 2 * i, 12 + 2 * i) for i in range(3)]
            mean_square("qk.k0")
            split_w(N_K + 2 + AHEAD)
            mean_square("qk.k1")
            qk_scale("k0", k_pair[0], V_K, ps_ada)
            split_w(N_Q + AHEAD)
            mean_square("qk.k2")
            qk_scale("k1", k_pair[1], V_K, ps_ada)
            rope_add("k0", k_pair[0])
            split_w(N_Q + 1 + AHEAD)
            mean_square("qk.qm1")
            qk_scale("k2", k_pair[2], V_K, ps_ada)
            rope_add("k1", k_pair[1])
            split_w(N_Q + 2 + AHEAD)
            mean_square("qk.q0")
            qk_scale("qm1", v_tok[:, 0, :], V_MQ + 1, ps_ada)
            rope_add("k2", k_pair[2])
            split_w(N_Q + 3 + AHEAD)
            mean_square("qk.q1")
            qk_scale("q0", q_pair[0], V_BQ, ps_ada)
            split_w(N_V + AHEAD)
            mean_square("qk.q2")
            qk_scale("q1", q_pair[1], V_BQ, ps_ada)
            rope_add("q0", q_pair[0])
            dve.wait_ge(lam_exp, 1)
            link(dve.tensor_tensor(stat[:, S_NLAM:S_NLAM + 1], stat[:, S_LAM + 1:S_LAM + 2], stat[:, S_LAM:S_LAM + 1],
                                   ALU.subtract))
            dve.tensor_scalar(stat[:, S_NLAM:S_NLAM + 1], stat[:, S_NLAM:S_NLAM + 1], -LAM_INIT, None, ALU.add)
            for g in range(2):
                maxima(G_M1 + g, FULL_SPAN, None)
                split_w(N_V + 1 + g + AHEAD)
                if g == 0:
                    qk_scale("q2", q_pair[2], V_BQ, ps_ada)
                    rope_add("q1", q_pair[1])
                else:
                    rope_add("q2", q_pair[2])
                attended("mem1.", g, G_M1 + g)

            def d_maxima(h):
                dve.wait_ge(d_score, h + 1)
                if h >= 2:
                    dve.wait_ge(d_turned, h - 1)
                for m in range(2):
                    for tt, (c0, c1) in enumerate(CAUSAL_SPAN):
                        at = 4 * (h % 2) + 2 * m + tt
                        last = dve.tensor_tensor_reduce(head_bias[:, 2 * (h % 2) + m, c0:c1], acc[2 * (h % 2) + m][:, c0:c1],
                                                        chunk_mask[:, c0:c1], 1.0, PICKED, ALU.add, ALU.max,
                                                        stat[:, S_DMAX + at:S_DMAX + at + 1])
                link(last)
                at = 4 * (h % 2)
                dve.tensor_scalar(stat[:, S_DNMAX + at:S_DNMAX + at + 4], stat[:, S_DMAX + at:S_DMAX + at + 4], -1.0, None,
                                  ALU.mult).then_inc(d_max, 1)

            def mix(h):
                dve.wait_ge(d_exp, h + 1)
                at = 4 * (h % 2)
                inv = stat[:, S_DINV + at:S_DINV + at + 4]
                link(dve.reciprocal(inv, stat[:, S_DSUM + at:S_DSUM + at + 4]))
                link(dve.tensor_scalar(inv[:, 2:4], inv[:, 2:4], stat[:, S_NLAM:S_NLAM + 1], None, ALU.mult))
                p1, p2 = head_bias[:, 2 * (h % 2), :], head_bias[:, 2 * (h % 2) + 1, :]
                for tt, (c0, c1) in enumerate(CAUSAL_SPAN):
                    last = dve.tensor_scalar(p2[:, c0:c1], p2[:, c0:c1], inv[:, 2 + tt:3 + tt], None, ALU.mult)
                link(last)
                for tt, (c0, c1) in enumerate(CAUSAL_SPAN):
                    last = dve.scalar_tensor_tensor(out=p1[:, c0:c1], in0=p1[:, c0:c1], scalar=inv[:, tt:tt + 1],
                                                    in1=p2[:, c0:c1], op0=ALU.mult, op1=ALU.add)
                last.then_inc(mixed, 1)

            def o_copy(h):
                from_misc(f"pv{h}")
                c0 = (h % 2) * P
                for tt in range(TT):
                    last = dve.tensor_copy(y_tok[:, tt, c0:c0 + P], ps_misc[:, tt * P:tt * P + P])
                last.then_inc(misc_read, 1)
                dve.drain().then_inc(o_copied, 1)

            def o_mean(h):
                dve.wait_ge(o_sq, h + 1)
                at = 2 * (h % 2)
                dve.tensor_scalar(stat[:, S_ORSTD + at:S_ORSTD + at + 2], stat[:, S_OSS + at:S_OSS + at + 2], 1.0 / (2 * HD),
                                  SUBLN_EPS, ALU.mult, ALU.add).then_inc(o_var, 1)

            def o_scale(h):
                dve.wait_ge(o_rstd, h + 1)
                c0 = (h % 2) * P
                for tt in range(TT):
                    at = S_ORSTD + 2 * (h % 2) + tt
                    last = dve.tensor_scalar(y_tok[:, tt, c0:c0 + P], y_tok[:, tt, c0:c0 + P], stat[:, at:at + 1], None, ALU.mult)
                last.then_inc(o_scaled, 1)

            def o_take(h):
                job = J_DIFF + h // 2
                from_misc(f"oT{h}")
                dst = fresh_slot(job)[:, (h % 2) * T:(h % 2) * T + T]
                dve.tensor_scalar(dst, ps_misc[:, 0:T], vec[:, V_SUBLN:V_SUBLN + 1], None, ALU.mult).then_inc(misc_read, 1)
                if h % 2:
                    dve.drain().then_inc(fresh_ready, 1)

            y_copy(J_YM1, 0, 6)
            split_w(N_O1 + AHEAD)
            d_maxima(0)
            for h in range(DIFF_HEADS):
                mix(h)
                if h >= 2:
                    o_take(h - 2)
                if h >= 1:
                    o_mean(h - 1)
                if h + 1 < DIFF_HEADS:
                    d_maxima(h + 1)
                if h >= 1:
                    o_scale(h - 1)
                o_copy(h)
            o_mean(DIFF_HEADS - 1)
            o_take(DIFF_HEADS - 2)
            o_scale(DIFF_HEADS - 1)
            o_take(DIFF_HEADS - 1)
            residual(N_O1, (1, 2))
            mean_square("sum7")
            dve.wait_ge(spread_full, spread_no["sum7"] + 1)
            normed(J_H7, vec[:, V_MLP + 8:V_MLP + 16], ps_ada)
            rstd_read()
            mlp(N_MLP2, J_MLP2, ahead=AHEAD - 1)


_WEIGHTS = {"w_ada": "w_ada", "w_in": "w_in", "w_branch_fox": "w_branch_fox", "w_branch_dsa": "w_branch_dsa",
            "w_out": "w_out", "w_mlp1": "w_mlp1", "w_mlp2": "w_mlp2", "a_w_in": "a_w_in_2", "b_w_q": "b_w_q_2",
            "w_kv": "w_kv_2", "w_mem_kv": "w_mem_kv_2", "w_o": "w_o_2", "w_up": "w_up_2", "w_down": "w_down_2"}
_VECTORS = {"rel_bias": "rel_bias", "b_forget": "b_forget", "b_lam": "b_lam_2"}
_COLUMNS = ("c", "b_ada", "g_norm1", "g_norm2", "g_final", "norm_mix_2", "norm_mlp_2", "kv_norm_2", "mem_norm_2",
            "a_conv_2", "b_subln_2")
_HEAD_COLUMNS = ("b_q_norm_2", "k_norm_2", "mem_q_norm_2", "mem_k_norm_2")


def kernel(**inputs):
    import numpy as _np
    import concourse.bacc as _bacc
    from concourse import mybir as _mybir
    from concourse.bass_utils import run_bass_kernel_spmd as _run

    nc = _bacc.Bacc("TRN2", target_bir_lowering=False, num_devices=1)
    arrays = {}

    def give(name, a):
        a = _np.ascontiguousarray(a)
        arrays[f"in_{name}"] = a
        return nc.dram_tensor(f"in_{name}", a.shape, _mybir.dt.from_np(a.dtype), kind="ExternalInput").ap()

    def feature_major(a):
        return _np.asarray(a).reshape(T, KT, P).transpose(2, 1, 0)

    x = give("x", feature_major(inputs["x"]))
    mem = give("mem", feature_major(inputs["mem_2"]))
    w = {name: give(name, inputs[key]) for name, key in _WEIGHTS.items()}
    vectors = {name: give(name, _np.asarray(inputs[key]).reshape(-1)) for name, key in _VECTORS.items()}
    tables = {name: give(name, table) for name, table in host_tables().items()}
    columns = [_np.asarray(inputs[key]).reshape(-1, P) for key in _COLUMNS]
    columns += [_np.tile(_np.asarray(inputs[key]).reshape(-1, HD), (1, 2)) for key in _HEAD_COLUMNS]
    tables["vec"] = give("vec", _np.concatenate(columns, 0).T)
    out = nc.dram_tensor("out_dram", (P, KT, T), _mybir.dt.float32, kind="ExternalOutput").ap()
    two_blocks(nc, x, mem, w, vectors, tables, out)
    r = _run(nc, [arrays], core_ids=[0])
    return r.results[0]["out_dram"].transpose(2, 1, 0).reshape(1, T, D)
```
